# Optimizing a Trainium2 kernel written in Bass

```python
import math
import jax, jax.numpy as jnp
from jax import lax
import numpy as np

D_MODEL = 1024
BATCH = 1
SEQ = 256
DEPTH = 4

N_MIXERS = 3
N_LAYERS_A = (DEPTH + 2) // 3
N_LAYERS_B = (DEPTH + 1) // 3
N_LAYERS_C = DEPTH // 3
EPS = 1e-6
ROPE_THETA = 10000.0
MASK_VALUE = -1e30
TINY = 1e-30

HG_HEADS = 8
HG_DK = 128
HG_DV = D_MODEL // HG_HEADS
HG_CHUNK = 64

AT_GROUPS = ((128, 1), (512, 4), (2048, 16))
AT_NGROUP = 3
AT_HEADS = 8
AT_HEAD_DIM = 64
AT_BLOCK = 128

RT_HEADS = 4
RT_DK = D_MODEL // RT_HEADS
RT_DV = 2 * RT_DK
RT_CHUNK = 128

PK_HEADS = 8
PK_NKEYS = 128
PK_EXPERTS = PK_NKEYS * PK_NKEYS
PK_DQ = 256
PK_TOPK = 16
PK_TOKEN_BLOCK = 128

kernel_name = 'hybrid_hgrn2_dilattn_retnet_peer'

F32 = jnp.float32

def _rmsnorm(x, gain):
    x32 = x.astype(F32)
    y = x32 * lax.rsqrt(jnp.mean(x32 * x32, axis=-1, keepdims=True) + EPS)
    return (y * gain.astype(F32)).astype(x.dtype)

def _rope(x, positions):
    half = x.shape[-1] // 2
    inv_freq = ROPE_THETA ** (-jnp.arange(half, dtype=F32) / half)
    ang = positions.astype(F32)[..., None] * inv_freq
    cos = jnp.cos(ang)[:, :, None, :]
    sin = jnp.sin(ang)[:, :, None, :]
    x32 = x.astype(F32)
    x1, x2 = x32[..., :half], x32[..., half:]
    return jnp.concatenate([x1 * cos - x2 * sin, x2 * cos + x1 * sin], axis=-1).astype(x.dtype)

def _gla_chunk_scan(q, k, v, log_f):
    B, S, H, DK = q.shape
    DV = v.shape[-1]
    C = HG_CHUNK
    n = S // C

    def chunks(t):
        return t.astype(F32).reshape(B, n, C, H, t.shape[-1]).transpose(1, 0, 3, 2, 4)

    qc, kc, vc = chunks(q), chunks(k), chunks(v)
    bc = jnp.cumsum(chunks(log_f), axis=3)
    causal = jnp.tril(jnp.ones((C, C), dtype=bool))[:, :, None]

    def step(state, inp):
        q_, k_, v_, b_ = inp
        diff = b_[:, :, :, None, :] - b_[:, :, None, :, :]
        dec = jnp.where(causal, jnp.exp(jnp.minimum(diff, 0.0)), 0.0)
        att = jnp.einsum('bhtk,bhsk,bhtsk->bhts', q_, k_, dec)
        o = jnp.einsum('bhts,bhsv->bhtv', att, v_)
        o = o + jnp.einsum('bhtk,bhkv->bhtv', q_ * jnp.exp(b_), state)
        b_last = b_[:, :, -1:, :]
        k_dec = k_ * jnp.exp(b_last - b_)
        state = jnp.exp(b_last[:, :, 0, :])[..., None] * state + jnp.einsum('bhsk,bhsv->bhkv', k_dec, v_)
        return state, o

    state0 = jnp.zeros((B, H, DK, DV), F32)
    _, oc = lax.scan(step, state0, (qc, kc, vc, bc))
    return oc.transpose(1, 0, 3, 2, 4).reshape(B, S, H, DV)

def _hgrn2_mixer(h, w_in, o_gain, w_out, lower_bound):
    B, S, _ = h.shape
    fd = HG_HEADS * HG_DK
    vd = HG_HEADS * HG_DV
    q, f, i, g = jnp.split(h @ w_in, [fd, 2 * fd, 2 * fd + vd], axis=-1)
    q = jax.nn.silu(q)
    f32 = f.astype(F32)
    lb = lower_bound.astype(F32)
    forget = lb + (1.0 - lb) * jax.nn.sigmoid(f32)
    log_f = jnp.log(jnp.maximum(forget, TINY))
    k = (1.0 - lb) * jax.nn.sigmoid(-f32)
    o = _gla_chunk_scan(q.reshape(B, S, HG_HEADS, HG_DK), k.reshape(B, S, HG_HEADS, HG_DK),
                        i.reshape(B, S, HG_HEADS, HG_DV), log_f.reshape(B, S, HG_HEADS, HG_DK))
    o = _rmsnorm(o, o_gain.reshape(HG_HEADS, HG_DV)).astype(h.dtype).reshape(B, S, vd)
    return (o * jax.nn.silu(g)) @ w_out

def _dilated_window_attention(q, k, v, window, dilation):
    B, S, H, Dh = q.shape
    span = window // dilation
    L = -(-S // dilation)
    Lp = -(-L // AT_BLOCK) * AT_BLOCK
    Sp = Lp * dilation
    nb = Lp // AT_BLOCK

    def strided_blocks(t):
        t = jnp.pad(t, ((0, 0), (0, Sp - S), (0, 0), (0, 0)))
        return t.reshape(B, nb, AT_BLOCK, dilation, H, Dh).transpose(0, 3, 4, 1, 2, 5)

    def with_prev(t):
        prev = jnp.pad(t[:, :, :, :-1], ((0, 0), (0, 0), (0, 0), (1, 0), (0, 0), (0, 0)))
        return jnp.concatenate([prev, t], axis=4)

    qb = strided_blocks(q)
    kk = with_prev(strided_blocks(k))
    vv = with_prev(strided_blocks(v))
    s = jnp.einsum('brhnqe,brhnke->brhnqk', qb, kk, preferred_element_type=F32) * (Dh ** -0.5)
    qi = jnp.arange(AT_BLOCK)[:, None] + AT_BLOCK
    ki = jnp.arange(2 * AT_BLOCK)[None, :]
    dist = qi - ki
    band = (dist >= 0) & (dist <= span)
    first = (jnp.arange(nb) == 0)[:, None, None]
    mask = band[None] & ~(first & (ki < AT_BLOCK)[None])
    s = jnp.where(mask, s, MASK_VALUE)
    m = jnp.max(s, axis=-1, keepdims=True)
    p = jnp.exp(s - m)
    l = jnp.sum(p, axis=-1, keepdims=True)
    o = jnp.einsum('brhnqk,brhnke->brhnqe', p, vv.astype(F32)) / l
    lse = (m + jnp.log(l))[..., 0]
    o = o.transpose(0, 3, 4, 1, 2, 5).reshape(B, Sp, H, Dh)[:, :S]
    lse = lse.transpose(0, 3, 4, 1, 2).reshape(B, Sp, H)[:, :S]
    return o, lse

def _dilated_attention_mixer(h, positions, w_in, q_gain, k_gain, w_out):
    B, S, _ = h.shape
    proj = (h @ w_in).reshape(B, S, 3, AT_NGROUP, AT_HEADS, AT_HEAD_DIM)
    outs = []
    lses = []
    for gi, (window, dilation) in enumerate(AT_GROUPS):
        q = _rope(_rmsnorm(proj[:, :, 0, gi], q_gain[gi]), positions)
        k = _rope(_rmsnorm(proj[:, :, 1, gi], k_gain[gi]), positions)
        o, lse = _dilated_window_attention(q, k, proj[:, :, 2, gi], window, dilation)
        outs.append(o)
        lses.append(lse)
    wts = jax.nn.softmax(jnp.stack(lses, axis=0), axis=0)
    o = jnp.sum(wts[..., None] * jnp.stack(outs, axis=0), axis=0)
    return o.astype(h.dtype).reshape(B, S, AT_HEADS * AT_HEAD_DIM) @ w_out

def _retention_chunk_scan(q, k, v):
    B, S, H, DK = q.shape
    DV = v.shape[-1]
    C = RT_CHUNK
    n = S // C
    log_gamma = jnp.log1p(-jnp.exp2(-5.0 - jnp.arange(H, dtype=F32)))
    idx = jnp.arange(C, dtype=F32)
    rel = idx[:, None] - idx[None, :]
    decay = jnp.where(rel >= 0, jnp.exp(log_gamma[:, None, None] * jnp.maximum(rel, 0.0)), 0.0)
    q_dec = jnp.exp(log_gamma[:, None] * (idx + 1.0))
    k_dec = jnp.exp(log_gamma[:, None] * (C - 1.0 - idx))
    chunk_dec = jnp.exp(log_gamma * C)

    def chunks(t):
        return t.astype(F32).reshape(B, n, C, H, t.shape[-1]).transpose(1, 0, 3, 2, 4)

    def step(state, inp):
        q_, k_, v_ = inp
        att = jnp.einsum('bhtk,bhsk->bhts', q_, k_) * decay
        o = jnp.einsum('bhts,bhsv->bhtv', att, v_)
        o = o + jnp.einsum('bhtk,bhkv->bhtv', q_ * q_dec[None, :, :, None], state)
        state = chunk_dec[None, :, None, None] * state + jnp.einsum('bhsk,bhsv->bhkv', k_ * k_dec[None, :, :, None], v_)
        return state, o

    state0 = jnp.zeros((B, H, DK, DV), F32)
    _, oc = lax.scan(step, state0, (chunks(q), chunks(k), chunks(v)))
    return oc.transpose(1, 0, 3, 2, 4).reshape(B, S, H, DV)

def _retention_mixer(h, positions, w_in, o_gain, w_out):
    B, S, _ = h.shape
    kd = RT_HEADS * RT_DK
    vd = RT_HEADS * RT_DV
    q, k, v, g = jnp.split(h @ w_in, [kd, 2 * kd, 2 * kd + vd], axis=-1)
    q = _rope(q.reshape(B, S, RT_HEADS, RT_DK), positions)
    k = _rope(k.reshape(B, S, RT_HEADS, RT_DK), positions) * (RT_DK ** -0.5)
    o = _retention_chunk_scan(q, k, v.reshape(B, S, RT_HEADS, RT_DV))
    o = _rmsnorm(o, o_gain.reshape(RT_HEADS, RT_DV)).astype(h.dtype).reshape(B, S, vd)
    return (jax.nn.silu(g) * o) @ w_out

def _peer_ffn(h, w_q, sub_keys, u, v):
    B, S, D = h.shape
    T = B * S
    ht = h.reshape(T, D)
    qh = (ht @ w_q).reshape(T, PK_HEADS, 2, PK_DQ // 2)
    s = jnp.einsum('thcd,hcnd->thcn', qh, sub_keys, preferred_element_type=F32)
    s_a, i_a = lax.top_k(s[:, :, 0], PK_TOPK)
    s_b, i_b = lax.top_k(s[:, :, 1], PK_TOPK)
    cand_s = (s_a[..., :, None] + s_b[..., None, :]).reshape(T, PK_HEADS, PK_TOPK * PK_TOPK)
    cand_i = (i_a[..., :, None] * PK_NKEYS + i_b[..., None, :]).reshape(T, PK_HEADS, PK_TOPK * PK_TOPK)
    top_s, sel = lax.top_k(cand_s, PK_TOPK)
    idx = jnp.take_along_axis(cand_i, sel, axis=-1)
    gate = jax.nn.softmax(top_s, axis=-1).astype(h.dtype)
    nblk = T // PK_TOKEN_BLOCK

    def expert_block(args):
        hb, ib, gb = args
        act = jax.nn.gelu(jnp.einsum('td,thkd->thk', hb, u[ib]), approximate=False)
        return jnp.einsum('thk,thkd->td', gb * act, v[ib])

    out = lax.map(expert_block, (ht.reshape(nblk, PK_TOKEN_BLOCK, D),
                                 idx.reshape(nblk, PK_TOKEN_BLOCK, PK_HEADS, PK_TOPK),
                                 gate.reshape(nblk, PK_TOKEN_BLOCK, PK_HEADS, PK_TOPK)))
    return out.reshape(B, S, D)

def setup_inputs(seed: int = 0) -> dict:
    key = jax.random.key(seed)
    ks = jax.random.split(key, 20)
    D = D_MODEL

    def nrm(k, shape, scale):
        return jax.random.normal(k, shape, F32) * scale

    hg_in = 2 * HG_HEADS * HG_DK + 2 * HG_HEADS * HG_DV
    at_in = 3 * AT_NGROUP * AT_HEADS * AT_HEAD_DIM
    rt_in = 2 * RT_HEADS * RT_DK + 2 * RT_HEADS * RT_DV
    hg_vd = HG_HEADS * HG_DV
    at_od = AT_HEADS * AT_HEAD_DIM
    rt_vd = RT_HEADS * RT_DV
    x = nrm(ks[0], (BATCH, SEQ, D), 1.0)
    positions = jnp.arange(SEQ, dtype=jnp.int32)[None, :] + jax.random.randint(ks[1], (BATCH, 1), 0, 1024, dtype=jnp.int32)
    return {
        'x': x,
        'positions': positions,
        'mix_norm': 1.0 + nrm(ks[2], (DEPTH, D), 0.02),
        'ffn_norm': 1.0 + nrm(ks[3], (DEPTH, D), 0.02),
        'hg_lb': nrm(ks[4], (DEPTH, HG_HEADS * HG_DK), 0.5),
        'hg_w_in': nrm(ks[5], (N_LAYERS_A, D, hg_in), D ** -0.5),
        'hg_onorm': 1.0 + nrm(ks[6], (N_LAYERS_A, hg_vd), 0.02),
        'hg_w_out': nrm(ks[7], (N_LAYERS_A, hg_vd, D), 0.5 * hg_vd ** -0.5),
        'at_w_in': nrm(ks[8], (N_LAYERS_B, D, at_in), D ** -0.5),
        'at_qnorm': 1.0 + nrm(ks[9], (N_LAYERS_B, AT_NGROUP, AT_HEAD_DIM), 0.02),
        'at_knorm': 1.0 + nrm(ks[10], (N_LAYERS_B, AT_NGROUP, AT_HEAD_DIM), 0.02),
        'at_w_out': nrm(ks[11], (N_LAYERS_B, at_od, D), 0.5 * at_od ** -0.5),
        'rt_w_in': nrm(ks[12], (N_LAYERS_C, D, rt_in), D ** -0.5),
        'rt_onorm': 1.0 + nrm(ks[13], (N_LAYERS_C, rt_vd), 0.02),
        'rt_w_out': nrm(ks[14], (N_LAYERS_C, rt_vd, D), 0.5 * rt_vd ** -0.5),
        'pk_w_q': nrm(ks[15], (DEPTH, D, PK_HEADS * PK_DQ), D ** -0.5),
        'pk_keys': nrm(ks[16], (DEPTH, PK_HEADS, 2, PK_NKEYS, PK_DQ // 2), (PK_DQ // 2) ** -0.5),
        'pk_u': nrm(ks[17], (DEPTH, PK_EXPERTS, D), D ** -0.5),
        'pk_v': nrm(ks[18], (DEPTH, PK_EXPERTS, D), 0.5 * PK_HEADS ** -0.5),
    }

def reference(x, positions, mix_norm, ffn_norm, hg_lb, hg_w_in, hg_onorm, hg_w_out,
              at_w_in, at_qnorm, at_knorm, at_w_out, rt_w_in, rt_onorm, rt_w_out,
              pk_w_q, pk_keys, pk_u, pk_v):
    lb_soft = jax.nn.softmax(hg_lb.astype(F32), axis=0)
    lb_all = jnp.cumsum(lb_soft, axis=0) - lb_soft[0:1]
    ia = 0
    ib = 0
    ic = 0
    for layer in range(DEPTH):
        h = _rmsnorm(x, mix_norm[layer])
        kind = layer % N_MIXERS
        if kind == 0:
            y = _hgrn2_mixer(h, hg_w_in[ia], hg_onorm[ia], hg_w_out[ia], lb_all[layer])
            ia += 1
        elif kind == 1:
            y = _dilated_attention_mixer(h, positions, at_w_in[ib], at_qnorm[ib], at_knorm[ib], at_w_out[ib])
            ib += 1
        else:
            y = _retention_mixer(h, positions, rt_w_in[ic], rt_onorm[ic], rt_w_out[ic])
            ic += 1
        x = x + y.astype(x.dtype)
        h = _rmsnorm(x, ffn_norm[layer])
        x = x + _peer_ffn(h, pk_w_q[layer], pk_keys[layer], pk_u[layer], pk_v[layer]).astype(x.dtype)
    return x


_drawn_inputs = setup_inputs


def setup_inputs(seed=0):
    import zlib

    import numpy as np

    out = dict(_drawn_inputs(seed))
    spreads = {}
    factors = {'hg_lb': 2.774, 'at_qnorm': 6.061, 'at_knorm': 5.983, 'rt_onorm': 5.018}
    for name, (base, spread) in spreads.items():
        noise = np.random.default_rng([zlib.crc32(name.encode()), seed]).standard_normal(out[name].shape)
        drawn = base * np.exp(spread * noise) if base else spread * noise
        out[name] = __import__('jax').numpy.asarray(drawn.astype(out[name].dtype))
    for name, factor in factors.items():
        out[name] = (out[name] * factor).astype(out[name].dtype)
    return out
```

```python
from contextlib import ExitStack
import math

import numpy as np
import concourse.bass as bass
from concourse import mybir

F32 = mybir.dt.float32
I32 = mybir.dt.int32
U32 = mybir.dt.uint32
ALU = mybir.AluOpType
ACT = mybir.ActivationFunctionType
AX = mybir.AxisListType

P = 128
D = 1024
S = 256
TILES = S // P
KT = D // P
PANEL = 512
DEPTH = 4
EPS = 1e-6
TINY = 1e-30
HEADS = 8
LEVELS = [64, 32, 16, 8, 4, 2, 1]
GROUPS = ((128, 1), (512, 4), (2048, 16))
NG = len(GROUPS)
AT_DIM = 64
RT_HEADS = 4
TOPK = 16
NKEYS = 128
SLOTS = HEADS * TOPK
RING = 16
NEG = -3.0e38
LN_SHIFT = 60
TWO_PI = 2.0 * math.pi
C1 = 6.28125
C2 = float(np.float32(np.round((TWO_PI - C1) * 2.0 ** 21) / 2.0 ** 21))
C3 = TWO_PI - C1 - C2
PI_IN = float(np.nextafter(np.float32(math.pi), np.float32(0)))


def shape_constants():
    s = np.arange(P)[:, None]
    t = np.arange(P)[None, :]
    level = [((s // (2 * m) == t // (2 * m)) & (s % (2 * m) < m) & (t % (2 * m) >= m)) for m in LEVELS]
    masks = np.stack(level, 1).astype(np.int32).reshape(P, -1)
    at = []
    for tile in range(TILES):
        q = tile * P + np.arange(P)[:, None]
        for window, dilation in GROUPS:
            k = np.arange(P * (tile + 1))[None, :]
            ok = (q >= k) & ((q - k) % dilation == 0) & ((q - k) // dilation <= window // dilation)
            at.append(np.where(ok, 0.0, -1e30))
    at = np.concatenate(at, 1).astype(np.float32)
    lg = np.log1p(-np.exp2(-5.0 - np.arange(RT_HEADS)))
    scale = 256.0 ** -0.5
    near = [np.where(t >= s, np.exp(g * np.maximum(t - s, 0)), 0.0) * scale for g in lg]
    far = [np.exp(g * (t - s + P)) * scale for g in lg]
    decay = np.stack([np.stack([n, n, f], 1) for n, f in zip(near, far)], 1)
    decay = decay.astype(np.float32).reshape(P, -1)
    theta = np.float32(10000.0)
    inv_at = theta ** (-np.arange(32, dtype=np.float32) / np.float32(32))
    inv_rt = theta ** (-np.arange(128, dtype=np.float32) / np.float32(128))
    return {
        "c_ident": np.eye(P, dtype=np.float32),
        "c_levels": masks,
        "c_window": at,
        "c_decay": decay,
        "c_inv_at": np.tile(inv_at.astype(np.float32), (P, 1)),
        "c_inv_rt": inv_rt.astype(np.float32).reshape(P, 1),
        "c_iota": np.tile(np.arange(TOPK, dtype=np.float32), (P, 1)),
    }


class Due:

    def __init__(self):
        self.value = {}

    def __call__(self, sem, more=1):
        self.value[sem.name] = self.value.get(sem.name, 0) + more
        return self.value[sem.name]


class Mine:

    def __init__(self, sem):
        self.sem, self.n = sem, 0

    def step(self, instruction):
        instruction.then_inc(self.sem, 1)
        self.n += 1


def trunk(nc, A, out):
    ctx = ExitStack()
    with ctx:
        def sb(name, shape, dt=F32):
            return ctx.enter_context(nc.sbuf_tensor(name, shape, dt))

        def pb(name, shape):
            return ctx.enter_context(nc.psum_tensor(name, shape, F32))

        def sem(name):
            return ctx.enter_context(nc.semaphore(name))

        x = sb("x", [P, TILES, D])
        hn = sb("hn", [P, TILES, D])
        hT = sb("hT", [P, KT, S])
        gain = sb("gain", [P, D])
        big = sb("big", [P, 16, D])
        wring = sb("wring", [P, 2, KT * PANEL])
        scr = sb("scr", [P, 16384])
        table = sb("table", [P, 1536])
        ident = sb("ident", [P, P])
        iota = sb("iota", [P, TOPK])
        ones = sb("ones", [P, P])
        at_gain = sb("at_gain", [P, 6, AT_DIM])
        sin_t = sb("sin_t", [P, 320])
        cos_t = sb("cos_t", [P, 320])
        rows = sb("rows", [64, P])
        feat = sb("feat", [P, 64])
        lb = sb("lb", [P, 2, 2, HEADS])
        stat = sb("stat", [P, 4, 96])
        val = sb("val", [P, 2 * HEADS, TOPK])
        nidx = sb("nidx", [P, 2 * HEADS, TOPK], U32)
        idx = sb("idx", [P, TILES, SLOTS], U32)
        gate = sb("gate", [P, TILES, SLOTS])
        act_v = sb("act_v", [P, TILES, SLOTS])
        dot16 = sb("dot16", [P, RING])
        idx16 = sb("idx16", [P, 2, RING], U32)

        PP = pb("PP", [P, 2, 1024])
        TP = pb("TP", [P, 2, 512])
        MI = pb("MI", [P, 2, 512])

        def cut(a, n):
            return scr[:, a:a + n]

        def small(a, n):
            return scr[:, 4096 + a:4096 + a + n]

        consts_in = sem("consts_in")
        x_in = sem("x_in")
        atgain_in = sem("atgain_in")
        gain_in = sem("gain_in")
        table_in = sem("table_in")
        keys_in = sem("keys_in")
        w_in = [sem(f"w_in{s}") for s in range(2)]
        pp_full = sem("pp_full")
        pp_free = [sem(f"pp_free{s}") for s in range(2)]
        tp_full = sem("tp_full")
        tp_free = [sem(f"tp_free{s}") for s in range(2)]
        x_ready = sem("x_ready")
        act_done = sem("act_done")
        dve_done = sem("dve_done")
        sq_ready = sem("sq_ready")
        ms_ready = sem("ms_ready")
        root_ready = sem("root_ready")
        hn_ready = sem("hn_ready")
        hT_ready = sem("hT_ready")
        trig_arg = sem("trig_arg")
        trig_ready = sem("trig_ready")
        feat_ready = sem("feat_ready")
        lb_arg = sem("lb_arg")
        lb_exp = sem("lb_exp")
        evac = sem("evac")
        sig_ready = sem("sig_ready")
        forget_ready = sem("forget_ready")
        log_ready = sem("log_ready")
        key_ready = sem("key_ready")
        diff_ready = sem("diff_ready")
        exp_ready = sem("exp_ready")
        pair_ready = sem("pair_ready")
        att_ready = sem("att_ready")
        o_ready = sem("o_ready")
        y_ready = sem("y_ready")
        yT_ready = sem("yT_ready")
        qk_ready = sem("qk_ready")
        sc_ready = sem("sc_ready")
        prob_ready = sem("prob_ready")
        pT_ready = sem("pT_ready")
        pv_done = sem("pv_done")
        q_ready = sem("q_ready")
        keysT_ready = sem("keysT_ready")
        s_ready = sem("s_ready")
        s_free = sem("s_free")
        idx_ready = sem("idx_ready")
        staged = sem("staged")
        turn_taken = sem("turn_taken")
        land = [sem(f"land{s}") for s in range(RING)]
        u_used = sem("u_used")
        v_used = sem("v_used")
        dots_ready = sem("dots_ready")
        shift_ready = sem("shift_ready")
        gate_exp = sem("gate_exp")
        gelu_ready = sem("gelu_ready")
        w_ready = sem("w_ready")
        diag_ready = sem("diag_ready")
        out_done = sem("out_done")

        def weights(l):
            kind, i = l % 3, l // 3
            if kind == 0:
                return A["hg_w_in"][i], 8, A["hg_w_out"][i], 1, KT
            if kind == 1:
                return A["at_w_in"][i], 9, A["at_w_out"][i], 1, 4
            return A["rt_w_in"][i], 12, A["rt_w_out"][i], 2, KT

        big_f = big[:, :, :].rearrange("p a b -> p (a b)")
        Q3 = big_f[:, 0:2048]
        E = [cut(2048 * i, 2048) for i in range(3)]
        ATT = cut(6144, 2048)
        B = cut(8192, 2048)
        ATTX = cut(10240, 1024)
        O = cut(11264, 2048)
        YT = cut(13312, 2048).rearrange("p (k s) -> p k s", k=KT)
        lvl = table[:, 0:len(LEVELS) * P].bitcast(I32).rearrange("p (l t) -> p l t", l=len(LEVELS))

        QKT = cut(0, 6144).rearrange("p (n b s) -> p n b s", n=6, b=4)
        TMP = cut(6144, 6144)
        PB = cut(6144, 1536).rearrange("p (a b) -> p a b", a=2)
        PT = cut(7680, 1536).rearrange("p (a b) -> p a b", a=2)
        AO = cut(9216, 1024).rearrange("p (t c) -> p t c", t=2)
        AYT = cut(10240, 1024).rearrange("p (k s) -> p k s", k=4)

        RTMP = [cut(2048 * i, 2048) for i in range(4)]
        RO = cut(0, 4096).rearrange("p (h t c) -> p h t c", h=4, t=2)
        RYT = cut(4096, 4096).rearrange("p (k s) -> p k s", k=16)
        RATT = cut(8192, 1536).rearrange("p (h j t) -> p h j t", h=4, j=3)
        RJ = cut(9728, 512)

        PQ = cut(0, 4096).rearrange("p (c s) -> p c s", c=16)
        KEYS = cut(4096, 2048).rearrange("p (c d) -> p c d", c=16)
        CAND = cut(14336, 2048).rearrange("p (h a b) -> p h a b", h=8, a=16)
        KEYST = cut(6144, 2048).rearrange("p (c n) -> p c n", c=16)
        SC = cut(8192, 2048).rearrange("p (c n) -> p c n", c=16)
        ONE = cut(10240, 2048).rearrange("p (h k i) -> p h k i", h=8, k=16)
        DIAG = cut(12288, 2048).rearrange("p (r n) -> p r n", r=RING)

        block = ctx.enter_context(nc.Block())

        @block.sync
        def _(sp):
            sp.dma_start(x[:, :, :], A["x"][0].rearrange("(t p) d -> p t d", p=P)).then_inc(x_in, 16)
            g = p = 0
            free_at = [0, 0]

            def panels(source, n, halves=1, kt=KT):
                nonlocal g, p
                view = source.rearrange("(h k p) (n c) -> n h p k c", p=P, k=kt, c=PANEL)
                flat = source.rearrange("(k p) n -> p k n", p=P)

                def load(src, slot, count):
                    sp.wait_ge(pp_full, count)
                    dst = wring[:, slot, 0:kt * PANEL].rearrange("p (k c) -> p k c", k=kt)
                    sp.dma_start(dst, src).then_inc(w_in[slot], 16)

                pairs = n // 2 if halves == 1 and n >= 4 else 0
                for j in range(2 if pairs else n * halves):
                    slot = (g + j) % 2
                    load(view[j // halves, j % halves], slot, free_at[slot])
                    free_at[slot] = p + j // halves + 1
                if pairs:
                    with sp.Fori(0, pairs - 1) as i:
                        for u in range(2):
                            load(flat[:, :, bass.ds((i * 2 + 2 + u) * PANEL, PANEL)], (g + u) % 2, i * 2 + (p + u + 1))
                    for j in range(n - 2, n):
                        free_at[(g + j) % 2] = p + j + 1
                    if n % 2:
                        slot = (g + n - 1) % 2
                        load(view[n - 1, 0], slot, p + n - 2)
                g += n * halves
                p += n

            for l in range(DEPTH):
                w, n, wo, halves, kt = weights(l)
                panels(w, n)
                p += (19, 16, 8)[l % 3]
                panels(wo, 2, halves, kt)
                panels(A["pk_w_q"][l], 4)
                p += 6
            sp.wait_ge(x_ready, 4 * DEPTH)
            sp.dma_start(out[0].rearrange("(t p) d -> p t d", p=P), x[:, :, :]).then_inc(out_done, 16)
            sp.wait_ge(out_done, 16)

        @block.gpsimd
        def _(pool):
            due = Due()
            pool.dma_start(ident[:, :], A["c_ident"]).then_inc(consts_in, 16)
            pool.dma_start(iota[:, :], A["c_iota"]).then_inc(consts_in, 16)
            pool.dma_start(rows[0:32, :], A["hg_lb"].rearrange("l (h p) -> (l h) p", p=P)).then_inc(consts_in, 16)
            pool.dma_start(rows[32:48, :], A["hg_onorm"].rearrange("l (h p) -> (l h) p", p=P)).then_inc(consts_in, 16)
            pool.dma_start(rows[48:64, :], A["rt_onorm"].rearrange("l (h p) -> (l h) p", p=P)).then_inc(consts_in, 16)
            pool.dma_start(E[0][:, 0:256].bitcast(I32), A["positions"].to_broadcast([P, S])).then_inc(consts_in, 16)
            pool.dma_start(E[0][:, 256:258].bitcast(I32), A["positions"].rearrange("a (t p) -> p (a t)", p=P),
                           allow_slow_non_contiguous=True).then_inc(consts_in, 16)
            pool.dma_start(E[0][:, 258:259], A["c_inv_rt"]).then_inc(consts_in, 16)
            pool.dma_start(E[0][:, 260:292], A["c_inv_at"]).then_inc(consts_in, 16)

            for n, name in enumerate(("at_qnorm", "at_knorm")):
                pool.dma_start(at_gain[:, 3 * n:3 * n + 3, :],
                               A[name][0].unsqueeze(0).to_broadcast([P, NG, AT_DIM])).then_inc(atgain_in, 16)

            def gather_group(src, t, half, column, waits):
                pool.tensor_copy(idx16[:, half, :], idx[:, t, bass.ds(column, RING)]).then_inc(staged, 1)
                for r in range(RING):
                    sem_used, count = waits
                    if sem_used is not None:
                        pool.wait_ge(sem_used, count + r + 1)
                    pool.wait_ge(staged, pool_steps[0])
                    pool.sem_inc(turn_taken, 1)
                    pool.indirect_dma_start(
                        big[:, r, :], None, src,
                        bass.IndirectOffsetOnAxis(ap=idx16[:, half, r:r + 1], axis=0),
                        element_offset=l * NKEYS * NKEYS * D).then_inc(land[r], 16)

            pool_steps = [0]
            n_u = n_v = 0
            for l in range(DEPTH):
                kind = l % 3
                if l:
                    pool.wait_ge(hn_ready, due(hn_ready, TILES))
                pool.dma_start(gain[:, :], A["mix_norm"][l:l + 1].to_broadcast([P, D])).then_inc(gain_in, 16)
                if l:
                    pool.wait_ge(x_ready, 4 * l - 2)
                name = ("c_levels", "c_window", "c_decay")[kind]
                cols = (len(LEVELS) * P, 3 * P * 3, 1536)[kind]
                dst = table[:, 0:cols].bitcast(I32) if kind == 0 else table[:, 0:cols]
                pool.dma_start(dst, A[name]).then_inc(table_in, 16)
                pool.wait_ge(hn_ready, due(hn_ready, TILES))
                pool.dma_start(gain[:, :], A["ffn_norm"][l:l + 1].to_broadcast([P, D])).then_inc(gain_in, 16)
                pool.wait_ge(x_ready, 4 * l + 2)
                pool.dma_start(KEYS, A["pk_keys"][l].rearrange("h c n d -> n (h c) d")).then_inc(keys_in, 16)
                for t in range(TILES):
                    pool.wait_ge(idx_ready, due(idx_ready))
                    for phase in range(2):
                        src = (A["pk_u"], A["pk_v"])[phase].rearrange("l e d -> (l e) d")
                        used, base = ((u_used, n_u), (v_used, n_v))[phase]
                        other, count = ((v_used, n_v), (u_used, n_u))[phase]
                        groups = SLOTS // RING
                        first = (other, count - RING) if count else (None, 0)
                        steps0 = pool_steps[0]
                        pool_steps[0] = steps0 + 1
                        gather_group(src, t, 0, 0, first)
                        with pool.Fori(0, groups // 2 - 1) as i:
                            for k in range(2):
                                pool_steps[0] = steps0 + 2 + k + i * 2
                                gather_group(src, t, 1 - k, i * (2 * RING) + RING * (1 + k),
                                             (used, base + i * (2 * RING) + RING * k))
                        pool_steps[0] = steps0 + groups
                        gather_group(src, t, 1, SLOTS - RING, (used, base + SLOTS - 2 * RING))
                        if phase == 0:
                            n_u += SLOTS
                        else:
                            n_v += SLOTS

        @block.tensor
        def _(pe):
            due = Due()
            state = {"g": 0, "p": 0, "k": 0}

            def wait_pp():
                p = state["p"]
                pe.wait_ge(pp_free[p % 2], p // 2 + 1)
                state["p"] = p + 1
                return PP[:, p % 2, :]

            def turn(blocks, offset=0):
                k = state["k"]
                pe.wait_ge(tp_free[k % 2], k // 2)
                for j, b in enumerate(blocks):
                    last = pe.transpose(TP[0:b.shape[-1], k % 2, j * P:j * P + b.shape[0]], b,
                                        ident[0:b.shape[0], 0:b.shape[0]])
                last.then_inc(tp_full, 1)
                state["k"] = k + 1

            def project(n, feature_major, src, kt=KT, halves=1):
                g, p = state["g"], state["p"]

                def panel(slot, w_turn, ps, p_turn, half):
                    pe.wait_ge(w_in[slot], w_turn * 16 + 16)
                    if half == 0:
                        pe.wait_ge(pp_free[ps], p_turn + 1)
                    w = wring[:, slot, 0:kt * PANEL].rearrange("p (k c) -> p k c", k=kt)
                    for o in range(4 if feature_major else TILES):
                        for k in range(kt):
                            flags = dict(start=(half == 0 and k == 0), stop=(half == halves - 1 and k == kt - 1))
                            if feature_major:
                                last = pe.matmul(PP[:, ps, o * S:(o + 1) * S], w[:, k, o * P:(o + 1) * P],
                                                 src[:, k, :], **flags)
                            else:
                                last = pe.matmul(PP[:, ps, o * PANEL:(o + 1) * PANEL],
                                                 src[:, half * kt + k, o * P:(o + 1) * P], w[:, k, :], **flags)
                    if half == halves - 1:
                        last.then_inc(pp_full, 1)

                pairs = n // 2 if halves == 1 and n >= 4 else 0
                if pairs:
                    with pe.Fori(0, pairs) as i:
                        for u in range(2):
                            panel((g + u) % 2, i + (g + u) // 2, (p + u) % 2, i + (p + u) // 2, 0)
                for j in range(2 * pairs, n):
                    for half in range(halves):
                        m = g + j * halves + half
                        panel(m % 2, m // 2, (p + j) % 2, (p + j) // 2, half)
                state["g"], state["p"] = g + n * halves, p + n

            def norm_turn():
                for t in range(TILES):
                    pe.wait_ge(hn_ready, due(hn_ready))
                    for half in range(2):
                        turn([hn[:, t, (4 * half + j) * P:(4 * half + j + 1) * P] for j in range(4)])
                pe.wait_ge(hT_ready, due(hT_ready, 4))

            def hgrn(l):
                project(4, True, hT)
                project(4, False, hT)
                pe.wait_ge(key_ready, due(key_ready))
                kk = big_f[:, 8 * D:10 * D]
                for f in range(2):
                    ps = wait_pp()
                    for j in range(8):
                        c = (8 * f + j) * P
                        last = pe.matmul(ps[:, j * P:(j + 1) * P], kk[:, c:c + P], Q3[:, c:c + P],
                                         start=True, stop=True)
                    last.then_inc(pp_full, 1)
                for n in range(len(LEVELS)):
                    pe.wait_ge(pair_ready, due(pair_ready))
                    for f in range(2):
                        ps = wait_pp()
                        for j in range(8):
                            c = (8 * f + j) * P
                            last = pe.matmul(ps[:, j * P:(j + 1) * P], E[n % 3][:, c:c + P], E[n % 3][:, c:c + P],
                                             start=True, stop=True)
                        last.then_inc(pp_full, 1)
                n = len(LEVELS)
                pe.wait_ge(pair_ready, due(pair_ready))
                ps = wait_pp()
                for h in range(HEADS):
                    c = h * S
                    last = pe.matmul(ps[:, h * P:(h + 1) * P], E[n % 3][:, c:c + P], E[n % 3][:, c + P:c + S],
                                     start=True, stop=True)
                last.then_inc(pp_full, 1)
                pe.wait_ge(att_ready, due(att_ready))
                pe.wait_ge(evac, due(evac, 8))
                for c in range(2):
                    ps = wait_pp()
                    for t in range(TILES):
                        for j in range(4):
                            h = 4 * c + j
                            o = ps[:, t * PANEL + j * P:t * PANEL + (j + 1) * P]
                            v = [big[:, 4 + c, s * PANEL + j * P:s * PANEL + (j + 1) * P] for s in range(2)]
                            a = ATT[:, (2 * h + t) * P:(2 * h + t + 1) * P]
                            last = pe.matmul(o, a, v[t], start=True, stop=(t == 0))
                            if t:
                                last = pe.matmul(o, ATTX[:, h * P:(h + 1) * P], v[0], start=False, stop=True)
                    last.then_inc(pp_full, 1)
                pe.wait_ge(y_ready, due(y_ready))
                for t in range(TILES):
                    for c in range(2):
                        b = c * 1024 + t * PANEL
                        turn([O[:, b + j * P:b + (j + 1) * P] for j in range(4)])
                pe.wait_ge(yT_ready, due(yT_ready, 4))
                project(2, False, YT)

            def attention(l):
                project(9, False, hT)
                for n in range(6):
                    pe.wait_ge(qk_ready, due(qk_ready))
                    for t in range(TILES):
                        turn([big[:, n, t * PANEL + j * P:t * PANEL + (j + 1) * P] for j in range(4)])
                pe.wait_ge(yT_ready, due(yT_ready, 12))
                pe.wait_ge(evac, due(evac, 9))

                def scores(it):
                    t, h = it // HEADS, it % HEADS
                    a = (h % 2) * AT_DIM
                    ps = wait_pp()
                    for g in range(NG):
                        last = pe.matmul(ps[:, g * S:g * S + P * (t + 1)],
                                         QKT[a:a + AT_DIM, g, h // 2, t * P:(t + 1) * P],
                                         QKT[a:a + AT_DIM, 3 + g, h // 2, 0:P * (t + 1)], start=True, stop=True)
                    last.then_inc(pp_full, 1)

                def values(it):
                    t, h = it // HEADS, it % HEADS
                    pe.wait_ge(prob_ready, due(prob_ready))
                    for half in range(t + 1):
                        turn([PB[:, it % 2, (3 * half + j) * P:(3 * half + j + 1) * P] for j in range(3)])
                    pe.wait_ge(pT_ready, due(pT_ready, t + 1))
                    for b in range(3 * (t + 1)):
                        g, s = b // (t + 1), b % (t + 1)
                        last = pe.matmul(MI[:, t, h * AT_DIM:(h + 1) * AT_DIM], PT[:, it % 2, b * P:(b + 1) * P],
                                         big[:, 6 + g, s * PANEL + h * AT_DIM:s * PANEL + (h + 1) * AT_DIM],
                                         start=(b == 0), stop=(b == 3 * (t + 1) - 1))
                    last.then_inc(pv_done, 1)

                scores(0)
                for it in range(2 * HEADS):
                    if it + 1 < 2 * HEADS:
                        scores(it + 1)
                    values(it)
                pe.wait_ge(y_ready, due(y_ready))
                for t in range(TILES):
                    turn([AO[:, t, j * P:(j + 1) * P] for j in range(4)])
                pe.wait_ge(yT_ready, due(yT_ready, 2))
                project(2, False, AYT, kt=4)

            def retention(l):
                project(4, True, hT)
                project(8, False, hT)
                pe.wait_ge(qk_ready, due(qk_ready))
                for h in range(RT_HEADS):
                    ps = wait_pp()
                    for j, (s, t) in enumerate(((0, 0), (1, 1), (0, 1))):
                        for b in range(2):
                            q = big_f[:, (2 * h + b) * S + t * P:(2 * h + b) * S + (t + 1) * P]
                            k = big_f[:, (8 + 2 * h + b) * S + s * P:(8 + 2 * h + b) * S + (s + 1) * P]
                            last = pe.matmul(ps[:, j * P:(j + 1) * P], k, q, start=(b == 0), stop=(b == 1))
                    last.then_inc(pp_full, 1)
                pe.wait_ge(evac, due(evac, 12))
                for h in range(RT_HEADS):
                    pe.wait_ge(att_ready, due(att_ready))
                    ps = wait_pp()
                    v = [big[:, 4 + h, s * PANEL:(s + 1) * PANEL] for s in range(2)]
                    pe.matmul(ps[:, 0:PANEL], RATT[:, h, 0, :], v[0], start=True, stop=True)
                    pe.matmul(ps[:, PANEL:], RATT[:, h, 1, :], v[1], start=True, stop=False)
                    pe.matmul(ps[:, PANEL:], RATT[:, h, 2, :], v[0], start=False, stop=True).then_inc(pp_full, 1)
                for h in range(RT_HEADS):
                    pe.wait_ge(y_ready, due(y_ready))
                    for t in range(TILES):
                        turn([RO[:, h, t, j * P:(j + 1) * P] for j in range(4)])
                pe.wait_ge(yT_ready, due(yT_ready, 8))
                project(2, False, RYT, halves=2)

            def peer(l):
                project(4, True, hT)
                pe.wait_ge(keys_in, due(keys_in, 16))
                for c in range(4):
                    turn([KEYS[:, 4 * c + j, :] for j in range(4)])
                pe.wait_ge(keysT_ready, due(keysT_ready, 4))
                pe.wait_ge(q_ready, due(q_ready, 4))
                for t in range(TILES):
                    for f in range(2):
                        ps = wait_pp()
                        for j in range(8):
                            c = 8 * f + j
                            last = pe.matmul(ps[:, j * P:(j + 1) * P], PQ[:, c, t * P:(t + 1) * P], KEYST[:, c, :],
                                             start=True, stop=True)
                        last.then_inc(pp_full, 1)
                for t in range(TILES):
                    ps = wait_pp()
                    for c in range(2):
                        pe.matmul(ps[:, c * PANEL:(c + 1) * PANEL], ident[:, :], x[:, t, c * PANEL:(c + 1) * PANEL],
                                  start=True, stop=False, skip_group_check=True)
                    base = (l * TILES + t) * SLOTS
                    turns = (l * TILES + t) * 2 * SLOTS // RING + SLOTS // RING

                    def group(i, end):
                        for r in range(RING):
                            pe.wait_ge(land[r], i * 16 + (turns + 1) * 16)
                            pe.wait_ge(diag_ready, i * RING + base + r + 1)
                            for c in range(2):
                                last = pe.matmul(ps[:, c * PANEL:(c + 1) * PANEL], DIAG[:, r, :],
                                                 big[:, r, c * PANEL:(c + 1) * PANEL], start=False,
                                                 stop=(end and r == RING - 1), skip_group_check=True)
                            last.then_inc(v_used, 1)

                    with pe.Fori(0, SLOTS // RING - 1) as i:
                        group(i, False)
                    group(SLOTS // RING - 1, True)
                    pe.wait_ge(v_used, base + SLOTS)
                    pe.nop().then_inc(pp_full, 1)

            pe.wait_ge(consts_in, 16 * 9)
            turn([rows[:, :]])
            pe.wait_ge(x_in, 16)
            for l in range(DEPTH):
                norm_turn()
                (hgrn, attention, retention)[l % 3](l)
                norm_turn()
                peer(l)

        @block.scalar
        def _(act):
            due = Due()
            mine = Mine(act_done)
            state = {"p": 0, "k": 0}

            def settle():
                act.wait_ge(act_done, mine.n)

            def take_pp():
                p = state["p"]
                act.wait_ge(pp_full, p + 1)
                state["p"] = p + 1
                return PP[:, p % 2, :], pp_free[p % 2]

            def take_tp():
                k = state["k"]
                act.wait_ge(tp_full, k + 1)
                state["k"] = k + 1
                return TP[:, k % 2, :], tp_free[k % 2]

            def to_features(dst, ready, blocks=4):
                tp, free = take_tp()
                mine.step(act.activation(dst, tp[:, 0:blocks * P].rearrange("p (b c) -> p b c", b=blocks), ACT.Copy))
                settle()
                act.nop().then_inc(free, 1)
                act.nop().then_inc(ready, 1)

            def norm(first):
                for t in range(TILES):
                    if first:
                        act.wait_ge(x_in, 16)
                    elif t == 0:
                        act.wait_ge(x_ready, due(x_ready, 2))
                    act.activation(hn[:, t, :], x[:, t, :], ACT.Square, accum_out=stat[:, 0, t:t + 1]).then_inc(sq_ready, 1)
                act.wait_ge(ms_ready, due(ms_ready))
                act.activation(stat[:, 2, 0:TILES], stat[:, 1, 0:TILES], ACT.Sqrt).then_inc(root_ready, 1)
                for t in range(TILES):
                    for half in range(2):
                        to_features(hT[:, 4 * half:4 * half + 4, t * P:(t + 1) * P], hT_ready)

            def move_panels(first, n, func=ACT.Copy):
                for j in range(first, first + n):
                    ps, free = take_pp()
                    mine.step(act.activation(big[:, j, :], ps, func))
                    settle()
                    act.nop().then_inc(free, 1)
                    act.nop().then_inc(evac, 1)

            def root(n):
                act.wait_ge(ms_ready, due(ms_ready))
                act.activation(stat[:, 2, 0:n], stat[:, 1, 0:n], ACT.Sqrt).then_inc(root_ready, 1)

            def hgrn(l):
                move_panels(0, 2, ACT.Silu)
                move_panels(2, 2)
                f = big_f[:, 2 * D:4 * D]
                act.activation(big_f[:, 10 * D:12 * D], f, ACT.Sigmoid, scale=-1.0).then_inc(sig_ready, 1)
                act.activation(big_f[:, 12 * D:14 * D], f, ACT.Sigmoid).then_inc(sig_ready, 1)
                move_panels(4, 4)
                act.wait_ge(forget_ready, due(forget_ready))
                act.activation(B, big_f[:, 12 * D:14 * D], ACT.Ln).then_inc(log_ready, 1)
                state["p"] += 2
                for n in range(len(LEVELS) + 1):
                    act.wait_ge(diff_ready, due(diff_ready))
                    act.activation(E[n % 3], E[n % 3], ACT.Exp).then_inc(exp_ready, 1)
                    state["p"] += 2 if n < len(LEVELS) else 1
                settle()
                mine.step(act.activation(big[:, 6:8, :], big[:, 6:8, :], ACT.Silu))
                for c in range(2):
                    ps, free = take_pp()
                    mine.step(act.activation(O[:, c * 1024:(c + 1) * 1024], ps, ACT.Copy))
                    settle()
                    act.nop().then_inc(free, 1)
                act.activation(E[0], O, ACT.Square).then_inc(o_ready, 1)
                root(16)
                state["k"] += 4
                state["p"] += 2

            def attention(l):
                move_panels(0, 9)
                for n in range(2):
                    act.activation(TMP[:, n * 3072:(n + 1) * 3072], big_f[:, n * 3072:(n + 1) * 3072],
                                   ACT.Square).then_inc(o_ready, 1)
                root(96)
                due(qk_ready, 6)
                for n in range(6):
                    for t in range(TILES):
                        to_features(QKT[:, n, :, t * P:(t + 1) * P], yT_ready)
                for it in range(2 * HEADS):
                    t = it // HEADS
                    w = 3 * P * (t + 1)
                    state["p"] += 1
                    act.wait_ge(sc_ready, due(sc_ready))
                    act.activation(PB[:, it % 2, 0:w], PB[:, it % 2, 0:w], ACT.Exp, bias=stat[:, 0, it:it + 1],
                                   accum_out=stat[:, 1, it:it + 1]).then_inc(prob_ready, 1)
                    if it >= 2:
                        act.wait_ge(pv_done, due(pv_done))
                    for half in range(t + 1):
                        to_features(PT[:, it % 2, 3 * half * P:(3 * half + 3) * P].rearrange("p (b c) -> p b c", b=3),
                                    pT_ready, 3)
                due(pv_done, 2)
                for t in range(TILES):
                    to_features(AYT[:, :, t * P:(t + 1) * P], yT_ready)
                state["p"] += 2

            def retention(l):
                move_panels(0, 8)
                move_panels(8, 4, ACT.Silu)
                state["p"] += 4
                for h in range(RT_HEADS):
                    ps, free = take_pp()
                    if h == 0:
                        act.wait_ge(qk_ready, due(qk_ready))
                    mine.step(act.activation(RO[:, h, :, :].rearrange("p t c -> p (t c)"), ps, ACT.Copy))
                    for t in range(TILES):
                        settle()
                        mine.step(act.activation(RJ, ps[:, t * PANEL:(t + 1) * PANEL], ACT.Square,
                                                 accum_out=stat[:, 0, 2 * h + t:2 * h + t + 1]))
                    settle()
                    act.nop().then_inc(free, 1)
                act.nop().then_inc(o_ready, 1)
                root(8)
                state["k"] += 8
                state["p"] += 2

            def peer(l):
                for j in range(4):
                    ps, free = take_pp()
                    mine.step(act.activation(PQ[:, 4 * j:4 * j + 4, :].rearrange("p c s -> p (c s)"), ps, ACT.Copy))
                    settle()
                    act.nop().then_inc(free, 1)
                    act.nop().then_inc(q_ready, 1)
                for c in range(4):
                    to_features(KEYST[:, 4 * c:4 * c + 4, :], keysT_ready)
                for t in range(TILES):
                    if t:
                        act.wait_ge(s_free, due(s_free))
                    for f in range(2):
                        ps, free = take_pp()
                        mine.step(act.activation(SC[:, 8 * f:8 * f + 8, :].rearrange("p c n -> p (c n)"), ps, ACT.Copy))
                        settle()
                        act.nop().then_inc(free, 1)
                    act.nop().then_inc(s_ready, 1)
                due(s_free)
                for t in range(TILES):
                    act.wait_ge(shift_ready, due(shift_ready))
                    act.activation(gate[:, t, :], gate[:, t, :], ACT.Exp).then_inc(gate_exp, 1)
                    act.wait_ge(dots_ready, due(dots_ready))
                    act.activation(act_v[:, t, :], act_v[:, t, :], ACT.Gelu).then_inc(gelu_ready, 1)
                    act.wait_ge(w_ready, due(w_ready))
                    base = (l * TILES + t) * SLOTS

                    def group(i, before):
                        for r in range(RING):
                            if before is not None:
                                act.wait_ge(v_used, before + r + 1)
                            act.wait_ge(w_ready, due(w_ready, 0))
                            act.activation(DIAG[:, r, :], ident[:, :], ACT.Copy,
                                           scale=act_v[:, t, bass.ds(i * RING + r, 1)]).then_inc(diag_ready, 1)

                    group(0, base - RING if base else None)
                    with act.Fori(0, SLOTS // RING - 1) as i:
                        group(i + 1, base + i * RING)
                    state["p"] += 1

            act.wait_ge(trig_arg, due(trig_arg))
            act.activation(sin_t[:, :], sin_t[:, :], ACT.Sin).then_inc(trig_ready, 1)
            act.activation(cos_t[:, :], cos_t[:, :], ACT.Sin).then_inc(trig_ready, 1)
            state["k"] += 1
            act.wait_ge(lb_arg, due(lb_arg))
            act.activation(feat[:, 0:32], feat[:, 0:32], ACT.Exp).then_inc(lb_exp, 1)
            for l in range(DEPTH):
                norm(l == 0)
                (hgrn, attention, retention)[l % 3](l)
                norm(False)
                peer(l)

        @block.vector
        def _(dve):
            due = Due()
            mine = Mine(dve_done)
            state = {"p": 0, "k": 0}
            step = mine.step

            def settle():
                dve.wait_ge(dve_done, mine.n)

            def take_pp():
                p = state["p"]
                dve.wait_ge(pp_full, p + 1)
                state["p"] = p + 1
                return PP[:, p % 2, :], pp_free[p % 2]

            def take_tp():
                k = state["k"]
                dve.wait_ge(tp_full, k + 1)
                state["k"] = k + 1
                return TP[:, k % 2, :], tp_free[k % 2]

            def do(instruction):
                step(instruction)
                settle()

            def tell(sem_):
                settle()
                dve.nop().then_inc(sem_, 1)

            def inverse_root(n, width):
                do(dve.tensor_scalar(stat[:, 1, 0:n], stat[:, 0, 0:n], 1.0 / width, EPS, ALU.mult, ALU.add))
                tell(ms_ready)
                dve.wait_ge(root_ready, due(root_ready))
                do(dve.reciprocal(stat[:, 2, 0:n], stat[:, 2, 0:n]))

            def norm():
                dve.wait_ge(sq_ready, due(sq_ready, TILES))
                inverse_root(TILES, D)
                dve.wait_ge(gain_in, due(gain_in, 16))
                for t in range(TILES):
                    dve.scalar_tensor_tensor(hn[:, t, :], x[:, t, :], stat[:, 2, t:t + 1], gain[:, :],
                                             ALU.mult, ALU.mult).then_inc(hn_ready, 1)
                dve.wait_ge(hn_ready, due(hn_ready, TILES))
                state["k"] += 4

            def residual():
                for c in range(2):
                    ps, free = take_pp()
                    xs = x[:, :, c * PANEL:(c + 1) * PANEL]
                    do(dve.tensor_tensor(xs, ps.rearrange("p (t n) -> p t n", t=TILES), xs, ALU.add))
                    dve.nop().then_inc(free, 1)
                    dve.nop().then_inc(x_ready, 1)

            def gained(dst, first, n=4):
                tp, free = take_tp()
                g = feat[:, first:first + n].unsqueeze(2).to_broadcast([P, n, P])
                do(dve.tensor_tensor(dst, tp.rearrange("p (b c) -> p b c", b=n), g, ALU.mult))
                dve.nop().then_inc(free, 1)
                dve.nop().then_inc(yT_ready, 1)

            def hgrn(l):
                n_l = l // 3
                state["p"] += 8
                lbb = lb[:, n_l, 0, :].unsqueeze(2).to_broadcast([P, HEADS, S])
                omb = lb[:, n_l, 1, :].unsqueeze(2).to_broadcast([P, HEADS, S])

                def by_head(a):
                    return a.rearrange("p (h s) -> p h s", h=HEADS)

                kk = big_f[:, 8 * D:10 * D]
                neg = big_f[:, 10 * D:12 * D]
                fg = big_f[:, 12 * D:14 * D]
                up = big_f[:, 14 * D:16 * D]
                dve.wait_ge(sig_ready, due(sig_ready))
                do(dve.tensor_tensor(by_head(kk), by_head(neg), omb, ALU.mult))
                dve.wait_ge(evac, due(evac, 2))
                dve.nop().then_inc(key_ready, 1)
                due(evac, 6)
                dve.wait_ge(sig_ready, due(sig_ready))
                do(dve.tensor_tensor(by_head(fg), by_head(fg), omb, ALU.mult))
                do(dve.tensor_tensor(by_head(fg), by_head(fg), lbb, ALU.add))
                do(dve.tensor_scalar(fg, fg, TINY, None, ALU.max))
                do(dve.tensor_scalar(neg, fg, 2.0 ** -40, None, ALU.is_lt))
                do(dve.tensor_scalar(up, neg, 2.0 ** LN_SHIFT, 1.0, ALU.mult, ALU.add))
                do(dve.tensor_tensor(fg, fg, up, ALU.mult))
                dve.nop().then_inc(forget_ready, 1)
                for f in range(2):
                    ps, free = take_pp()
                    a = ATT[:, f * 1024:(f + 1) * 1024].rearrange("p (n t) -> p n t", n=8)
                    idb = ident[:, :].unsqueeze(1).to_broadcast([P, 8, P])
                    do(dve.tensor_tensor(a, ps.rearrange("p (n t) -> p n t", n=8), idb, ALU.mult))
                    dve.nop().then_inc(free, 1)
                dve.wait_ge(log_ready, due(log_ready))
                do(dve.scalar_tensor_tensor(fg, neg, -LN_SHIFT * math.log(2.0), B, ALU.mult, ALU.add))
                for n in range(2 * HEADS):
                    seg = slice(n * P, (n + 1) * P)
                    step(dve.tensor_tensor_scan(B[:, seg], ones[:, :], fg[:, seg], 0.0, ALU.mult, ALU.add))
                settle()
                dve.wait_ge(table_in, due(table_in, 16))

                def halves(a, m):
                    v = a.rearrange("p (n two m) -> p n two m", two=2, m=m)
                    return v[:, :, 0, :], v[:, :, 1, :]

                def middle(m):
                    b0, b1 = halves(B, m)
                    return b0[:, :, m - 1:m].to_broadcast([P, 2048 // (2 * m), m])

                def level(n):
                    return LEVELS[n] if n < len(LEVELS) else P

                def diffs(n):
                    m = level(n)
                    e0, e1 = halves(E[n % 3], m)
                    b0, b1 = halves(B, m)
                    step(dve.tensor_tensor(e0, middle(m), b0, ALU.subtract))
                    if m < P:
                        step(dve.tensor_tensor(e1, b1, middle(m), ALU.subtract))
                    else:
                        step(dve.tensor_copy(e1, b1))
                    tell(diff_ready)

                def products(n):
                    m = level(n)
                    dve.wait_ge(exp_ready, due(exp_ready))
                    e0, e1 = halves(E[n % 3], m)
                    step(dve.tensor_tensor(e0, e0, halves(kk, m)[0], ALU.mult))
                    step(dve.tensor_tensor(e1, e1, halves(Q3, m)[1], ALU.mult))
                    tell(pair_ready)

                def select(n):
                    if n == len(LEVELS):
                        ps, free = take_pp()
                        do(dve.tensor_copy(ATTX, ps))
                        dve.nop().then_inc(free, 1)
                        return
                    for f in range(2):
                        ps, free = take_pp()
                        a = ATT[:, f * 1024:(f + 1) * 1024].rearrange("p (n t) -> p n t", n=8)
                        mask = lvl[:, n, :].unsqueeze(1).to_broadcast([P, 8, P])
                        do(dve.copy_predicated(a, mask, ps.rearrange("p (n t) -> p n t", n=8)))
                        dve.nop().then_inc(free, 1)

                total = len(LEVELS) + 1
                diffs(0)
                for n in range(total):
                    if n + 1 < total:
                        diffs(n + 1)
                    products(n)
                    if n:
                        select(n - 1)
                select(total - 1)
                tell(att_ready)
                state["p"] += 2
                dve.wait_ge(o_ready, due(o_ready))
                do(dve.tensor_reduce(stat[:, 0, 0:16], E[0].rearrange("p (n c) -> p n c", c=P), AX.X, ALU.add))
                inverse_root(16, P)
                do(dve.tensor_tensor(O.rearrange("p (n c) -> p n c", c=P), O.rearrange("p (n c) -> p n c", c=P),
                                     stat[:, 2, 0:16].unsqueeze(2).to_broadcast([P, 16, P]), ALU.mult))
                do(dve.tensor_tensor(O, O, big_f[:, 6 * D:8 * D], ALU.mult))
                dve.nop().then_inc(y_ready, 1)
                for t in range(TILES):
                    for c in range(2):
                        gained(YT[:, 4 * c:4 * c + 4, t * P:(t + 1) * P], 32 + 8 * n_l + 4 * c)
                residual()

            def attention(l):
                state["p"] += 9
                due(evac, 9)
                qk = big_f[:, 0:6 * D]
                v64 = qk.rearrange("p (n c) -> p n c", c=AT_DIM)
                dve.wait_ge(o_ready, due(o_ready, 2))
                do(dve.tensor_reduce(stat[:, 0, 0:96], TMP.rearrange("p (n c) -> p n c", c=AT_DIM), AX.X, ALU.add))
                inverse_root(96, AT_DIM)
                do(dve.tensor_tensor(v64, v64, stat[:, 2, 0:96].unsqueeze(2).to_broadcast([P, 96, AT_DIM]), ALU.mult))
                dve.wait_ge(atgain_in, 32)
                do(dve.tensor_tensor(qk.rearrange("p (n h c) -> p n h c", n=6, c=AT_DIM),
                                     qk.rearrange("p (n h c) -> p n h c", n=6, c=AT_DIM),
                                     at_gain[:, :, :].unsqueeze(2).to_broadcast([P, 6, 16, AT_DIM]), ALU.mult))
                for n in range(6):
                    v = big[:, n, :].rearrange("p (t h a c) -> p t h a c", t=2, h=8, a=2)
                    w = TMP[:, 0:2048].rearrange("p (a t h c) -> p a t h c", a=4, t=2, h=8)
                    for t in range(TILES):
                        x1, x2 = v[:, t, :, 0, :], v[:, t, :, 1, :]
                        c = cos_t[:, 256 + 32 * t:288 + 32 * t].unsqueeze(1).to_broadcast([P, 8, 32])
                        s = sin_t[:, 256 + 32 * t:288 + 32 * t].unsqueeze(1).to_broadcast([P, 8, 32])
                        step(dve.tensor_tensor(w[:, 0, t], x1, c, ALU.mult))
                        step(dve.tensor_tensor(w[:, 1, t], x2, s, ALU.mult))
                        step(dve.tensor_tensor(w[:, 2, t], x2, c, ALU.mult))
                        step(dve.tensor_tensor(w[:, 3, t], x1, s, ALU.mult))
                    settle()
                    for t in range(TILES):
                        step(dve.tensor_tensor(v[:, t, :, 0, :], w[:, 0, t], w[:, 1, t], ALU.subtract))
                        step(dve.tensor_tensor(v[:, t, :, 1, :], w[:, 2, t], w[:, 3, t], ALU.add))
                    tell(qk_ready)
                state["k"] += 12
                dve.wait_ge(table_in, due(table_in, 16))
                for it in range(2 * HEADS):
                    t = it // HEADS
                    n = P * (t + 1)
                    ps, free = take_pp()
                    if it >= 2:
                        k_done = state["k"] + (it - 1 if it - 1 <= HEADS else HEADS + 2 * (it - 1 - HEADS))
                        dve.wait_ge(tp_full, k_done)
                    pb_ = PB[:, it % 2, 0:3 * n].rearrange("p (g k) -> p g k", g=NG)
                    mask = table[:, 3 * P * t:3 * P * t + 3 * n].rearrange("p (g k) -> p g k", g=NG)
                    do(dve.scalar_tensor_tensor(pb_, ps[:, 0:3 * S].rearrange("p (g k) -> p g k", g=NG)[:, :, 0:n],
                                                AT_DIM ** -0.5, mask, ALU.mult, ALU.add))
                    dve.nop().then_inc(free, 1)
                    do(dve.tensor_reduce(stat[:, 0, it:it + 1], PB[:, it % 2, 0:3 * n], AX.X, ALU.max, negate=True))
                    dve.nop().then_inc(sc_ready, 1)
                state["k"] += 8 + 16
                dve.wait_ge(pv_done, due(pv_done, 16))
                dve.wait_ge(prob_ready, due(prob_ready, 16))
                do(dve.reciprocal(stat[:, 2, 0:16], stat[:, 1, 0:16]))
                do(dve.tensor_tensor(AO.rearrange("p t (h c) -> p (t h) c", h=8),
                                     MI[:, :, :].rearrange("p t (h c) -> p (t h) c", h=8),
                                     stat[:, 2, 0:16].unsqueeze(2).to_broadcast([P, 16, AT_DIM]), ALU.mult))
                dve.nop().then_inc(y_ready, 1)
                state["k"] += 2
                residual()

            def retention(l):
                state["p"] += 12
                dve.wait_ge(evac, due(evac, 4))
                due(evac, 8)
                v = big_f[:, 0:4 * D].rearrange("p (h a s) -> p h a s", a=2, s=S)
                x1, x2 = v[:, :, 0, :], v[:, :, 1, :]
                c = cos_t[:, 0:S].unsqueeze(1).to_broadcast([P, 8, S])
                s = sin_t[:, 0:S].unsqueeze(1).to_broadcast([P, 8, S])
                w = [r.rearrange("p (h s) -> p h s", h=8) for r in RTMP]
                step(dve.tensor_tensor(w[0], x1, c, ALU.mult))
                step(dve.tensor_tensor(w[1], x2, s, ALU.mult))
                step(dve.tensor_tensor(w[2], x2, c, ALU.mult))
                do(dve.tensor_tensor(w[3], x1, s, ALU.mult))
                step(dve.tensor_tensor(x1, w[0], w[1], ALU.subtract))
                step(dve.tensor_tensor(x2, w[2], w[3], ALU.add))
                tell(qk_ready)
                dve.wait_ge(table_in, due(table_in, 16))
                for h in range(RT_HEADS):
                    ps, free = take_pp()
                    do(dve.tensor_tensor(RATT[:, h, :, :].rearrange("p j t -> p (j t)"), ps[:, 0:3 * P],
                                         table[:, h * 3 * P:(h + 1) * 3 * P], ALU.mult))
                    dve.nop().then_inc(free, 1)
                    dve.nop().then_inc(att_ready, 1)
                state["p"] += 4
                dve.wait_ge(o_ready, due(o_ready))
                inverse_root(8, PANEL)
                for h in range(RT_HEADS):
                    for t in range(TILES):
                        n = 2 * h + t
                        step(dve.scalar_tensor_tensor(RO[:, h, t, :], RO[:, h, t, :], stat[:, 2, n:n + 1],
                                                      big[:, 8 + h, t * PANEL:(t + 1) * PANEL], ALU.mult, ALU.mult))
                    tell(y_ready)
                for h in range(RT_HEADS):
                    for t in range(TILES):
                        gained(RYT[:, 4 * h:4 * h + 4, t * P:(t + 1) * P], 48 + 4 * h)
                residual()

            def top16(src, n, out_v, out_i):
                for half in range(2):
                    lo = slice(8 * half, 8 * half + 8)
                    for c in range(n):
                        step(dve.max(out_v[:, c, lo], src[:, c, :]))
                    settle()
                    for c in range(n):
                        step(dve.max_index(out_i[:, c, lo], out_v[:, c, lo], src[:, c, :]))
                    settle()
                    if half == 0:
                        for c in range(n):
                            step(dve.match_replace(src[:, c, :], out_v[:, c, lo], src[:, c, :], NEG))
                        settle()

            def route(t):
                dve.wait_ge(s_ready, due(s_ready))
                top16(SC, 2 * HEADS, val, nidx)
                tell(s_free)
                fi = small(0, 256)
                do(dve.tensor_copy(fi, nidx[:, :, :].rearrange("p c k -> p (c k)")))
                v = val[:, :, :].rearrange("p (h c) k -> p h c k", c=2)
                a = v[:, :, 0, :].unsqueeze(3).to_broadcast([P, HEADS, TOPK, TOPK])
                b = v[:, :, 1, :].unsqueeze(2).to_broadcast([P, HEADS, TOPK, TOPK])
                do(dve.tensor_tensor(CAND, a, b, ALU.add))
                top_v = small(256, 128).rearrange("p (h k) -> p h k", h=HEADS)
                pos = small(384, 128).bitcast(U32)
                top16(CAND.rearrange("p h a b -> p h (a b)"), HEADS, top_v,
                      pos.rearrange("p (h k) -> p h k", h=HEADS))
                do(dve.tensor_tensor(gate[:, t, :].rearrange("p (h k) -> p h k", h=HEADS), top_v,
                                     top_v[:, :, 0:1].to_broadcast([P, HEADS, TOPK]), ALU.subtract))
                dve.nop().then_inc(shift_ready, 1)
                ab = small(512, 256).bitcast(U32)
                step(dve.tensor_scalar(ab[:, 0:128], pos, 4, None, ALU.logical_shift_right))
                do(dve.tensor_scalar(ab[:, 128:256], pos, 15, None, ALU.bitwise_and))
                abf = small(768, 256)
                do(dve.tensor_copy(abf, ab))
                io = iota[:, :].unsqueeze(1).unsqueeze(1).to_broadcast([P, HEADS, TOPK, TOPK])
                f4 = fi.rearrange("p (h c k) -> p h c k", h=HEADS, c=2)
                got = small(1024, 256)
                for c in range(2):
                    n = abf[:, 128 * c:128 * c + 128].rearrange("p (h k) -> p h k", h=HEADS)
                    one = ONE.rearrange("p h k i -> p (h k) i")
                    do(dve.tensor_tensor(one, n.rearrange("p h k -> p (h k)").unsqueeze(2).to_broadcast([P, SLOTS, TOPK]),
                                         iota[:, :].unsqueeze(1).to_broadcast([P, SLOTS, TOPK]), ALU.is_equal))
                    do(dve.tensor_tensor(ONE, ONE, f4[:, :, c, :].unsqueeze(2).to_broadcast([P, HEADS, TOPK, TOPK]),
                                         ALU.mult))
                    do(dve.tensor_reduce(got[:, 128 * c:128 * c + 128], one, AX.X, ALU.add))
                do(dve.scalar_tensor_tensor(idx[:, t, :], got[:, 0:128], float(NKEYS), got[:, 128:256],
                                            ALU.mult, ALU.add))
                dve.nop().then_inc(idx_ready, 1)

            def dots(l, t):
                base = (l * TILES + t) * SLOTS
                turns = (l * TILES + t) * 2 * SLOTS // RING
                copies = mine.n
                with dve.Fori(0, SLOTS // RING) as i:
                    dve.wait_ge(dve_done, i + copies)
                    for r in range(RING):
                        dve.wait_ge(land[r], i * 16 + (turns + 1) * 16)
                        dve.tensor_tensor_reduce(big[:, r, :], big[:, r, :], hn[:, t, :], 1.0, 0.0, ALU.mult,
                                                 ALU.add, dot16[:, r:r + 1]).then_inc(u_used, 1)
                    dve.wait_ge(u_used, i * RING + base + RING)
                    dve.wait_ge(idx_ready, l * TILES + t + 1)
                    dve.tensor_copy(act_v[:, t, bass.ds(i * RING, RING)], dot16[:, :]).then_inc(dve_done, 1)
                mine.n += SLOTS // RING
                tell(dots_ready)

            def weigh(t):
                dve.wait_ge(gate_exp, due(gate_exp))
                g3 = gate[:, t, :].rearrange("p (h k) -> p h k", h=HEADS)
                do(dve.tensor_reduce(stat[:, 0, 0:8], g3, AX.X, ALU.add))
                do(dve.reciprocal(stat[:, 1, 0:8], stat[:, 0, 0:8]))
                do(dve.tensor_tensor(g3, g3, stat[:, 1, 0:8].unsqueeze(2).to_broadcast([P, HEADS, TOPK]), ALU.mult))
                dve.wait_ge(gelu_ready, due(gelu_ready))
                do(dve.tensor_tensor(act_v[:, t, :], act_v[:, t, :], gate[:, t, :], ALU.mult))
                dve.nop().then_inc(w_ready, 1)

            def peer(l):
                state["p"] += 4 + 4
                state["k"] += 4
                route(0)
                dots(l, 0)
                weigh(0)
                route(1)
                dots(l, 1)
                weigh(1)
                for t in range(TILES):
                    ps, free = take_pp()
                    do(dve.tensor_copy(x[:, t, :], ps))
                    dve.nop().then_inc(free, 1)
                    dve.nop().then_inc(x_ready, 1)

            for s in range(2):
                dve.nop().then_inc(pp_free[s], 1)
            dve.wait_ge(consts_in, 16 * 9)
            ang, w1, w2 = E[1][:, 0:320], E[1][:, 320:640], E[1][:, 640:960]
            wi = E[1][:, 960:1280].bitcast(I32)
            pf = E[2][:, 0:258]
            step(dve.memset(ones[:, :], 1.0))
            do(dve.tensor_copy(pf, E[0][:, 0:258].bitcast(I32)))
            step(dve.tensor_scalar(ang[:, 0:256], pf[:, 0:256], E[0][:, 258:259], None, ALU.mult))
            for t in range(TILES):
                step(dve.tensor_scalar(ang[:, 256 + 32 * t:288 + 32 * t], E[0][:, 260:292], pf[:, 256 + t:257 + t],
                                       None, ALU.mult))
            settle()
            do(dve.tensor_scalar(w1, ang, 1.0 / TWO_PI, None, ALU.mult))
            do(dve.tensor_copy(wi, w1))
            do(dve.tensor_copy(w1, wi))
            for part in (C1, C2, C3):
                do(dve.scalar_tensor_tensor(ang, w1, -part, ang, ALU.mult, ALU.add))
            for limit, compare, shift in ((math.pi, ALU.is_gt, -TWO_PI), (-math.pi, ALU.is_lt, TWO_PI)):
                do(dve.tensor_scalar(w2, ang, limit, shift, compare, ALU.mult))
                do(dve.tensor_tensor(ang, ang, w2, ALU.add))
            do(dve.tensor_scalar(sin_t[:, :], ang, PI_IN, -PI_IN, ALU.min, ALU.max))
            do(dve.scalar_tensor_tensor(w2, sin_t[:, :], -1.0, sin_t[:, :], ALU.mult, ALU.max))
            do(dve.tensor_scalar(cos_t[:, :], w2, -1.0, math.pi / 2, ALU.mult, ALU.add))
            dve.nop().then_inc(trig_arg, 1)
            tp, free = take_tp()
            do(dve.tensor_copy(feat[:, :], tp[:, 0:64]))
            dve.nop().then_inc(free, 1)
            f4 = feat[:, 0:32].rearrange("p (l h) -> p l h", l=DEPTH)
            m8 = stat[:, 3, 0:8]
            do(dve.tensor_reduce(m8, feat[:, 0:32].rearrange("p (l h) -> p h l", l=DEPTH), AX.X, ALU.max))
            do(dve.tensor_tensor(f4, f4, m8.unsqueeze(1).to_broadcast([P, DEPTH, HEADS]), ALU.subtract))
            dve.nop().then_inc(lb_arg, 1)
            dve.wait_ge(lb_exp, due(lb_exp))
            do(dve.tensor_reduce(m8, feat[:, 0:32].rearrange("p (l h) -> p h l", l=DEPTH), AX.X, ALU.add))
            do(dve.reciprocal(stat[:, 3, 8:16], m8))
            do(dve.tensor_tensor(f4, f4, stat[:, 3, 8:16].unsqueeze(1).to_broadcast([P, DEPTH, HEADS]), ALU.mult))
            run = stat[:, 3, 16:24]
            do(dve.tensor_copy(run, f4[:, 0, :]))
            for l in range(DEPTH):
                if l:
                    do(dve.tensor_tensor(run, run, f4[:, l, :], ALU.add))
                if l % 3 == 0:
                    do(dve.tensor_tensor(lb[:, l // 3, 0, :], run, f4[:, 0, :], ALU.subtract))
                    do(dve.tensor_scalar(lb[:, l // 3, 1, :], lb[:, l // 3, 0, :], -1.0, 1.0, ALU.mult, ALU.add))
            dve.wait_ge(trig_ready, due(trig_ready, 2))
            for l in range(DEPTH):
                norm()
                (hgrn, attention, retention)[l % 3](l)
                norm()
                peer(l)


def kernel(**inputs):
    import concourse.bacc as _bacc
    from concourse.bass_utils import run_bass_kernel_spmd as _run

    nc = _bacc.Bacc("TRN2", target_bir_lowering=False, num_devices=1)
    arrays, args = {}, {}
    for name, a in {**inputs, **shape_constants()}.items():
        a = np.ascontiguousarray(a)
        arrays[f"in_{name}"] = a
        args[name] = nc.dram_tensor(f"in_{name}", a.shape, mybir.dt.from_np(a.dtype), kind="ExternalInput").ap()
    out = nc.dram_tensor("out_0", (1, S, D), F32, kind="ExternalOutput").ap()
    trunk(nc, args, out)
    r = _run(nc, [arrays], core_ids=[0])
    return r.results[0]["out_0"]
```

```python
from contextlib import ExitStack
import math

import numpy as np
import concourse.bass as bass
from concourse import mybir

F32 = mybir.dt.float32
I32 = mybir.dt.int32
U32 = mybir.dt.uint32
ALU = mybir.AluOpType
ACT = mybir.ActivationFunctionType
AX = mybir.AxisListType

P = 128
D = 1024
S = 256
TILES = S // P
KT = D // P
PANEL = 512
DEPTH = 4
EPS = 1e-6
TINY = 1e-30
HEADS = 8
LEVELS = [64, 32, 16, 8, 4, 2, 1]
GROUPS = ((128, 1), (512, 4), (2048, 16))
NG = len(GROUPS)
AT_DIM = 64
RT_HEADS = 4
TOPK = 16
NKEYS = 128
SLOTS = HEADS * TOPK
RING = 16
PAIR = 2 * TOPK
PAIRS = SLOTS // PAIR
V_DVE = (3, 7, 11, 15)
V_PE = tuple(r for r in range(RING) if r not in V_DVE)
NEG = -3.0e38
LN_SHIFT = 60
TWO_PI = 2.0 * math.pi
C1 = 6.28125
C2 = float(np.float32(np.round((TWO_PI - C1) * 2.0 ** 21) / 2.0 ** 21))
C3 = TWO_PI - C1 - C2
PI_IN = float(np.nextafter(np.float32(math.pi), np.float32(0)))


def shape_constants():
    s = np.arange(P)[:, None]
    t = np.arange(P)[None, :]
    level = [((s // (2 * m) == t // (2 * m)) & (s % (2 * m) < m) & (t % (2 * m) >= m)) for m in LEVELS]
    masks = np.stack(level, 1).astype(np.int32).reshape(P, -1)
    at = []
    for tile in range(TILES):
        q = tile * P + np.arange(P)[:, None]
        for window, dilation in GROUPS:
            k = np.arange(P * (tile + 1))[None, :]
            ok = (q >= k) & ((q - k) % dilation == 0) & ((q - k) // dilation <= window // dilation)
            at.append(np.where(ok, 0.0, -1e30))
    at = np.concatenate(at, 1).astype(np.float32)
    lg = np.log1p(-np.exp2(-5.0 - np.arange(RT_HEADS)))
    scale = 256.0 ** -0.5
    near = [np.where(t >= s, np.exp(g * np.maximum(t - s, 0)), 0.0) * scale for g in lg]
    far = [np.exp(g * (t - s + P)) * scale for g in lg]
    decay = np.stack([np.stack([n, n, f], 1) for n, f in zip(near, far)], 1)
    decay = decay.astype(np.float32).reshape(P, -1)
    theta = np.float32(10000.0)
    inv_at = theta ** (-np.arange(32, dtype=np.float32) / np.float32(32))
    inv_rt = theta ** (-np.arange(128, dtype=np.float32) / np.float32(128))
    return {
        "c_ident": np.eye(P, dtype=np.float32),
        "c_levels": masks,
        "c_window": at,
        "c_decay": decay,
        "c_inv_at": np.tile(inv_at.astype(np.float32), (P, 1)),
        "c_inv_rt": inv_rt.astype(np.float32).reshape(P, 1),
        "c_iota": np.tile(np.arange(TOPK, dtype=np.float32), (P, 1)),
    }


class Due:

    def __init__(self):
        self.value = {}

    def __call__(self, sem, more=1):
        self.value[sem.name] = self.value.get(sem.name, 0) + more
        return self.value[sem.name]


class Mine:

    def __init__(self, sem):
        self.sem, self.n = sem, 0

    def step(self, instruction):
        instruction.then_inc(self.sem, 1)
        self.n += 1


def trunk(nc, A, out):
    ctx = ExitStack()
    with ctx:
        def sb(name, shape, dt=F32):
            return ctx.enter_context(nc.sbuf_tensor(name, shape, dt))

        def pb(name, shape):
            return ctx.enter_context(nc.psum_tensor(name, shape, F32))

        def sem(name):
            return ctx.enter_context(nc.semaphore(name))

        x = sb("x", [P, TILES, D])
        hn = sb("hn", [P, TILES, D])
        hT = sb("hT", [P, KT, S])
        gain = sb("gain", [P, D])
        big = sb("big", [P, 16, D])
        wring = sb("wring", [P, 2, KT * PANEL])
        scr = sb("scr", [P, 16384])
        table = sb("table", [P, 1536])
        ident = sb("ident", [P, P])
        iota = sb("iota", [P, TOPK])
        ones = sb("ones", [P, P])
        at_gain = sb("at_gain", [P, 6, AT_DIM])
        sin_t = sb("sin_t", [P, 320])
        cos_t = sb("cos_t", [P, 320])
        rows = sb("rows", [64, P])
        feat = sb("feat", [P, 64])
        lb = sb("lb", [P, 2, 2, HEADS])
        stat = sb("stat", [P, 4, 96])
        val = sb("val", [P, 4, TOPK])
        nidx = sb("nidx", [P, 4, TOPK], U32)
        idx = sb("idx", [P, TILES, SLOTS], U32)
        gate = sb("gate", [P, TILES, SLOTS])
        act_v = sb("act_v", [P, TILES, SLOTS])
        dot16 = sb("dot16", [P, RING])
        idx16 = sb("idx16", [P, 2, RING], U32)

        PP = pb("PP", [P, 2, 1024])
        TP = pb("TP", [P, 2, 512])
        MI = pb("MI", [P, 2, 512])

        def cut(a, n):
            return scr[:, a:a + n]

        def small(a, n):
            return scr[:, 4096 + a:4096 + a + n]

        consts_in = sem("consts_in")
        x_in = sem("x_in")
        atgain_in = sem("atgain_in")
        gain_in = sem("gain_in")
        table_in = sem("table_in")
        keys_in = sem("keys_in")
        w_in = [sem(f"w_in{s}") for s in range(2)]
        pp_full = sem("pp_full")
        pp_free = [sem(f"pp_free{s}") for s in range(2)]
        tp_full = sem("tp_full")
        tp_free = [sem(f"tp_free{s}") for s in range(2)]
        x_ready = sem("x_ready")
        act_done = sem("act_done")
        dve_done = sem("dve_done")
        sq_ready = sem("sq_ready")
        ms_ready = sem("ms_ready")
        root_ready = sem("root_ready")
        hn_ready = sem("hn_ready")
        trig_arg = sem("trig_arg")
        trig_ready = sem("trig_ready")
        lb_ready = sem("lb_ready")
        lb_arg = sem("lb_arg")
        lb_exp = sem("lb_exp")
        sig_ready = sem("sig_ready")
        forget_ready = sem("forget_ready")
        log_ready = sem("log_ready")
        key_ready = sem("key_ready")
        sums_ready = sem("sums_ready")
        diff_ready = sem("diff_ready")
        exp_ready = sem("exp_ready")
        pair_ready = sem("pair_ready")
        level_taken = sem("level_taken")
        att_ready = sem("att_ready")
        o_ready = sem("o_ready")
        y_ready = sem("y_ready")
        qk_ready = sem("qk_ready")
        sc_ready = sem("sc_ready")
        prob_ready = sem("prob_ready")
        pv_done = sem("pv_done")
        idx_ready = sem("idx_ready")
        staged = sem("staged")
        turn_taken = sem("turn_taken")
        land = [sem(f"land{s}") for s in range(RING)]
        u_used = sem("u_used")
        vp_used = sem("vp_used")
        vd_used = sem("vd_used")
        dots_ready = sem("dots_ready")
        shift_ready = sem("shift_ready")
        gate_exp = sem("gate_exp")
        gelu_ready = sem("gelu_ready")
        w_ready = sem("w_ready")
        diag_ready = sem("diag_ready")
        out_done = sem("out_done")

        def weights(l):
            kind, i = l % 3, l // 3
            if kind == 0:
                return A["hg_w_in"][i], A["hg_w_out"][i], 1, KT
            if kind == 1:
                return A["at_w_in"][i], A["at_w_out"][i], 1, 4
            return A["rt_w_in"][i], A["rt_w_out"][i], 2, KT

        big_f = big[:, :, :].rearrange("p a b -> p (a b)")
        Q3 = big_f[:, 0:2048]
        E = [cut(2048 * i, 2048) for i in range(3)]
        ATT = cut(6144, 2048)
        B = cut(8192, 2048)
        ATTX = cut(10240, 1024)
        O = cut(11264, 2048)
        YT = cut(13312, 2048).rearrange("p (k s) -> p k s", k=KT)
        lvl = table[:, 0:len(LEVELS) * P].bitcast(I32).rearrange("p (l t) -> p l t", l=len(LEVELS))

        QKT = cut(0, 6144).rearrange("p (n b s) -> p n b s", n=6, b=4)
        TMP = cut(6144, 6144)
        SQ = cut(10240, 2048).rearrange("p (a b) -> p a b", a=2)
        PB = cut(6144, 1536).rearrange("p (a b) -> p a b", a=2)
        PT = cut(7680, 1536).rearrange("p (a b) -> p a b", a=2)
        AO = cut(9216, 1024).rearrange("p (t c) -> p t c", t=2)
        AYT = cut(12288, 1024).rearrange("p (k s) -> p k s", k=4)

        RTMP = [cut(2048 * i, 2048) for i in range(4)]
        RO = cut(0, 4096).rearrange("p (h t c) -> p h t c", h=4, t=2)
        RYT = cut(4096, 4096).rearrange("p (k s) -> p k s", k=16)
        RATT = cut(8192, 1536).rearrange("p (h j t) -> p h j t", h=4, j=3)
        RJ = cut(10240, 4096).rearrange("p (n c) -> p n c", n=8)

        PQ = cut(0, 4096).rearrange("p (c s) -> p c s", c=16)
        ACC = [cut(1024 * t, 1024) for t in range(TILES)]
        KEYS = cut(4096, 2048).rearrange("p (c d) -> p c d", c=16)
        KEYST = cut(6144, 2048).rearrange("p (c n) -> p c n", c=16)
        SC = cut(8192, 4096).rearrange("p (t c n) -> p t c n", t=TILES, c=16)
        ONE = cut(12288, 512).rearrange("p (h k i) -> p h k i", h=2, k=TOPK)
        CAND = cut(12800, 512).rearrange("p (h a b) -> p h a b", h=2, a=TOPK)
        DIAG = cut(13312, 2048).rearrange("p (r n) -> p r n", r=RING)

        block = ctx.enter_context(nc.Block())

        @block.sync
        def _(sp):
            sp.dma_start(x[:, :, :], A["x"][0].rearrange("(t p) d -> p t d", p=P)).then_inc(x_in, 16)
            g = p = 0
            free_at = [0, 0]

            def panels(source, n, halves=1, kt=KT, first=0):
                nonlocal g, p
                view = source.rearrange("(h k p) (n c) -> n h p k c", p=P, k=kt, c=PANEL)
                flat = source.rearrange("(k p) n -> p k n", p=P)

                def load(src, slot, count):
                    sp.wait_ge(pp_full, count)
                    dst = wring[:, slot, 0:kt * PANEL].rearrange("p (k c) -> p k c", k=kt)
                    sp.dma_start(dst, src).then_inc(w_in[slot], 16)

                pairs = n // 2 if halves == 1 and n >= 4 else 0
                for j in range(2 if pairs else n * halves):
                    slot = (g + j) % 2
                    load(view[first + j // halves, j % halves], slot, free_at[slot])
                    free_at[slot] = p + j // halves + 1
                if pairs:
                    with sp.Fori(0, pairs - 1) as i:
                        for u in range(2):
                            load(flat[:, :, bass.ds((i * 2 + (first + 2 + u)) * PANEL, PANEL)], (g + u) % 2, i * 2 + (p + u + 1))
                    for j in range(n - 2, n):
                        free_at[(g + j) % 2] = p + j + 1
                    if n % 2:
                        slot = (g + n - 1) % 2
                        load(view[first + n - 1, 0], slot, p + n - 2)
                g += n * halves
                p += n

            for l in range(DEPTH):
                w, wo, halves, kt = weights(l)
                plan = {0: ((6, 6), (1, 6), (1, 7)), 1: ((9, 16),), 2: ((8, 4), (2, 2), (2, 2))}[l % 3]
                first = 0
                for n, own in plan:
                    panels(w, n, first=first)
                    first += n
                    p += own
                panels(wo, 2, halves, kt)
                panels(A["pk_w_q"][l], 4)
                p += TILES
            sp.wait_ge(x_ready, 4 * DEPTH)
            sp.dma_start(out[0].rearrange("(t p) d -> p t d", p=P), x[:, :, :]).then_inc(out_done, 16)
            sp.wait_ge(out_done, 16)

        @block.gpsimd
        def _(pool):
            due = Due()
            pool.dma_start(ident[:, :], A["c_ident"]).then_inc(consts_in, 16)
            pool.dma_start(iota[:, :], A["c_iota"]).then_inc(consts_in, 16)
            pool.dma_start(rows[0:32, :], A["hg_lb"].rearrange("l (h p) -> (l h) p", p=P)).then_inc(consts_in, 16)
            pool.dma_start(rows[32:48, :], A["hg_onorm"].rearrange("l (h p) -> (l h) p", p=P)).then_inc(consts_in, 16)
            pool.dma_start(rows[48:64, :], A["rt_onorm"].rearrange("l (h p) -> (l h) p", p=P)).then_inc(consts_in, 16)
            pool.dma_start(E[0][:, 0:256].bitcast(I32), A["positions"].to_broadcast([P, S])).then_inc(consts_in, 16)
            pool.dma_start(E[0][:, 256:258].bitcast(I32), A["positions"].rearrange("a (t p) -> p (a t)", p=P),
                           allow_slow_non_contiguous=True).then_inc(consts_in, 16)
            pool.dma_start(E[0][:, 258:259], A["c_inv_rt"]).then_inc(consts_in, 16)
            pool.dma_start(E[0][:, 260:292], A["c_inv_at"]).then_inc(consts_in, 16)

            for n, name in enumerate(("at_qnorm", "at_knorm")):
                pool.dma_start(at_gain[:, 3 * n:3 * n + 3, :],
                               A[name][0].unsqueeze(0).to_broadcast([P, NG, AT_DIM])).then_inc(atgain_in, 16)

            def gather_group(src, t, half, column, ready, used):
                pool.wait_ge(idx_ready, ready)
                pool.sem_inc(turn_taken, 1)
                pool.tensor_copy(idx16[:, half, :], idx[:, t, bass.ds(column, RING)]).then_inc(staged, 1)
                for r in range(RING):
                    if used is not None:
                        pool.wait_ge(*used(r))
                    pool.wait_ge(staged, steps[0])
                    pool.sem_inc(turn_taken, 1)
                    pool.indirect_dma_start(
                        big[:, r, :], None, src,
                        bass.IndirectOffsetOnAxis(ap=idx16[:, half, r:r + 1], axis=0),
                        element_offset=l * NKEYS * NKEYS * D).then_inc(land[r], 16)

            def u_through(n):
                return lambda r: (u_used, n * RING + (r + 1))

            def v_through(turn, i):
                def count(r):
                    if r in V_DVE:
                        return vd_used, i * len(V_DVE) + (turn * (1 + PAIRS * 2 * len(V_DVE)) + V_DVE.index(r) + 2)
                    return vp_used, i * len(V_PE) + (turn * 2 * PAIRS * len(V_PE) + V_PE.index(r) + 1)
                return count

            def table_load(l):
                kind = l % 3
                cols = (len(LEVELS) * P, 3 * P * 3, 1536)[kind]
                dst = table[:, 0:cols].bitcast(I32) if kind == 0 else table[:, 0:cols]
                pool.dma_start(dst, A[("c_levels", "c_window", "c_decay")[kind]]).then_inc(table_in, 16)
                pool.dma_start(gain[:, :], A["mix_norm"][l:l + 1].to_broadcast([P, D])).then_inc(gain_in, 16)

            def differences(l):
                pool.wait_ge(lb_ready, 1)
                pool.wait_ge(sig_ready, due(sig_ready, 2) - 1)
                kk, neg = big_f[:, 8 * D:10 * D], big_f[:, 10 * D:12 * D]
                pool.tensor_tensor(kk.rearrange("p (h s) -> p h s", h=HEADS), neg.rearrange("p (h s) -> p h s", h=HEADS),
                                   lb[:, l // 3, 1, :].unsqueeze(2).to_broadcast([P, HEADS, S]),
                                   ALU.mult).then_inc(key_ready, 1)
                pool.wait_ge(sums_ready, due(sums_ready))
                for n, m in enumerate(LEVELS + [P]):
                    b = B.rearrange("p (n two m) -> p n two m", two=2, m=m)
                    e = E[n % 3].rearrange("p (n two m) -> p n two m", two=2, m=m)
                    mid = b[:, :, 0, m - 1:m].to_broadcast([P, 2048 // (2 * m), m])
                    if n >= 3:
                        pool.wait_ge(level_taken, due(level_taken))
                    pool.tensor_tensor(e[:, :, 0, :], mid, b[:, :, 0, :], ALU.subtract).then_inc(diff_ready, 1)
                    if m < P:
                        pool.tensor_tensor(e[:, :, 1, :], b[:, :, 1, :], mid, ALU.subtract).then_inc(diff_ready, 1)
                    else:
                        pool.tensor_copy(e[:, :, 1, :], b[:, :, 1, :]).then_inc(diff_ready, 1)
                due(level_taken, 3)

            steps = [0]
            table_load(0)
            for l in range(DEPTH):
                if l % 3 == 0:
                    differences(l)
                pool.wait_ge(hn_ready, due(hn_ready, TILES))
                pool.dma_start(gain[:, :], A["ffn_norm"][l:l + 1].to_broadcast([P, D])).then_inc(gain_in, 16)
                pool.wait_ge(x_ready, 4 * l + 2)
                pool.dma_start(KEYS, A["pk_keys"][l].rearrange("h c n d -> n (h c) d")).then_inc(keys_in, 16)
                pool.wait_ge(hn_ready, due(hn_ready, TILES))
                if l + 1 < DEPTH:
                    table_load(l + 1)
                groups = SLOTS // RING
                for t in range(TILES):
                    turn = l * TILES + t
                    for phase in range(2):
                        src = (A["pk_u"], A["pk_v"])[phase].rearrange("l e d -> (l e) d")

                        def through(i):
                            return v_through(turn, i) if phase else u_through(i + turn * groups)

                        if phase:
                            before = u_through(turn * groups + groups - 1)
                        else:
                            before = v_through(turn - 1, groups - 1) if turn else None
                        routed = turn * PAIRS + (PAIRS if phase else 1)
                        now = steps[0]
                        steps[0] = now + 1
                        gather_group(src, t, 0, 0, routed, before)
                        with pool.Fori(0, groups // 2 - 1) as i:
                            for k in range(2):
                                steps[0] = i * 2 + (now + 2 + k)
                                gather_group(src, t, 1 - k, i * (2 * RING) + RING * (1 + k),
                                             routed if phase else i + (routed + k), through(i * 2 + k))
                        steps[0] = now + groups
                        gather_group(src, t, 1, SLOTS - RING, turn * PAIRS + PAIRS, through(groups - 2))

        @block.tensor
        def _(pe):
            due = Due()
            state = {"g": 0, "p": 0, "k": 0}

            def wait_pp():
                p = state["p"]
                pe.wait_ge(pp_free[p % 2], p // 2 + 1)
                state["p"] = p + 1
                return PP[:, p % 2, :]

            def turn(blocks, offset=0):
                k = state["k"]
                pe.wait_ge(tp_free[k % 2], k // 2)
                for j, b in enumerate(blocks):
                    last = pe.transpose(TP[0:b.shape[-1], k % 2, j * P:j * P + b.shape[0]], b,
                                        ident[0:b.shape[0], 0:b.shape[0]])
                last.then_inc(tp_full, 1)
                state["k"] = k + 1

            def project(n, feature_major, src, kt=KT, halves=1):
                g, p = state["g"], state["p"]

                def panel(slot, w_turn, ps, p_turn, half):
                    pe.wait_ge(w_in[slot], w_turn * 16 + 16)
                    if half == 0:
                        pe.wait_ge(pp_free[ps], p_turn + 1)
                    w = wring[:, slot, 0:kt * PANEL].rearrange("p (k c) -> p k c", k=kt)
                    for o in range(4 if feature_major else TILES):
                        for k in range(kt):
                            flags = dict(start=(half == 0 and k == 0), stop=(half == halves - 1 and k == kt - 1))
                            if feature_major:
                                last = pe.matmul(PP[:, ps, o * S:(o + 1) * S], w[:, k, o * P:(o + 1) * P],
                                                 src[:, k, :], **flags)
                            else:
                                last = pe.matmul(PP[:, ps, o * PANEL:(o + 1) * PANEL],
                                                 src[:, half * kt + k, o * P:(o + 1) * P], w[:, k, :], **flags)
                    if half == halves - 1:
                        last.then_inc(pp_full, 1)

                pairs = n // 2 if halves == 1 and n >= 4 else 0
                if pairs:
                    with pe.Fori(0, pairs) as i:
                        for u in range(2):
                            panel((g + u) % 2, i + (g + u) // 2, (p + u) % 2, i + (p + u) // 2, 0)
                for j in range(2 * pairs, n):
                    for half in range(halves):
                        m = g + j * halves + half
                        panel(m % 2, m // 2, (p + j) % 2, (p + j) // 2, half)
                state["g"], state["p"] = g + n * halves, p + n

            def left_pp(back=1):
                p = state["p"] - back
                pe.wait_ge(pp_free[p % 2], p // 2 + 2)

            def left_tp(back=1):
                k = state["k"] - back
                pe.wait_ge(tp_free[k % 2], k // 2 + 1)

            def norm_turn(t):
                pe.wait_ge(hn_ready, due(hn_ready))
                for half in range(2):
                    turn([hn[:, t, (4 * half + j) * P:(4 * half + j + 1) * P] for j in range(4)])

            def hgrn(l):
                kk = big_f[:, 8 * D:10 * D]

                def level(n):
                    pe.wait_ge(pair_ready, due(pair_ready))
                    for f in range(2):
                        ps = wait_pp()
                        for j in range(8):
                            c = (8 * f + j) * P
                            last = pe.matmul(ps[:, j * P:(j + 1) * P], E[n % 3][:, c:c + P], E[n % 3][:, c:c + P],
                                             start=True, stop=True)
                        last.then_inc(pp_full, 1)

                project(4, True, hT)
                project(2, False, hT)
                pe.wait_ge(key_ready, due(key_ready))
                for f in range(2):
                    ps = wait_pp()
                    for j in range(8):
                        c = (8 * f + j) * P
                        last = pe.matmul(ps[:, j * P:(j + 1) * P], kk[:, c:c + P], Q3[:, c:c + P],
                                         start=True, stop=True)
                    last.then_inc(pp_full, 1)
                level(0)
                level(1)
                project(1, False, hT)
                for n in range(2, 5):
                    level(n)
                project(1, False, hT)
                for n in range(5, len(LEVELS)):
                    level(n)
                n = len(LEVELS)
                pe.wait_ge(pair_ready, due(pair_ready))
                ps = wait_pp()
                for h in range(HEADS):
                    c = h * S
                    last = pe.matmul(ps[:, h * P:(h + 1) * P], E[n % 3][:, c:c + P], E[n % 3][:, c + P:c + S],
                                     start=True, stop=True)
                last.then_inc(pp_full, 1)
                pe.wait_ge(att_ready, due(att_ready))
                for c in range(2):
                    ps = wait_pp()
                    for t in range(TILES):
                        for j in range(4):
                            h = 4 * c + j
                            o = ps[:, t * PANEL + j * P:t * PANEL + (j + 1) * P]
                            v = [big[:, 4 + c, s * PANEL + j * P:s * PANEL + (j + 1) * P] for s in range(2)]
                            a = ATT[:, (2 * h + t) * P:(2 * h + t + 1) * P]
                            last = pe.matmul(o, a, v[t], start=True, stop=(t == 0))
                            if t:
                                last = pe.matmul(o, ATTX[:, h * P:(h + 1) * P], v[0], start=False, stop=True)
                    last.then_inc(pp_full, 1)
                for c in range(2):
                    pe.wait_ge(y_ready, due(y_ready))
                    for t in range(TILES):
                        b = c * 1024 + t * PANEL
                        turn([O[:, b + j * P:b + (j + 1) * P] for j in range(4)])
                left_tp(1)
                left_tp(2)
                project(2, False, YT)

            def attention(l):
                def turn_qk(n):
                    pe.wait_ge(qk_ready, due(qk_ready))
                    for t in range(TILES):
                        turn([big[:, n, t * PANEL + j * P:t * PANEL + (j + 1) * P] for j in range(4)])

                for n in range(9):
                    project(1, False, hT)
                    if 2 <= n < 8:
                        turn_qk(n - 2)
                left_tp(1)
                left_tp(2)

                def scores(it):
                    t, h = it // HEADS, it % HEADS
                    a = (h % 2) * AT_DIM
                    ps = wait_pp()
                    for g in range(NG):
                        last = pe.matmul(ps[:, g * S:g * S + P * (t + 1)],
                                         QKT[a:a + AT_DIM, g, h // 2, t * P:(t + 1) * P],
                                         QKT[a:a + AT_DIM, 3 + g, h // 2, 0:P * (t + 1)], start=True, stop=True)
                    last.then_inc(pp_full, 1)

                def turn_probs(it):
                    pe.wait_ge(prob_ready, due(prob_ready))
                    for half in range(it // HEADS + 1):
                        turn([PB[:, it % 2, (3 * half + j) * P:(3 * half + j + 1) * P] for j in range(3)])

                def values(it, behind):
                    t, h = it // HEADS, it % HEADS
                    for half in range(t + 1):
                        left_tp(behind + half + 1)
                    for b in range(3 * (t + 1)):
                        g, s = b // (t + 1), b % (t + 1)
                        last = pe.matmul(MI[:, t, h * AT_DIM:(h + 1) * AT_DIM], PT[:, it % 2, b * P:(b + 1) * P],
                                         big[:, 6 + g, s * PANEL + h * AT_DIM:s * PANEL + (h + 1) * AT_DIM],
                                         start=(b == 0), stop=(b == 3 * (t + 1) - 1))
                    last.then_inc(pv_done, 1)

                last_it = 2 * HEADS - 1
                scores(0)
                scores(1)
                turn_probs(0)
                for it in range(2 * HEADS):
                    if it + 2 <= last_it:
                        scores(it + 2)
                    if it < last_it:
                        turn_probs(it + 1)
                    values(it, (it + 1) // HEADS + 1 if it < last_it else 0)
                pe.wait_ge(y_ready, due(y_ready))
                for t in range(TILES):
                    turn([AO[:, t, j * P:(j + 1) * P] for j in range(4)])
                left_tp(1)
                left_tp(2)
                project(2, False, AYT, kt=4)

            def retention(l):
                project(4, True, hT)
                project(4, False, hT)
                pe.wait_ge(qk_ready, due(qk_ready))
                for h in range(RT_HEADS):
                    ps = wait_pp()
                    for j, (s, t) in enumerate(((0, 0), (1, 1), (0, 1))):
                        for b in range(2):
                            q = big_f[:, (2 * h + b) * S + t * P:(2 * h + b) * S + (t + 1) * P]
                            k = big_f[:, (8 + 2 * h + b) * S + s * P:(8 + 2 * h + b) * S + (s + 1) * P]
                            last = pe.matmul(ps[:, j * P:(j + 1) * P], k, q, start=(b == 0), stop=(b == 1))
                    last.then_inc(pp_full, 1)
                for pair in range(2):
                    project(2, False, hT)
                    for h in range(2 * pair, 2 * pair + 2):
                        pe.wait_ge(att_ready, due(att_ready))
                        ps = wait_pp()
                        v = [big[:, 4 + h, s * PANEL:(s + 1) * PANEL] for s in range(2)]
                        pe.matmul(ps[:, 0:PANEL], RATT[:, h, 0, :], v[0], start=True, stop=True)
                        pe.matmul(ps[:, PANEL:], RATT[:, h, 1, :], v[1], start=True, stop=False)
                        pe.matmul(ps[:, PANEL:], RATT[:, h, 2, :], v[0], start=False, stop=True).then_inc(pp_full, 1)
                for h in range(RT_HEADS):
                    pe.wait_ge(y_ready, due(y_ready))
                    for t in range(TILES):
                        turn([RO[:, h, t, j * P:(j + 1) * P] for j in range(4)])
                left_tp(1)
                left_tp(2)
                project(2, False, RYT, halves=2)

            def peer(l):
                pe.wait_ge(keys_in, due(keys_in, 16))
                for c in range(4):
                    turn([KEYS[:, 4 * c + j, :] for j in range(4)])

                def scores(t, pair):
                    k = state["k"]
                    pe.wait_ge(tp_free[k % 2], k // 2)
                    state["k"] = k + 1
                    for j in range(4):
                        c = 4 * pair + j
                        last = pe.matmul(TP[:, k % 2, j * P:(j + 1) * P], PQ[:, c, t * P:(t + 1) * P], KEYST[:, c, :],
                                         start=True, stop=True)
                    last.then_inc(tp_full, 1)

                for pair in range(PAIRS):
                    project(1, True, hT)
                    left_pp()
                    scores(0, pair)
                for pair in range(PAIRS):
                    scores(1, pair)
                for t in range(TILES):
                    ps = wait_pp()
                    for c in range(2):
                        pe.matmul(ps[:, c * PANEL:(c + 1) * PANEL], ident[:, :], x[:, t, c * PANEL:(c + 1) * PANEL],
                                  start=True, stop=False, skip_group_check=True)
                    groups = SLOTS // RING
                    base = (l * TILES + t) * groups * len(V_PE)
                    turns = (l * TILES + t) * 2 * groups + groups

                    def group(i, end):
                        for n, r in enumerate(V_PE):
                            pe.wait_ge(land[r], i * 16 + (turns + 1) * 16)
                            pe.wait_ge(diag_ready, i * len(V_PE) + (base + n + 1))
                            for c in range(2):
                                last = pe.matmul(ps[:, c * PANEL:(c + 1) * PANEL], DIAG[:, r, :],
                                                 big[:, r, c * PANEL:(c + 1) * PANEL], start=False,
                                                 stop=(end and n == len(V_PE) - 1), skip_group_check=True)
                            last.then_inc(vp_used, 1)

                    with pe.Fori(0, groups - 1) as i:
                        group(i, False)
                    group(groups - 1, True)
                    pe.wait_ge(vp_used, base + groups * len(V_PE))
                    pe.nop().then_inc(pp_full, 1)
                    if l + 1 < DEPTH:
                        norm_turn(t)

            pe.wait_ge(consts_in, 16 * 9)
            turn([rows[:, :]])
            pe.wait_ge(x_in, 16)
            for t in range(TILES):
                norm_turn(t)
            for l in range(DEPTH):
                left_tp(1)
                left_tp(2)
                (hgrn, attention, retention)[l % 3](l)
                for t in range(TILES):
                    norm_turn(t)
                left_tp(1)
                left_tp(2)
                peer(l)

        @block.scalar
        def _(act):
            due = Due()
            mine = Mine(act_done)
            state = {"p": 0, "k": 0}

            def settle():
                act.wait_ge(act_done, mine.n)

            def take_pp():
                p = state["p"]
                act.wait_ge(pp_full, p + 1)
                state["p"] = p + 1
                return PP[:, p % 2, :], pp_free[p % 2]

            def take_tp():
                k = state["k"]
                act.wait_ge(tp_full, k + 1)
                state["k"] = k + 1
                return TP[:, k % 2, :], tp_free[k % 2]

            def to_features(dst, blocks=4):
                tp, free = take_tp()
                act.activation(dst, tp[:, 0:blocks * P].rearrange("p (b c) -> p b c", b=blocks),
                               ACT.Copy).then_inc(free, 1)

            def left_pp(back=1):
                p = state["p"] - back
                act.wait_ge(pp_free[p % 2], p // 2 + 2)

            def norm(t, first=False, more=1):
                if first:
                    act.wait_ge(x_in, 16)
                elif more:
                    act.wait_ge(x_ready, due(x_ready, more))
                act.activation(hn[:, t, :], x[:, t, :], ACT.Square, accum_out=stat[:, 0, t:t + 1]).then_inc(sq_ready, 1)
                root(t, 1)
                for half in range(2):
                    to_features(hT[:, 4 * half:4 * half + 4, t * P:(t + 1) * P])

            def move_panel(j, func=ACT.Copy):
                ps, free = take_pp()
                act.activation(big[:, j, :], ps, func).then_inc(free, 1)

            def root(first, n):
                act.wait_ge(ms_ready, due(ms_ready))
                act.activation(stat[:, 2, first:first + n], stat[:, 1, first:first + n], ACT.Sqrt).then_inc(root_ready, 1)

            def hgrn(l):
                for j in range(2):
                    move_panel(j, ACT.Silu)
                for j in range(2, 4):
                    move_panel(j)
                left_pp(1)
                left_pp(2)
                f = big_f[:, 2 * D:4 * D]
                act.activation(big_f[:, 10 * D:12 * D], f, ACT.Sigmoid, scale=-1.0).then_inc(sig_ready, 1)
                act.activation(big_f[:, 12 * D:14 * D], f, ACT.Sigmoid).then_inc(sig_ready, 1)
                move_panel(4)
                move_panel(5)
                act.wait_ge(forget_ready, due(forget_ready))
                act.activation(B, big_f[:, 12 * D:14 * D], ACT.Ln).then_inc(log_ready, 1)
                state["p"] += 2

                def decays(n):
                    act.wait_ge(diff_ready, due(diff_ready, 2))
                    act.activation(E[n % 3], E[n % 3], ACT.Exp).then_inc(exp_ready, 1)

                for n in range(3):
                    decays(n)
                state["p"] += 4
                move_panel(6)
                for n in range(3, 6):
                    decays(n)
                state["p"] += 6
                move_panel(7)
                for n in range(6, 8):
                    decays(n)
                left_pp(1)
                state["p"] += 5
                mine.step(act.activation(big[:, 6:8, :], big[:, 6:8, :], ACT.Silu))
                for c in range(2):
                    ps, free = take_pp()
                    act.activation(O[:, c * 1024:(c + 1) * 1024], ps, ACT.Copy).then_inc(free, 1)
                    left_pp()
                    act.activation(E[0][:, c * 1024:(c + 1) * 1024], O[:, c * 1024:(c + 1) * 1024],
                                   ACT.Square).then_inc(o_ready, 1)
                for c in range(2):
                    root(8 * c, 8)
                state["k"] += 4
                state["p"] += 2

            def attention(l):
                for n in range(9):
                    move_panel(n)
                    if n < 6:
                        left_pp()
                        if n >= 2:
                            act.wait_ge(qk_ready, due(qk_ready))
                        act.activation(SQ[:, n % 2, :], big[:, n, :], ACT.Square).then_inc(o_ready, 1)
                        root(16 * n, 16)
                    if 2 <= n < 8:
                        for t in range(TILES):
                            to_features(QKT[:, n - 2, :, t * P:(t + 1) * P])
                due(qk_ready, 2)
                for it in range(2 * HEADS):
                    t = it // HEADS
                    w = 3 * P * (t + 1)
                    state["p"] += 1
                    act.wait_ge(sc_ready, due(sc_ready))
                    act.activation(PB[:, it % 2, 0:w], PB[:, it % 2, 0:w], ACT.Exp, bias=stat[:, 0, it:it + 1],
                                   accum_out=stat[:, 1, it:it + 1]).then_inc(prob_ready, 1)
                    if it >= 2:
                        act.wait_ge(pv_done, due(pv_done))
                    for half in range(t + 1):
                        to_features(PT[:, it % 2, 3 * half * P:(3 * half + 3) * P].rearrange("p (b c) -> p b c", b=3), 3)
                due(pv_done, 2)
                for t in range(TILES):
                    to_features(AYT[:, :, t * P:(t + 1) * P])
                state["p"] += 2

            def retention(l):
                for j in range(8):
                    move_panel(j)
                state["p"] += 4
                for pair in range(2):
                    for h in range(2 * pair, 2 * pair + 2):
                        move_panel(8 + h, ACT.Silu)
                    for h in range(2 * pair, 2 * pair + 2):
                        ps, free = take_pp()
                        if h == 0:
                            act.wait_ge(qk_ready, due(qk_ready))
                        for t in range(TILES):
                            mine.step(act.activation(RJ[:, 2 * h + t, :], ps[:, t * PANEL:(t + 1) * PANEL],
                                                     ACT.Square, accum_out=stat[:, 0, 2 * h + t:2 * h + t + 1]))
                        act.activation(RO[:, h, :, :].rearrange("p t c -> p (t c)"), ps, ACT.Copy).then_inc(free, 1)
                        settle()
                        left_pp()
                        act.nop().then_inc(o_ready, 1)
                    root(4 * pair, 4)
                state["k"] += 8
                state["p"] += 2

            def peer(l):
                for c in range(4):
                    to_features(KEYST[:, 4 * c:4 * c + 4, :])
                for pair in range(PAIRS):
                    ps, free = take_pp()
                    act.activation(PQ[:, 4 * pair:4 * pair + 4, :].rearrange("p c s -> p (c s)"), ps,
                                   ACT.Copy).then_inc(free, 1)
                    to_features(SC[:, 0, 4 * pair:4 * pair + 4, :])
                for pair in range(PAIRS):
                    to_features(SC[:, 1, 4 * pair:4 * pair + 4, :])
                for t in range(TILES):
                    act.wait_ge(shift_ready, due(shift_ready, PAIRS))
                    act.activation(gate[:, t, :], gate[:, t, :], ACT.Exp).then_inc(gate_exp, 1)
                    act.wait_ge(dots_ready, due(dots_ready))
                    act.activation(act_v[:, t, :], act_v[:, t, :], ACT.Gelu).then_inc(gelu_ready, 1)
                    act.wait_ge(w_ready, due(w_ready))
                    base = (l * TILES + t) * SLOTS // RING * len(V_PE)

                    def group(i, before):
                        for n, r in enumerate(V_PE):
                            if before is not None:
                                act.wait_ge(vp_used, before + (n + 1))
                            act.wait_ge(w_ready, due(w_ready, 0))
                            act.activation(DIAG[:, r, :], ident[:, :], ACT.Copy,
                                           scale=act_v[:, t, bass.ds(i * RING + r, 1)]).then_inc(diag_ready, 1)

                    group(0, base - len(V_PE) if base else None)
                    with act.Fori(0, SLOTS // RING - 1) as i:
                        group(i + 1, i * len(V_PE) + base)
                    state["p"] += 1
                    if l + 1 < DEPTH:
                        norm(t)

            act.wait_ge(trig_arg, due(trig_arg))
            act.activation(sin_t[:, :], sin_t[:, :], ACT.Sin).then_inc(trig_ready, 1)
            act.activation(cos_t[:, :], cos_t[:, :], ACT.Sin).then_inc(trig_ready, 1)
            state["k"] += 1
            act.wait_ge(lb_arg, due(lb_arg))
            act.activation(feat[:, 0:32], feat[:, 0:32], ACT.Exp).then_inc(lb_exp, 1)
            for t in range(TILES):
                norm(t, first=True)
            for l in range(DEPTH):
                (hgrn, attention, retention)[l % 3](l)
                for t in range(TILES):
                    norm(t, more=2 if t == 0 else 0)
                peer(l)

        @block.vector
        def _(dve):
            due = Due()
            mine = Mine(dve_done)
            state = {"p": 0, "k": 0}
            step = mine.step

            def settle():
                dve.wait_ge(dve_done, mine.n)

            def take_pp():
                p = state["p"]
                dve.wait_ge(pp_full, p + 1)
                state["p"] = p + 1
                return PP[:, p % 2, :], pp_free[p % 2]

            def take_tp():
                k = state["k"]
                dve.wait_ge(tp_full, k + 1)
                state["k"] = k + 1
                return TP[:, k % 2, :], tp_free[k % 2]

            def do(instruction):
                step(instruction)
                settle()

            def tell(sem_):
                settle()
                dve.nop().then_inc(sem_, 1)

            def inverse_root(first, n, width):
                at = slice(first, first + n)
                dve.tensor_scalar(stat[:, 1, at], stat[:, 0, at], 1.0 / width, EPS, ALU.mult, ALU.add).then_inc(ms_ready, 1)
                dve.wait_ge(root_ready, due(root_ready))
                do(dve.reciprocal(stat[:, 2, at], stat[:, 2, at]))

            def norm(t):
                dve.wait_ge(sq_ready, due(sq_ready))
                inverse_root(t, 1, D)
                if t == 0:
                    dve.wait_ge(gain_in, due(gain_in, 16))
                dve.scalar_tensor_tensor(hn[:, t, :], x[:, t, :], stat[:, 2, t:t + 1], gain[:, :],
                                         ALU.mult, ALU.mult).then_inc(hn_ready, 1)
                dve.wait_ge(hn_ready, due(hn_ready))
                state["k"] += 2

            def left_pp(back=1):
                p = state["p"] - back
                dve.wait_ge(pp_free[p % 2], p // 2 + 2)

            def residual():
                for c in range(2):
                    ps, free = take_pp()
                    xs = x[:, :, c * PANEL:(c + 1) * PANEL]
                    do(dve.tensor_tensor(xs, ps.rearrange("p (t n) -> p t n", t=TILES), xs, ALU.add))
                    dve.nop().then_inc(free, 1)
                    dve.nop().then_inc(x_ready, 1)

            def gained(dst, first, n=4):
                tp, free = take_tp()
                g = feat[:, first:first + n].unsqueeze(2).to_broadcast([P, n, P])
                dve.tensor_tensor(dst, tp.rearrange("p (b c) -> p b c", b=n), g, ALU.mult).then_inc(free, 1)

            def hgrn(l):
                n_l = l // 3
                state["p"] += 4
                lbb = lb[:, n_l, 0, :].unsqueeze(2).to_broadcast([P, HEADS, S])
                omb = lb[:, n_l, 1, :].unsqueeze(2).to_broadcast([P, HEADS, S])

                def by_head(a):
                    return a.rearrange("p (h s) -> p h s", h=HEADS)

                kk = big_f[:, 8 * D:10 * D]
                fg = big_f[:, 12 * D:14 * D]
                up = big_f[:, 14 * D:16 * D]
                tiny = E[2]
                dve.wait_ge(sig_ready, due(sig_ready, 2))
                do(dve.tensor_tensor(by_head(fg), by_head(fg), omb, ALU.mult))
                do(dve.tensor_tensor(by_head(fg), by_head(fg), lbb, ALU.add))
                do(dve.tensor_scalar(tiny, fg, 2.0 ** -40, None, ALU.is_lt))
                do(dve.tensor_scalar(up, tiny, 2.0 ** LN_SHIFT, 1.0, ALU.mult, ALU.add))
                dve.scalar_tensor_tensor(fg, fg, TINY, up, ALU.max, ALU.mult).then_inc(forget_ready, 1)
                dve.wait_ge(log_ready, due(log_ready))
                do(dve.scalar_tensor_tensor(fg, tiny, -LN_SHIFT * math.log(2.0), B, ALU.mult, ALU.add))
                for n in range(2 * HEADS):
                    seg = slice(n * P, (n + 1) * P)
                    step(dve.tensor_tensor_scan(B[:, seg], ones[:, :], fg[:, seg], 0.0, ALU.mult, ALU.add))
                tell(sums_ready)
                state["p"] += 2
                for f in range(2):
                    ps, free = take_pp()
                    a = ATT[:, f * 1024:(f + 1) * 1024].rearrange("p (n t) -> p n t", n=8)
                    idb = ident[:, :].unsqueeze(1).to_broadcast([P, 8, P])
                    dve.tensor_tensor(a, ps.rearrange("p (n t) -> p n t", n=8), idb, ALU.mult).then_inc(free, 1)
                dve.wait_ge(key_ready, due(key_ready))
                dve.wait_ge(table_in, due(table_in, 16))

                def products(n):
                    m = (LEVELS + [P])[n]
                    dve.wait_ge(exp_ready, due(exp_ready))

                    def half(a, which):
                        return a.rearrange("p (n two m) -> p n two m", two=2, m=m)[:, :, which, :]

                    e = E[n % 3]
                    step(dve.tensor_tensor(half(e, 0), half(e, 0), half(kk, 0), ALU.mult))
                    step(dve.tensor_tensor(half(e, 1), half(e, 1), half(Q3, 1), ALU.mult))
                    tell(pair_ready)

                def select(n):
                    if n == len(LEVELS):
                        ps, free = take_pp()
                        dve.tensor_copy(ATTX, ps).then_inc(free, 1)
                    else:
                        for f in range(2):
                            ps, free = take_pp()
                            left_pp(3)
                            a = ATT[:, f * 1024:(f + 1) * 1024].rearrange("p (n t) -> p n t", n=8)
                            mask = lvl[:, n, :].unsqueeze(1).to_broadcast([P, 8, P])
                            dve.copy_predicated(a, mask, ps.rearrange("p (n t) -> p n t", n=8)).then_inc(free, 1)
                            if n in (1, 4) and f == 1:
                                left_pp()
                                state["p"] += 1
                    if n not in (1, 4):
                        left_pp()
                    dve.nop().then_inc(level_taken, 1)

                total = len(LEVELS) + 1
                for n in range(total):
                    products(n)
                    if n:
                        select(n - 1)
                select(total - 1)
                dve.nop().then_inc(att_ready, 1)
                state["p"] += 2
                for c in range(2):
                    dve.wait_ge(o_ready, due(o_ready))
                    oc = O[:, c * 1024:(c + 1) * 1024]
                    do(dve.tensor_reduce(stat[:, 0, 8 * c:8 * c + 8],
                                         E[0][:, c * 1024:(c + 1) * 1024].rearrange("p (n c) -> p n c", c=P), AX.X, ALU.add))
                    inverse_root(8 * c, 8, P)
                    do(dve.tensor_tensor(oc.rearrange("p (n c) -> p n c", c=P), oc.rearrange("p (n c) -> p n c", c=P),
                                         stat[:, 2, 8 * c:8 * c + 8].unsqueeze(2).to_broadcast([P, 8, P]), ALU.mult))
                    dve.tensor_tensor(oc, oc, big[:, 6 + c, :], ALU.mult).then_inc(y_ready, 1)
                for c in range(2):
                    for t in range(TILES):
                        gained(YT[:, 4 * c:4 * c + 4, t * P:(t + 1) * P], 32 + 8 * n_l + 4 * c)
                residual()

            def attention(l):
                state["p"] += 9
                dve.wait_ge(atgain_in, 32)
                for n in range(6):
                    dve.wait_ge(o_ready, due(o_ready))
                    do(dve.tensor_reduce(stat[:, 0, 16 * n:16 * n + 16],
                                         SQ[:, n % 2, :].rearrange("p (n c) -> p n c", c=AT_DIM), AX.X, ALU.add))
                    inverse_root(16 * n, 16, AT_DIM)
                    v16 = big[:, n, :].rearrange("p (n c) -> p n c", c=AT_DIM)
                    do(dve.tensor_tensor(v16, v16, stat[:, 2, 16 * n:16 * n + 16].unsqueeze(2).to_broadcast([P, 16, AT_DIM]),
                                         ALU.mult))
                    do(dve.tensor_tensor(v16, v16, at_gain[:, n, :].unsqueeze(1).to_broadcast([P, 16, AT_DIM]), ALU.mult))
                    v = big[:, n, :].rearrange("p (t h a c) -> p t h a c", t=2, h=8, a=2)
                    w = TMP[:, 0:2048].rearrange("p (a t h c) -> p a t h c", a=4, t=2, h=8)
                    for t in range(TILES):
                        x1, x2 = v[:, t, :, 0, :], v[:, t, :, 1, :]
                        c = cos_t[:, 256 + 32 * t:288 + 32 * t].unsqueeze(1).to_broadcast([P, 8, 32])
                        s = sin_t[:, 256 + 32 * t:288 + 32 * t].unsqueeze(1).to_broadcast([P, 8, 32])
                        step(dve.tensor_tensor(w[:, 0, t], x1, c, ALU.mult))
                        step(dve.tensor_tensor(w[:, 1, t], x2, s, ALU.mult))
                        step(dve.tensor_tensor(w[:, 2, t], x2, c, ALU.mult))
                        step(dve.tensor_tensor(w[:, 3, t], x1, s, ALU.mult))
                    settle()
                    step(dve.tensor_tensor(v[:, :, :, 0, :], w[:, 0], w[:, 1], ALU.subtract))
                    step(dve.tensor_tensor(v[:, :, :, 1, :], w[:, 2], w[:, 3], ALU.add))
                    tell(qk_ready)
                state["k"] += 12
                dve.wait_ge(table_in, due(table_in, 16))
                for it in range(2 * HEADS):
                    t = it // HEADS
                    n = P * (t + 1)
                    ps, free = take_pp()
                    if it >= 2:
                        k_done = state["k"] + (it - 1 if it - 1 <= HEADS else HEADS + 2 * (it - 1 - HEADS))
                        dve.wait_ge(tp_full, k_done)
                    pb_ = PB[:, it % 2, 0:3 * n].rearrange("p (g k) -> p g k", g=NG)
                    mask = table[:, 3 * P * t:3 * P * t + 3 * n].rearrange("p (g k) -> p g k", g=NG)
                    dve.scalar_tensor_tensor(pb_, ps[:, 0:3 * S].rearrange("p (g k) -> p g k", g=NG)[:, :, 0:n],
                                             AT_DIM ** -0.5, mask, ALU.mult, ALU.add).then_inc(free, 1)
                    left_pp()
                    dve.tensor_reduce(stat[:, 0, it:it + 1], PB[:, it % 2, 0:3 * n], AX.X, ALU.max,
                                      negate=True).then_inc(sc_ready, 1)
                state["k"] += 8 + 16
                dve.wait_ge(pv_done, due(pv_done, 16))
                dve.wait_ge(prob_ready, due(prob_ready, 16))
                do(dve.reciprocal(stat[:, 2, 0:16], stat[:, 1, 0:16]))
                dve.tensor_tensor(AO.rearrange("p t (h c) -> p (t h) c", h=8),
                                  MI[:, :, :].rearrange("p t (h c) -> p (t h) c", h=8),
                                  stat[:, 2, 0:16].unsqueeze(2).to_broadcast([P, 16, AT_DIM]), ALU.mult).then_inc(y_ready, 1)
                state["k"] += 2
                residual()

            def retention(l):
                state["p"] += 4
                left_pp(1)
                left_pp(2)
                v = big_f[:, 0:4 * D].rearrange("p (h a s) -> p h a s", a=2, s=S)
                x1, x2 = v[:, :, 0, :], v[:, :, 1, :]
                c = cos_t[:, 0:S].unsqueeze(1).to_broadcast([P, 8, S])
                s = sin_t[:, 0:S].unsqueeze(1).to_broadcast([P, 8, S])
                w = [r.rearrange("p (h s) -> p h s", h=8) for r in RTMP]
                step(dve.tensor_tensor(w[0], x1, c, ALU.mult))
                step(dve.tensor_tensor(w[1], x2, s, ALU.mult))
                step(dve.tensor_tensor(w[2], x2, c, ALU.mult))
                do(dve.tensor_tensor(w[3], x1, s, ALU.mult))
                step(dve.tensor_tensor(x1, w[0], w[1], ALU.subtract))
                step(dve.tensor_tensor(x2, w[2], w[3], ALU.add))
                tell(qk_ready)
                state["p"] += 4
                dve.wait_ge(table_in, due(table_in, 16))
                for h in range(RT_HEADS):
                    ps, free = take_pp()
                    do(dve.tensor_tensor(RATT[:, h, :, :].rearrange("p j t -> p (j t)"), ps[:, 0:3 * P],
                                         table[:, h * 3 * P:(h + 1) * 3 * P], ALU.mult))
                    dve.nop().then_inc(free, 1)
                    dve.nop().then_inc(att_ready, 1)
                state["p"] += 8
                for pair in range(2):
                    dve.wait_ge(o_ready, due(o_ready, 2))
                    inverse_root(4 * pair, 4, PANEL)
                    for h in range(2 * pair, 2 * pair + 2):
                        for t in range(TILES):
                            n = 2 * h + t
                            step(dve.scalar_tensor_tensor(RO[:, h, t, :], RO[:, h, t, :], stat[:, 2, n:n + 1],
                                                          big[:, 8 + h, t * PANEL:(t + 1) * PANEL], ALU.mult, ALU.mult))
                        tell(y_ready)
                for h in range(RT_HEADS):
                    for t in range(TILES):
                        gained(RYT[:, 4 * h:4 * h + 4, t * P:(t + 1) * P], 48 + 4 * h)
                residual()

            def top16(src, n, out_v, out_i):
                for half in range(2):
                    lo = slice(8 * half, 8 * half + 8)
                    for c in range(n):
                        step(dve.max(out_v[:, c, lo], src[:, c, :]))
                    settle()
                    for c in range(n):
                        step(dve.max_index(out_i[:, c, lo], out_v[:, c, lo], src[:, c, :]))
                    settle()
                    if half == 0:
                        for c in range(n):
                            step(dve.match_replace(src[:, c, :], out_v[:, c, lo], src[:, c, :], NEG))
                        settle()

            def route(t, pair):
                k = state["k"] + PAIRS * t + pair
                dve.wait_ge(tp_free[k % 2], k // 2 + 1)
                top16(SC[:, t, 4 * pair:4 * pair + 4, :], 4, val, nidx)
                fi = small(0, 64)
                v = val[:, :, :].rearrange("p (h c) k -> p h c k", c=2)
                a = v[:, :, 0, :].unsqueeze(3).to_broadcast([P, 2, TOPK, TOPK])
                b = v[:, :, 1, :].unsqueeze(2).to_broadcast([P, 2, TOPK, TOPK])
                step(dve.tensor_copy(fi, nidx[:, :, :].rearrange("p c k -> p (c k)")))
                do(dve.tensor_tensor(CAND, a, b, ALU.add))
                top_v = small(64, PAIR).rearrange("p (h k) -> p h k", h=2)
                pos = small(96, PAIR).bitcast(U32)
                top16(CAND.rearrange("p h a b -> p h (a b)"), 2, top_v, pos.rearrange("p (h k) -> p h k", h=2))
                mine_ = slice(PAIR * pair, PAIR * (pair + 1))
                dve.tensor_tensor(gate[:, t, mine_].rearrange("p (h k) -> p h k", h=2), top_v,
                                  top_v[:, :, 0:1].to_broadcast([P, 2, TOPK]), ALU.subtract).then_inc(shift_ready, 1)
                ab = small(128, 2 * PAIR).bitcast(U32)
                step(dve.tensor_scalar(ab[:, 0:PAIR], pos, 4, None, ALU.logical_shift_right))
                do(dve.tensor_scalar(ab[:, PAIR:], pos, 15, None, ALU.bitwise_and))
                abf = small(192, 2 * PAIR)
                do(dve.tensor_copy(abf, ab))
                f4 = fi.rearrange("p (h c k) -> p h c k", h=2, c=2)
                got = small(256, 2 * PAIR)
                for c in range(2):
                    one = ONE.rearrange("p h k i -> p (h k) i")
                    do(dve.tensor_tensor(one, abf[:, PAIR * c:PAIR * (c + 1)].unsqueeze(2).to_broadcast([P, PAIR, TOPK]),
                                         iota[:, :].unsqueeze(1).to_broadcast([P, PAIR, TOPK]), ALU.is_equal))
                    do(dve.tensor_tensor(ONE, ONE, f4[:, :, c, :].unsqueeze(2).to_broadcast([P, 2, TOPK, TOPK]),
                                         ALU.mult))
                    do(dve.tensor_reduce(got[:, PAIR * c:PAIR * (c + 1)], one, AX.X, ALU.add))
                do(dve.scalar_tensor_tensor(idx[:, t, mine_], got[:, 0:PAIR], float(NKEYS), got[:, PAIR:],
                                            ALU.mult, ALU.add))
                dve.nop().then_inc(idx_ready, 1)

            def dots(l, t, pair):
                base = (l * TILES + t) * SLOTS + PAIR * pair
                turns = (l * TILES + t) * 2 * SLOTS // RING + 2 * pair
                copies = mine.n
                with dve.Fori(0, 2) as i:
                    dve.wait_ge(dve_done, i + copies)
                    for r in range(RING):
                        dve.wait_ge(land[r], i * 16 + (turns + 1) * 16)
                        dve.tensor_tensor_reduce(big[:, r, :], big[:, r, :], hn[:, t, :], 1.0, 0.0, ALU.mult,
                                                 ALU.add, dot16[:, r:r + 1]).then_inc(u_used, 1)
                    dve.wait_ge(u_used, i * RING + (base + RING))
                    dve.wait_ge(idx_ready, (l * TILES + t) * PAIRS + pair + 1)
                    dve.tensor_copy(act_v[:, t, bass.ds(i * RING + PAIR * pair, RING)], dot16[:, :]).then_inc(dve_done, 1)
                mine.n += 2

            def sums(l, t, pair):
                turns = (l * TILES + t) * 2 * SLOTS // RING + SLOTS // RING + 2 * pair
                base = (l * TILES + t) * (1 + PAIRS * 2 * len(V_DVE)) + 1 + 2 * pair * len(V_DVE)
                with dve.Fori(0, 2) as i:
                    for n, r in enumerate(V_DVE):
                        dve.wait_ge(land[r], i * 16 + (turns + 1) * 16)
                        dve.wait_ge(vd_used, i * len(V_DVE) + (base + n))
                        dve.scalar_tensor_tensor(ACC[t], big[:, r, :],
                                                 act_v[:, t, bass.ds(i * RING + (PAIR * pair + r), 1)], ACC[t],
                                                 ALU.mult, ALU.add).then_inc(vd_used, 1)

            def weigh(t):
                dve.wait_ge(gate_exp, due(gate_exp))
                g3 = gate[:, t, :].rearrange("p (h k) -> p h k", h=HEADS)
                do(dve.tensor_reduce(stat[:, 0, 0:8], g3, AX.X, ALU.add))
                do(dve.reciprocal(stat[:, 1, 0:8], stat[:, 0, 0:8]))
                do(dve.tensor_tensor(g3, g3, stat[:, 1, 0:8].unsqueeze(2).to_broadcast([P, HEADS, TOPK]), ALU.mult))
                dve.wait_ge(gelu_ready, due(gelu_ready))
                do(dve.tensor_tensor(act_v[:, t, :], act_v[:, t, :], gate[:, t, :], ALU.mult))
                dve.nop().then_inc(w_ready, 1)

            def peer(l):
                state["p"] += 4
                state["k"] += 4
                scored = state["k"] + 2 * PAIRS
                route(0, 0)
                route(0, 1)
                dots(l, 0, 0)
                route(0, 2)
                dots(l, 0, 1)
                route(0, 3)
                dots(l, 0, 2)
                dots(l, 0, 3)
                tell(dots_ready)
                weigh(0)
                dve.wait_ge(tp_full, scored)
                for t in range(TILES):
                    dve.memset(ACC[t], 0.0).then_inc(vd_used, 1)
                    for pair in range(PAIRS):
                        sums(l, t, pair)
                        if t == 0:
                            route(1, pair)
                    if t == 0:
                        for pair in range(PAIRS):
                            dots(l, 1, pair)
                            if pair == 1:
                                state["k"] = scored
                                finish(l, 0)
                        tell(dots_ready)
                        weigh(1)
                finish(l, 1)

            def finish(l, t):
                ps, free = take_pp()
                dve.wait_ge(vd_used, (l * TILES + t + 1) * (1 + PAIRS * 2 * len(V_DVE)))
                do(dve.tensor_tensor(x[:, t, :], ps, ACC[t], ALU.add))
                dve.nop().then_inc(free, 1)
                dve.nop().then_inc(x_ready, 1)
                if l + 1 < DEPTH:
                    norm(t)

            for s in range(2):
                dve.nop().then_inc(pp_free[s], 1)
            dve.wait_ge(consts_in, 16 * 9)
            ang, w1, w2 = E[1][:, 0:320], E[1][:, 320:640], E[1][:, 640:960]
            wi = E[1][:, 960:1280].bitcast(I32)
            pf = E[2][:, 0:258]
            step(dve.memset(ones[:, :], 1.0))
            do(dve.tensor_copy(pf, E[0][:, 0:258].bitcast(I32)))
            step(dve.tensor_scalar(ang[:, 0:256], pf[:, 0:256], E[0][:, 258:259], None, ALU.mult))
            for t in range(TILES):
                step(dve.tensor_scalar(ang[:, 256 + 32 * t:288 + 32 * t], E[0][:, 260:292], pf[:, 256 + t:257 + t],
                                       None, ALU.mult))
            settle()
            do(dve.tensor_scalar(w1, ang, 1.0 / TWO_PI, None, ALU.mult))
            do(dve.tensor_copy(wi, w1))
            do(dve.tensor_copy(w1, wi))
            for part in (C1, C2, C3):
                do(dve.scalar_tensor_tensor(ang, w1, -part, ang, ALU.mult, ALU.add))
            for limit, compare, shift in ((math.pi, ALU.is_gt, -TWO_PI), (-math.pi, ALU.is_lt, TWO_PI)):
                do(dve.tensor_scalar(w2, ang, limit, shift, compare, ALU.mult))
                do(dve.tensor_tensor(ang, ang, w2, ALU.add))
            do(dve.tensor_scalar(sin_t[:, :], ang, PI_IN, -PI_IN, ALU.min, ALU.max))
            do(dve.scalar_tensor_tensor(w2, sin_t[:, :], -1.0, sin_t[:, :], ALU.mult, ALU.max))
            do(dve.tensor_scalar(cos_t[:, :], w2, -1.0, math.pi / 2, ALU.mult, ALU.add))
            dve.nop().then_inc(trig_arg, 1)
            tp, free = take_tp()
            do(dve.tensor_copy(feat[:, :], tp[:, 0:64]))
            dve.nop().then_inc(free, 1)
            f4 = feat[:, 0:32].rearrange("p (l h) -> p l h", l=DEPTH)
            m8 = stat[:, 3, 0:8]
            do(dve.tensor_reduce(m8, feat[:, 0:32].rearrange("p (l h) -> p h l", l=DEPTH), AX.X, ALU.max))
            do(dve.tensor_tensor(f4, f4, m8.unsqueeze(1).to_broadcast([P, DEPTH, HEADS]), ALU.subtract))
            dve.nop().then_inc(lb_arg, 1)
            dve.wait_ge(lb_exp, due(lb_exp))
            do(dve.tensor_reduce(m8, feat[:, 0:32].rearrange("p (l h) -> p h l", l=DEPTH), AX.X, ALU.add))
            do(dve.reciprocal(stat[:, 3, 8:16], m8))
            do(dve.tensor_tensor(f4, f4, stat[:, 3, 8:16].unsqueeze(1).to_broadcast([P, DEPTH, HEADS]), ALU.mult))
            run = stat[:, 3, 16:24]
            do(dve.tensor_copy(run, f4[:, 0, :]))
            for l in range(DEPTH):
                if l:
                    do(dve.tensor_tensor(run, run, f4[:, l, :], ALU.add))
                if l % 3 == 0:
                    do(dve.tensor_tensor(lb[:, l // 3, 0, :], run, f4[:, 0, :], ALU.subtract))
                    do(dve.tensor_scalar(lb[:, l // 3, 1, :], lb[:, l // 3, 0, :], -1.0, 1.0, ALU.mult, ALU.add))
            dve.nop().then_inc(lb_ready, 1)
            dve.wait_ge(trig_ready, due(trig_ready, 2))
            for t in range(TILES):
                norm(t)
            for l in range(DEPTH):
                (hgrn, attention, retention)[l % 3](l)
                for t in range(TILES):
                    norm(t)
                peer(l)


def kernel(**inputs):
    import concourse.bacc as _bacc
    from concourse.bass_utils import run_bass_kernel_spmd as _run

    nc = _bacc.Bacc("TRN2", target_bir_lowering=False, num_devices=1)
    arrays, args = {}, {}
    for name, a in {**inputs, **shape_constants()}.items():
        a = np.ascontiguousarray(a)
        arrays[f"in_{name}"] = a
        args[name] = nc.dram_tensor(f"in_{name}", a.shape, mybir.dt.from_np(a.dtype), kind="ExternalInput").ap()
    out = nc.dram_tensor("out_0", (1, S, D), F32, kind="ExternalOutput").ap()
    trunk(nc, args, out)
    r = _run(nc, [arrays], core_ids=[0])
    return r.results[0]["out_0"]
```

```python
from contextlib import ExitStack
import math

import numpy as np
import concourse.bass as bass
from concourse import mybir

F32 = mybir.dt.float32
I32 = mybir.dt.int32
U32 = mybir.dt.uint32
ALU = mybir.AluOpType
ACT = mybir.ActivationFunctionType
AX = mybir.AxisListType

P = 128
D = 1024
S = 256
TILES = S // P
KT = D // P
PANEL = 512
DEPTH = 4
EPS = 1e-6
TINY = 1e-30
HEADS = 8
LEVELS = [64, 32, 16, 8, 4, 2, 1]
GATE_AFTER = (0, 1, 4)
GROUPS = ((128, 1), (512, 4), (2048, 16))
NG = len(GROUPS)
AT_TURN = 10
AT_DIM = 64
RT_HEADS = 4
TOPK = 16
NKEYS = 128
SLOTS = HEADS * TOPK
RING = 16
PAIR = 2 * TOPK
PAIRS = SLOTS // PAIR
V_DVE = (3, 7, 11, 15)
V_PE = tuple(r for r in range(RING) if r not in V_DVE)
NEG = -3.0e38
LN_SHIFT = 60
TWO_PI = 2.0 * math.pi
C1 = 6.28125
C2 = float(np.float32(np.round((TWO_PI - C1) * 2.0 ** 21) / 2.0 ** 21))
C3 = TWO_PI - C1 - C2
PI_IN = float(np.nextafter(np.float32(math.pi), np.float32(0)))


def shape_constants():
    s = np.arange(P)[:, None]
    t = np.arange(P)[None, :]
    level = [((s // (2 * m) == t // (2 * m)) & (s % (2 * m) < m) & (t % (2 * m) >= m)) for m in LEVELS]
    masks = np.stack(level, 1).astype(np.int32).reshape(P, -1)
    at = []
    for tile in range(TILES):
        q = tile * P + np.arange(P)[:, None]
        for window, dilation in GROUPS:
            k = np.arange(P * (tile + 1))[None, :]
            ok = (q >= k) & ((q - k) % dilation == 0) & ((q - k) // dilation <= window // dilation)
            at.append(np.where(ok, 0.0, -1e30))
    at = np.concatenate(at, 1).astype(np.float32)
    lg = np.log1p(-np.exp2(-5.0 - np.arange(RT_HEADS)))
    scale = 256.0 ** -0.5
    near = [np.where(t >= s, np.exp(g * np.maximum(t - s, 0)), 0.0) * scale for g in lg]
    far = [np.exp(g * (t - s + P)) * scale for g in lg]
    decay = np.stack([np.stack([n, n, f], 1) for n, f in zip(near, far)], 1)
    decay = decay.astype(np.float32).reshape(P, -1)
    theta = np.float32(10000.0)
    inv_at = theta ** (-np.arange(32, dtype=np.float32) / np.float32(32))
    inv_rt = theta ** (-np.arange(128, dtype=np.float32) / np.float32(128))
    return {
        "c_ident": np.eye(P, dtype=np.float32),
        "c_levels": masks,
        "c_window": at,
        "c_decay": decay,
        "c_inv_at": np.tile(inv_at.astype(np.float32), (P, 1)),
        "c_inv_rt": inv_rt.astype(np.float32).reshape(P, 1),
        "c_iota": np.tile(np.arange(TOPK, dtype=np.float32), (P, 1)),
    }


def routings(layer, tile, pair):
    return layer * (TILES * PAIRS + 1) + tile * (PAIRS + 1) + pair + (2 if tile == 0 else 1)


class Due:

    def __init__(self):
        self.value = {}

    def __call__(self, sem, more=1):
        self.value[sem.name] = self.value.get(sem.name, 0) + more
        return self.value[sem.name]


class Mine:

    def __init__(self, sem):
        self.sem, self.n = sem, 0

    def step(self, instruction):
        instruction.then_inc(self.sem, 1)
        self.n += 1


def trunk(nc, A, out):
    ctx = ExitStack()
    with ctx:
        def sb(name, shape, dt=F32):
            return ctx.enter_context(nc.sbuf_tensor(name, shape, dt))

        def pb(name, shape):
            return ctx.enter_context(nc.psum_tensor(name, shape, F32))

        def sem(name):
            return ctx.enter_context(nc.semaphore(name))

        x = sb("x", [P, TILES, D])
        hn = sb("hn", [P, TILES, D])
        hT = sb("hT", [P, KT, S])
        gain = sb("gain", [P, D])
        big = sb("big", [P, 16, D])
        wring = sb("wring", [P, 2, KT * PANEL])
        scr = sb("scr", [P, 16384])
        table = sb("table", [P, 1536])
        ident = sb("ident", [P, P])
        iota = sb("iota", [P, TOPK])
        ones = sb("ones", [P, P])
        at_gain = sb("at_gain", [P, 6, AT_DIM])
        sin_t = sb("sin_t", [P, 320])
        cos_t = sb("cos_t", [P, 320])
        rows = sb("rows", [64, P])
        feat = sb("feat", [P, 64])
        lb = sb("lb", [P, 2, 2, HEADS])
        stat = sb("stat", [P, 4, 96])
        val = sb("val", [P, 4, TOPK])
        nidx = sb("nidx", [P, 4, TOPK], U32)
        idx = sb("idx", [P, TILES, SLOTS], U32)
        gate = sb("gate", [P, TILES, SLOTS])
        act_v = sb("act_v", [P, TILES, SLOTS])
        dot16 = sb("dot16", [P, RING])
        idx16 = sb("idx16", [P, 2, RING], U32)

        PP = pb("PP", [P, 2, 1024])
        TP = pb("TP", [P, 2, 512])
        MI = pb("MI", [P, 2, 512])

        def cut(a, n):
            return scr[:, a:a + n]

        def small(a, n):
            return scr[:, 4096 + a:4096 + a + n]

        ident_in = sem("ident_in")
        consts_in = sem("consts_in")
        x_in = sem("x_in")
        atgain_in = sem("atgain_in")
        gain_in = sem("gain_in")
        table_in = sem("table_in")
        keys_in = sem("keys_in")
        w_in = [sem(f"w_in{s}") for s in range(2)]
        half_used = sem("half_used")
        pp_full = sem("pp_full")
        pp_free = [sem(f"pp_free{s}") for s in range(2)]
        tp_full = sem("tp_full")
        tp_free = [sem(f"tp_free{s}") for s in range(2)]
        x_ready = sem("x_ready")
        act_done = sem("act_done")
        dve_done = sem("dve_done")
        sq_ready = sem("sq_ready")
        ms_ready = sem("ms_ready")
        root_ready = sem("root_ready")
        hn_ready = sem("hn_ready")
        trig_arg = sem("trig_arg")
        trig_ready = sem("trig_ready")
        lb_ready = sem("lb_ready")
        lb_arg = sem("lb_arg")
        lb_exp = sem("lb_exp")
        sig_ready = sem("sig_ready")
        forget_ready = sem("forget_ready")
        log_ready = sem("log_ready")
        key_ready = sem("key_ready")
        sums_ready = sem("sums_ready")
        diff_ready = sem("diff_ready")
        exp_ready = sem("exp_ready")
        pair_ready = sem("pair_ready")
        level_taken = sem("level_taken")
        att_ready = sem("att_ready")
        o_ready = sem("o_ready")
        y_ready = sem("y_ready")
        qk_ready = sem("qk_ready")
        sc_ready = sem("sc_ready")
        prob_ready = sem("prob_ready")
        pv_done = sem("pv_done")
        v_full = sem("v_full")
        v_ready = sem("v_ready")
        query_full = sem("query_full")
        query_ready = sem("query_ready")
        idx_ready = sem("idx_ready")
        staged = sem("staged")
        turn_taken = sem("turn_taken")
        land = [sem(f"land{s}") for s in range(RING)]
        u_used = sem("u_used")
        vp_used = sem("vp_used")
        vd_used = sem("vd_used")
        dots_ready = sem("dots_ready")
        shift_ready = sem("shift_ready")
        gate_exp = sem("gate_exp")
        gelu_ready = sem("gelu_ready")
        w_ready = sem("w_ready")
        diag_ready = sem("diag_ready")
        out_done = sem("out_done")

        def weights(l):
            kind, i = l % 3, l // 3
            if kind == 0:
                return A["hg_w_in"][i], A["hg_w_out"][i], 1, KT
            if kind == 1:
                return A["at_w_in"][i], A["at_w_out"][i], 1, 4
            return A["rt_w_in"][i], A["rt_w_out"][i], 2, KT

        big_f = big[:, :, :].rearrange("p a b -> p (a b)")
        Q3 = big_f[:, 0:2048]
        E = [cut(2048 * i, 2048) for i in range(3)]
        ATT = cut(6144, 2048)
        B = cut(8192, 2048)
        ATTX = cut(10240, 1024)
        O = cut(11264, 2048)
        YT = cut(13312, 2048).rearrange("p (k s) -> p k s", k=KT)
        lvl = table[:, 0:len(LEVELS) * P].bitcast(I32).rearrange("p (l t) -> p l t", l=len(LEVELS))

        QKT = cut(0, 6144).rearrange("p (n b s) -> p n b s", n=6, b=4)
        TMP = cut(6144, 6144)
        SQ = cut(10240, 2048).rearrange("p (a b) -> p a b", a=2)
        PB = cut(6144, 1536).rearrange("p (a b) -> p a b", a=2)
        PT = cut(7680, 1536).rearrange("p (a b) -> p a b", a=2)
        AO = cut(9216, 1024).rearrange("p (t c) -> p t c", t=2)
        AYT = cut(12288, 1024).rearrange("p (k s) -> p k s", k=4)

        RTMP = [cut(2048 * i, 2048) for i in range(4)]
        RO = cut(0, 4096).rearrange("p (h t c) -> p h t c", h=4, t=2)
        RYT = cut(4096, 4096).rearrange("p (k s) -> p k s", k=16)
        RATT = cut(8192, 1536).rearrange("p (h j t) -> p h j t", h=4, j=3)
        RJ = cut(10240, 4096).rearrange("p (n c) -> p n c", n=8)

        PQ = cut(0, 4096).rearrange("p (c s) -> p c s", c=16)
        ACC = [cut(1024 * t, 1024) for t in range(TILES)]
        KEYS = cut(4096, 2048).rearrange("p (c d) -> p c d", c=16)
        KEYST = cut(6144, 2048).rearrange("p (c n) -> p c n", c=16)
        SC = cut(8192, 4096).rearrange("p (t c n) -> p t c n", t=TILES, c=16)
        ONE = cut(12288, 512).rearrange("p (h k i) -> p h k i", h=2, k=TOPK)
        CAND = cut(12800, 512).rearrange("p (h a b) -> p h a b", h=2, a=TOPK)
        DIAG = cut(13312, 2048).rearrange("p (r n) -> p r n", r=RING)

        block = ctx.enter_context(nc.Block())

        @block.sync
        def _(sp):
            sp.dma_start(ident[:, :], A["c_ident"]).then_inc(ident_in, 16)
            sp.dma_start(x[:, :, :], A["x"][0].rearrange("(t p) d -> p t d", p=P)).then_inc(x_in, 16)
            g = p = 0
            halved = 0
            free_at = [(pp_full, 0), (pp_full, 0)]

            def panels(source, n, halves=1, kt=KT, first=0):
                nonlocal g, p, halved
                view = source.rearrange("(h k p) (n c) -> n h p k c", p=P, k=kt, c=PANEL)
                flat = source.rearrange("(k p) n -> p k n", p=P)

                def load(src, slot, used, count):
                    if not isinstance(count, int) or count:
                        sp.wait_ge(used, count)
                    dst = wring[:, slot, 0:kt * PANEL].rearrange("p (k c) -> p k c", k=kt)
                    sp.dma_start(dst, src).then_inc(w_in[slot], 16)

                pairs = n // 2 if halves == 1 and n >= 4 else 0
                for j in range(2 if pairs else n * halves):
                    slot = (g + j) % 2
                    if halves == 2 and j >= 2 and j % 2 == 0:
                        halved += 1
                        load(view[first + j // 2, 0], slot, half_used, halved)
                    else:
                        load(view[first + j // halves, j % halves], slot, *free_at[slot])
                    free_at[slot] = (pp_full, p + j // halves + 1)
                if pairs:
                    with sp.Fori(0, pairs - 1) as i:
                        for u in range(2):
                            load(flat[:, :, bass.ds((i * 2 + (first + 2 + u)) * PANEL, PANEL)], (g + u) % 2, pp_full,
                                 i * 2 + (p + u + 1))
                    for j in range(n - 2, n):
                        free_at[(g + j) % 2] = (pp_full, p + j + 1)
                    if n % 2:
                        slot = (g + n - 1) % 2
                        load(view[first + n - 1, 0], slot, pp_full, p + n - 2)
                if halves == 2 or source is wo:
                    halved += 1
                    free_at[g % 2] = (half_used, halved)
                g += n * halves
                p += n

            for l in range(DEPTH):
                w, wo, halves, kt = weights(l)
                plan = {0: ((6, 5), (1, 9), (1, 7)), 1: ((9, 16),), 2: ((8, 4), (2, 2), (2, 2))}[l % 3]
                first = 0
                for n, own in plan:
                    panels(w, n, first=first)
                    first += n
                    p += own
                if l % 3 == 1:
                    free_at[(g - 1) % 2] = (pp_full, p - 2 * HEADS + HEADS + 3)
                panels(wo, 2, halves, kt)
                panels(A["pk_w_q"][l], 4)
                p += TILES
            sp.wait_ge(x_ready, 4 * DEPTH)
            sp.dma_start(out[0].rearrange("(t p) d -> p t d", p=P), x[:, :, :]).then_inc(out_done, 16)
            sp.wait_ge(out_done, 16)

        @block.gpsimd
        def _(pool):
            due = Due()
            pool.dma_start(gain[:, :], A["mix_norm"][0:1].to_broadcast([P, D])).then_inc(gain_in, 16)
            pool.dma_start(iota[:, :], A["c_iota"]).then_inc(consts_in, 16)
            pool.dma_start(rows[0:32, :], A["hg_lb"].rearrange("l (h p) -> (l h) p", p=P)).then_inc(consts_in, 16)
            pool.dma_start(rows[32:48, :], A["hg_onorm"].rearrange("l (h p) -> (l h) p", p=P)).then_inc(consts_in, 16)
            pool.dma_start(rows[48:64, :], A["rt_onorm"].rearrange("l (h p) -> (l h) p", p=P)).then_inc(consts_in, 16)
            pool.dma_start(E[0][:, 0:256].bitcast(I32), A["positions"].to_broadcast([P, S])).then_inc(consts_in, 16)
            pool.dma_start(E[0][:, 256:258].bitcast(I32), A["positions"].rearrange("a (t p) -> p (a t)", p=P),
                           allow_slow_non_contiguous=True).then_inc(consts_in, 16)
            pool.dma_start(E[0][:, 258:259], A["c_inv_rt"]).then_inc(consts_in, 16)
            pool.dma_start(E[0][:, 260:292], A["c_inv_at"]).then_inc(consts_in, 16)

            for n, name in enumerate(("at_qnorm", "at_knorm")):
                pool.dma_start(at_gain[:, 3 * n:3 * n + 3, :],
                               A[name][0].unsqueeze(0).to_broadcast([P, NG, AT_DIM])).then_inc(atgain_in, 16)

            def gather_group(src, t, half, column, ready, used):
                pool.wait_ge(idx_ready, ready)
                pool.sem_inc(turn_taken, 1)
                pool.tensor_copy(idx16[:, half, :], idx[:, t, bass.ds(column, RING)]).then_inc(staged, 1)
                for r in range(RING):
                    if used is not None:
                        pool.wait_ge(*used(r))
                    pool.wait_ge(staged, steps[0])
                    pool.sem_inc(turn_taken, 1)
                    pool.indirect_dma_start(
                        big[:, r, :], None, src,
                        bass.IndirectOffsetOnAxis(ap=idx16[:, half, r:r + 1], axis=0),
                        element_offset=l * NKEYS * NKEYS * D).then_inc(land[r], 16)

            def u_through(n):
                return lambda r: (u_used, n * RING + (r + 1))

            def v_through(turn, i):
                def count(r):
                    if r in V_DVE:
                        return vd_used, i * len(V_DVE) + (turn * (1 + PAIRS * 2 * len(V_DVE)) + V_DVE.index(r) + 2)
                    return vp_used, i * len(V_PE) + (turn * 2 * PAIRS * len(V_PE) + V_PE.index(r) + 1)
                return count

            def table_load(l):
                kind = l % 3
                cols = (len(LEVELS) * P, 3 * P * 3, 1536)[kind]
                dst = table[:, 0:cols].bitcast(I32) if kind == 0 else table[:, 0:cols]
                pool.dma_start(dst, A[("c_levels", "c_window", "c_decay")[kind]]).then_inc(table_in, 16)
                if l:
                    pool.dma_start(gain[:, :], A["mix_norm"][l:l + 1].to_broadcast([P, D])).then_inc(gain_in, 16)

            def differences(l):
                pool.wait_ge(lb_ready, 1)
                pool.wait_ge(sig_ready, due(sig_ready, 2) - 1)
                kk, neg = big_f[:, 8 * D:10 * D], big_f[:, 10 * D:12 * D]
                pool.tensor_tensor(kk.rearrange("p (h s) -> p h s", h=HEADS), neg.rearrange("p (h s) -> p h s", h=HEADS),
                                   lb[:, l // 3, 1, :].unsqueeze(2).to_broadcast([P, HEADS, S]),
                                   ALU.mult).then_inc(key_ready, 1)
                pool.wait_ge(sums_ready, due(sums_ready))
                for n, m in enumerate(LEVELS + [P]):
                    b = B.rearrange("p (n two m) -> p n two m", two=2, m=m)
                    e = E[n % 3].rearrange("p (n two m) -> p n two m", two=2, m=m)
                    mid = b[:, :, 0, m - 1:m].to_broadcast([P, 2048 // (2 * m), m])
                    if n >= 3:
                        pool.wait_ge(level_taken, due(level_taken))
                    pool.tensor_tensor(e[:, :, 0, :], mid, b[:, :, 0, :], ALU.subtract).then_inc(diff_ready, 1)
                    if m < P:
                        pool.tensor_tensor(e[:, :, 1, :], b[:, :, 1, :], mid, ALU.subtract).then_inc(diff_ready, 1)
                    else:
                        pool.tensor_copy(e[:, :, 1, :], b[:, :, 1, :]).then_inc(diff_ready, 1)
                due(level_taken, 3)

            steps = [0]
            table_load(0)
            for l in range(DEPTH):
                if l % 3 == 0:
                    differences(l)
                pool.wait_ge(hn_ready, due(hn_ready, TILES))
                pool.dma_start(gain[:, :], A["ffn_norm"][l:l + 1].to_broadcast([P, D])).then_inc(gain_in, 16)
                pool.wait_ge(x_ready, 4 * l + (2 if l % 3 == 2 else 1))
                pool.dma_start(KEYS, A["pk_keys"][l].rearrange("h c n d -> n (h c) d")).then_inc(keys_in, 16)
                pool.wait_ge(hn_ready, due(hn_ready, TILES))
                if l + 1 < DEPTH:
                    table_load(l + 1)
                groups = SLOTS // RING
                for t in range(TILES):
                    turn = l * TILES + t
                    for phase in range(2):
                        src = (A["pk_u"], A["pk_v"])[phase].rearrange("l e d -> (l e) d")

                        def through(i):
                            return v_through(turn, i) if phase else u_through(i + turn * groups)

                        if phase:
                            before = u_through(turn * groups + groups - 1)
                        else:
                            before = v_through(turn - 1, groups - 1) if turn else None
                        routed = routings(l, t, PAIRS - 1) if phase else routings(l, t, 0) - (t == 0)
                        now = steps[0]
                        steps[0] = now + 1
                        gather_group(src, t, 0, 0, routed, before)
                        with pool.Fori(0, groups // 2 - 1) as i:
                            for k in range(2):
                                steps[0] = i * 2 + (now + 2 + k)
                                gather_group(src, t, 1 - k, i * (2 * RING) + RING * (1 + k),
                                             routed if phase else i + (routings(l, t, 0) + k), through(i * 2 + k))
                        steps[0] = now + groups
                        gather_group(src, t, 1, SLOTS - RING, routings(l, t, PAIRS - 1), through(groups - 2))

        @block.tensor
        def _(pe):
            due = Due()
            state = {"g": 0, "p": 0, "k": 0}

            def wait_pp():
                p = state["p"]
                pe.wait_ge(pp_free[p % 2], p // 2 + 1)
                state["p"] = p + 1
                return PP[:, p % 2, :]

            def turn(blocks, offset=0):
                k = state["k"]
                pe.wait_ge(tp_free[k % 2], k // 2)
                for j, b in enumerate(blocks):
                    last = pe.transpose(TP[0:b.shape[-1], k % 2, j * P:j * P + b.shape[0]], b,
                                        ident[0:b.shape[0], 0:b.shape[0]])
                last.then_inc(tp_full, 1)
                state["k"] = k + 1

            def project(n, feature_major, src, kt=KT, halves=1, between=None):
                g, p = state["g"], state["p"]

                def panel(slot, w_turn, ps, p_turn, half):
                    pe.wait_ge(w_in[slot], w_turn * 16 + 16)
                    if half == 0:
                        pe.wait_ge(pp_free[ps], p_turn + 1)
                    w = wring[:, slot, 0:kt * PANEL].rearrange("p (k c) -> p k c", k=kt)
                    for o in range(4 if feature_major else TILES):
                        for k in range(kt):
                            flags = dict(start=(half == 0 and k == 0), stop=(half == halves - 1 and k == kt - 1))
                            if feature_major:
                                last = pe.matmul(PP[:, ps, o * S:(o + 1) * S], w[:, k, o * P:(o + 1) * P],
                                                 src[:, k, :], **flags)
                            else:
                                last = pe.matmul(PP[:, ps, o * PANEL:(o + 1) * PANEL],
                                                 src[:, half * kt + k, o * P:(o + 1) * P], w[:, k, :], **flags)
                    last.then_inc(pp_full if half == halves - 1 else half_used, 1)

                pairs = n // 2 if halves == 1 and n >= 4 else 0
                if pairs:
                    with pe.Fori(0, pairs) as i:
                        for u in range(2):
                            panel((g + u) % 2, i + (g + u) // 2, (p + u) % 2, i + (p + u) // 2, 0)
                for j in range(2 * pairs, n):
                    for half in range(halves):
                        m = g + j * halves + half
                        if between is not None and (j, half) == (0, 1):
                            between()
                        panel(m % 2, m // 2, (p + j) % 2, (p + j) // 2, half)
                state["g"], state["p"] = g + n * halves, p + n

            def split_panel(feature_major, between, told=None):
                g, p = state["g"], state["p"]
                pe.wait_ge(w_in[g % 2], g // 2 * 16 + 16)
                pe.wait_ge(pp_free[p % 2], p // 2 + 1)
                w = wring[:, g % 2, :].rearrange("p (k c) -> p k c", k=KT)
                for t in range(TILES):
                    if t:
                        between()
                    tokens = slice(t * P, (t + 1) * P)
                    for o in range(4 if feature_major else 1):
                        for k in range(KT):
                            flags = dict(start=(k == 0), stop=(k == KT - 1))
                            if feature_major:
                                last = pe.matmul(PP[:, p % 2, o * S + t * P:o * S + (t + 1) * P],
                                                 w[:, k, o * P:(o + 1) * P], hT[:, k, tokens], **flags)
                            else:
                                last = pe.matmul(PP[:, p % 2, t * PANEL:(t + 1) * PANEL], hT[:, k, tokens],
                                                 w[:, k, :], **flags)
                    if t == 0 and told is not None:
                        last.then_inc(told, 1)
                last.then_inc(pp_full, 1)
                state["g"], state["p"] = g + 1, p + 1

            def out_project(src, kt, between):
                g = state["g"]
                w = [wring[:, (g + c) % 2, 0:kt * PANEL].rearrange("p (k c) -> p k c", k=kt) for c in range(2)]
                for t in range(TILES):
                    if t:
                        between()
                    ps = wait_pp()
                    for c in range(2):
                        pe.wait_ge(w_in[(g + c) % 2], (g + c) // 2 * 16 + 16)
                        for k in range(kt):
                            last = pe.matmul(ps[:, c * PANEL:(c + 1) * PANEL], src[:, k, t * P:(t + 1) * P],
                                             w[c][:, k, :], start=(k == 0), stop=(k == kt - 1))
                        if t and c == 0:
                            last.then_inc(half_used, 1)
                            norm_turn(0)
                    last.then_inc(pp_full, 1)
                state["g"] = g + 2

            def first_panel(feature_major):
                left_tp(1)
                left_tp(2)
                split_panel(feature_major, tile1_turned)

            def tile1_turned():
                norm_turn(1)
                left_tp(1)
                left_tp(2)

            def left_pp(back=1):
                p = state["p"] - back
                pe.wait_ge(pp_free[p % 2], p // 2 + 2)

            def left_tp(back=1):
                k = state["k"] - back
                pe.wait_ge(tp_free[k % 2], k // 2 + 1)

            def norm_turn(t):
                pe.wait_ge(hn_ready, due(hn_ready))
                for half in range(2):
                    turn([hn[:, t, (4 * half + j) * P:(4 * half + j + 1) * P] for j in range(4)])

            def hgrn(l):
                kk = big_f[:, 8 * D:10 * D]

                def level(n):
                    pe.wait_ge(pair_ready, due(pair_ready))
                    for f in range(2):
                        ps = wait_pp()
                        for j in range(8):
                            c = (8 * f + j) * P
                            last = pe.matmul(ps[:, j * P:(j + 1) * P], E[n % 3][:, c:c + P], E[n % 3][:, c:c + P],
                                             start=True, stop=True)
                        last.then_inc(pp_full, 1)

                first_panel(True)
                if l == 0:
                    pe.wait_ge(consts_in, 16 * 8)
                    turn([rows[:, :]])
                project(3, True, hT)
                project(2, False, hT)

                def gate_part(t):
                    g = state["g"]
                    pe.wait_ge(w_in[g % 2], g // 2 * 16 + 16)
                    w = wring[:, g % 2, :].rearrange("p (k c) -> p k c", k=KT)
                    ps = wait_pp()
                    for k in range(KT):
                        last = pe.matmul(ps[:, 0:PANEL], hT[:, k, t * P:(t + 1) * P], w[:, k, :],
                                         start=(k == 0), stop=(k == KT - 1))
                    last.then_inc(pp_full, 1)
                    state["g"] = g + t

                gate_part(0)
                pe.wait_ge(key_ready, due(key_ready))
                for f in range(2):
                    ps = wait_pp()
                    for j in range(8):
                        c = (8 * f + j) * P
                        last = pe.matmul(ps[:, j * P:(j + 1) * P], kk[:, c:c + P], Q3[:, c:c + P],
                                         start=True, stop=True)
                    last.then_inc(pp_full, 1)
                level(0)
                gate_part(1)
                level(1)
                gate_part(0)
                for n in (2, 3, 4):
                    level(n)
                gate_part(1)
                for n in range(5, len(LEVELS)):
                    level(n)
                n = len(LEVELS)
                pe.wait_ge(pair_ready, due(pair_ready))
                ps = wait_pp()
                for h in range(HEADS):
                    c = h * S
                    last = pe.matmul(ps[:, h * P:(h + 1) * P], E[n % 3][:, c:c + P], E[n % 3][:, c + P:c + S],
                                     start=True, stop=True)
                last.then_inc(pp_full, 1)
                for t in range(TILES):
                    pe.wait_ge(att_ready, due(att_ready))
                    ps = wait_pp()
                    for h in range(HEADS):
                        o = ps[:, h * P:(h + 1) * P]
                        v = [big[:, 4 + h // 4, s * PANEL + h % 4 * P:s * PANEL + (h % 4 + 1) * P] for s in range(2)]
                        a = ATT[:, (2 * h + t) * P:(2 * h + t + 1) * P]
                        last = pe.matmul(o, a, v[t], start=True, stop=(t == 0))
                        if t:
                            last = pe.matmul(o, ATTX[:, h * P:(h + 1) * P], v[0], start=False, stop=True)
                    last.then_inc(pp_full, 1)

                def turn_y(t):
                    pe.wait_ge(y_ready, due(y_ready))
                    for c in range(2):
                        b = t * D + c * PANEL
                        turn([O[:, b + j * P:b + (j + 1) * P] for j in range(4)])
                    left_tp(1)
                    left_tp(2)

                turn_y(0)
                out_project(YT, KT, lambda: turn_y(1))

            def attention(l):
                def turn_qk(n):
                    pe.wait_ge(qk_ready, due(qk_ready))
                    for t in range(TILES):
                        turn([big[:, n, t * PANEL + j * P:t * PANEL + (j + 1) * P] for j in range(4)])

                for n in range(9):
                    if n == 0:
                        first_panel(False)
                    elif n < 8:
                        project(1, False, hT)
                    else:
                        g = state["g"]
                        pe.wait_ge(w_in[g % 2], g // 2 * 16 + 16)
                        w = wring[:, g % 2, :].rearrange("p (k c) -> p k c", k=KT)
                        ps = wait_pp()
                        for k in range(KT):
                            last = pe.matmul(ps[:, 0:PANEL], hT[:, k, 0:P], w[:, k, :],
                                             start=(k == 0), stop=(k == KT - 1))
                        last.then_inc(pp_full, 1)
                        state["g"] = g + 1
                    if 2 <= n < 8:
                        turn_qk(n - 2)
                left_tp(1)
                left_tp(2)

                def scores(it):
                    t, h = it // HEADS, it % HEADS
                    a = (h % 2) * AT_DIM
                    ps = wait_pp()
                    for g in range(NG):
                        last = pe.matmul(ps[:, g * S:g * S + P * (t + 1)],
                                         QKT[a:a + AT_DIM, g, h // 2, t * P:(t + 1) * P],
                                         QKT[a:a + AT_DIM, 3 + g, h // 2, 0:P * (t + 1)], start=True, stop=True)
                    last.then_inc(pp_full, 1)

                def turn_probs(it):
                    pe.wait_ge(prob_ready, due(prob_ready))
                    for half in range(it // HEADS + 1):
                        turn([PB[:, it % 2, (3 * half + j) * P:(3 * half + j + 1) * P] for j in range(3)])

                def values(it, behind):
                    t, h = it // HEADS, it % HEADS
                    for half in range(t + 1):
                        left_tp(behind + half + 1)
                    for b in range(3 * (t + 1)):
                        g, s = b // (t + 1), b % (t + 1)
                        last = pe.matmul(MI[:, t, h * AT_DIM:(h + 1) * AT_DIM], PT[:, it % 2, b * P:(b + 1) * P],
                                         big[:, 6 + g, s * PANEL + h * AT_DIM:s * PANEL + (h + 1) * AT_DIM],
                                         start=(b == 0), stop=(b == 3 * (t + 1) - 1))
                    last.then_inc(pv_done, 1)

                last_it = 2 * HEADS - 1
                scores(0)
                scores(1)
                turn_probs(0)

                def turn_output(t):
                    pe.wait_ge(y_ready, due(y_ready))
                    turn([AO[:, t, j * P:(j + 1) * P] for j in range(4)])

                def tile1_output():
                    turn_output(1)
                    left_tp(1)

                for it in range(2 * HEADS):
                    if it == AT_TURN:
                        turn_output(0)
                    if it + 2 <= last_it:
                        scores(it + 2)
                    if it < last_it:
                        turn_probs(it + 1)
                    if it < KT:
                        last = pe.matmul(MI[:, 1, :], hT[:, it, P:S], w[:, it, :], start=(it == 0), stop=(it == KT - 1))
                        if it == KT - 1:
                            last.then_inc(v_full, 1)
                    if it == HEADS:
                        pe.wait_ge(v_ready, due(v_ready))
                    values(it, ((it + 1) // HEADS + 1 if it < last_it else 0) + (it == AT_TURN))
                out_project(AYT, 4, tile1_output)

            def retention(l):
                first_panel(True)
                project(3, True, hT)
                project(4, False, hT)
                pe.wait_ge(qk_ready, due(qk_ready))
                for h in range(RT_HEADS):
                    ps = wait_pp()
                    for j, (s, t) in enumerate(((0, 0), (1, 1), (0, 1))):
                        for b in range(2):
                            q = big_f[:, (2 * h + b) * S + t * P:(2 * h + b) * S + (t + 1) * P]
                            k = big_f[:, (8 + 2 * h + b) * S + s * P:(8 + 2 * h + b) * S + (s + 1) * P]
                            last = pe.matmul(ps[:, j * P:(j + 1) * P], k, q, start=(b == 0), stop=(b == 1))
                    last.then_inc(pp_full, 1)
                def turn_y(pair):
                    for h in range(2 * pair, 2 * pair + 2):
                        pe.wait_ge(y_ready, due(y_ready))
                        for t in range(TILES):
                            turn([RO[:, h, t, j * P:(j + 1) * P] for j in range(4)])

                for pair in range(2):
                    project(1, False, hT)
                    if pair:
                        turn_y(0)
                    project(1, False, hT)
                    for h in range(2 * pair, 2 * pair + 2):
                        pe.wait_ge(att_ready, due(att_ready))
                        ps = wait_pp()
                        v = [big[:, 4 + h, s * PANEL:(s + 1) * PANEL] for s in range(2)]
                        pe.matmul(ps[:, 0:PANEL], RATT[:, h, 0, :], v[0], start=True, stop=True)
                        pe.matmul(ps[:, PANEL:], RATT[:, h, 1, :], v[1], start=True, stop=False)
                        pe.matmul(ps[:, PANEL:], RATT[:, h, 2, :], v[0], start=False, stop=True).then_inc(pp_full, 1)
                def second_half():
                    turn_y(1)
                    left_tp(1)
                    left_tp(2)

                left_tp(1)
                left_tp(2)
                project(2, False, RYT, halves=2, between=second_half)
                norm_turn(0)

            def peer(l):
                def keys_turn(pair):
                    turn([KEYS[:, 4 * pair + j, :] for j in range(4)])

                def scores(t, pair):
                    k = state["k"]
                    pe.wait_ge(tp_free[k % 2], k // 2)
                    state["k"] = k + 1
                    for j in range(4):
                        c = 4 * pair + j
                        last = pe.matmul(TP[:, k % 2, j * P:(j + 1) * P], PQ[:, c, t * P:(t + 1) * P], KEYST[:, c, :],
                                         start=True, stop=True)
                    last.then_inc(tp_full, 1)

                def between():
                    pe.wait_ge(keys_in, due(keys_in, 16))
                    keys_turn(0)
                    left_tp()
                    pe.wait_ge(query_ready, due(query_ready))
                    scores(0, 0)
                    tile1_turned()

                left_tp(1)
                left_tp(2)
                split_panel(True, between, query_full)
                for pair in range(1, PAIRS):
                    project(1, True, hT)
                    keys_turn(pair)
                    left_pp()
                    left_tp()
                    scores(0, pair)
                for pair in range(PAIRS):
                    scores(1, pair)
                for t in range(TILES):
                    ps = wait_pp()
                    for c in range(2):
                        pe.matmul(ps[:, c * PANEL:(c + 1) * PANEL], ident[:, :], x[:, t, c * PANEL:(c + 1) * PANEL],
                                  start=True, stop=False, skip_group_check=True)
                    groups = SLOTS // RING
                    base = (l * TILES + t) * groups * len(V_PE)
                    turns = (l * TILES + t) * 2 * groups + groups

                    def group(i, end):
                        for n, r in enumerate(V_PE):
                            pe.wait_ge(land[r], i * 16 + (turns + 1) * 16)
                            pe.wait_ge(diag_ready, i * len(V_PE) + (base + n + 1))
                            for c in range(2):
                                last = pe.matmul(ps[:, c * PANEL:(c + 1) * PANEL], DIAG[:, r, :],
                                                 big[:, r, c * PANEL:(c + 1) * PANEL], start=False,
                                                 stop=(end and n == len(V_PE) - 1), skip_group_check=True)
                            last.then_inc(vp_used, 1)

                    with pe.Fori(0, groups - 1) as i:
                        group(i, False)
                    group(groups - 1, True)
                    pe.wait_ge(vp_used, base + groups * len(V_PE))
                    pe.nop().then_inc(pp_full, 1)
                    if l + 1 < DEPTH and t == 0:
                        norm_turn(0)

            pe.wait_ge(ident_in, 16)
            norm_turn(0)
            for l in range(DEPTH):
                (hgrn, attention, retention)[l % 3](l)
                peer(l)

        @block.scalar
        def _(act):
            due = Due()
            mine = Mine(act_done)
            state = {"p": 0, "k": 0}

            def settle():
                act.wait_ge(act_done, mine.n)

            def take_pp():
                p = state["p"]
                act.wait_ge(pp_full, p + 1)
                state["p"] = p + 1
                return PP[:, p % 2, :], pp_free[p % 2]

            def take_tp():
                k = state["k"]
                act.wait_ge(tp_full, k + 1)
                state["k"] = k + 1
                return TP[:, k % 2, :], tp_free[k % 2]

            def to_features(dst, blocks=4):
                tp, free = take_tp()
                act.activation(dst, tp[:, 0:blocks * P].rearrange("p (b c) -> p b c", b=blocks),
                               ACT.Copy).then_inc(free, 1)

            def left_pp(back=1):
                p = state["p"] - back
                act.wait_ge(pp_free[p % 2], p // 2 + 2)

            def norm_root(t, first=False, more=1):
                if first:
                    act.wait_ge(x_in, 16)
                elif more:
                    act.wait_ge(x_ready, due(x_ready, more))
                act.activation(hn[:, t, :], x[:, t, :], ACT.Square, accum_out=stat[:, 0, t:t + 1]).then_inc(sq_ready, 1)
                root(t, 1)

            def norm_features(t):
                for half in range(2):
                    to_features(hT[:, 4 * half:4 * half + 4, t * P:(t + 1) * P])

            def move_panel(j, func=ACT.Copy):
                ps, free = take_pp()
                act.activation(big[:, j, :], ps, func).then_inc(free, 1)

            def root(first, n):
                act.wait_ge(ms_ready, due(ms_ready))
                act.activation(stat[:, 2, first:first + n], stat[:, 1, first:first + n], ACT.Sqrt).then_inc(root_ready, 1)

            def hgrn(l):
                for j in range(2):
                    move_panel(j, ACT.Silu)
                for j in range(2, 4):
                    move_panel(j)
                left_pp(1)
                left_pp(2)
                f = big_f[:, 2 * D:4 * D]
                act.activation(big_f[:, 10 * D:12 * D], f, ACT.Sigmoid, scale=-1.0).then_inc(sig_ready, 1)
                act.activation(big_f[:, 12 * D:14 * D], f, ACT.Sigmoid).then_inc(sig_ready, 1)
                move_panel(4)
                act.wait_ge(forget_ready, due(forget_ready))
                act.activation(B, big_f[:, 12 * D:14 * D], ACT.Ln).then_inc(log_ready, 1)
                move_panel(5)
                gate_uses = []

                def decays(*levels):
                    for n in levels:
                        act.wait_ge(diff_ready, due(diff_ready, 2))
                        act.activation(E[n % 3], E[n % 3], ACT.Exp).then_inc(exp_ready, 1)

                def gate_part(c, t):
                    gate_uses.append(state["p"])
                    ps, free = take_pp()
                    act.activation(big[:, 6 + c, t * PANEL:(t + 1) * PANEL], ps[:, 0:PANEL], ACT.Copy).then_inc(free, 1)

                gate_part(0, 0)
                decays(0, 1, 2)
                state["p"] += 4
                gate_part(0, 1)
                decays(3)
                state["p"] += 2
                gate_part(1, 0)
                decays(4, 5, 6)
                state["p"] += 6
                gate_part(1, 1)
                decays(7)
                for p in gate_uses:
                    act.wait_ge(pp_free[p % 2], p // 2 + 2)
                state["p"] += 5
                mine.step(act.activation(big[:, 6:8, :], big[:, 6:8, :], ACT.Silu))
                for t in range(TILES):
                    ps, free = take_pp()
                    act.activation(O[:, t * D:(t + 1) * D], ps, ACT.Copy).then_inc(free, 1)
                    left_pp()
                    act.activation(E[0][:, t * D:(t + 1) * D], O[:, t * D:(t + 1) * D], ACT.Square).then_inc(o_ready, 1)
                for t in range(TILES):
                    root(8 * t, 8)
                state["k"] += 4
                state["p"] += 2

            def attention(l):
                for n in range(9):
                    if n < 8:
                        move_panel(n)
                    else:
                        ps, free = take_pp()
                        act.activation(big[:, 8, 0:PANEL], ps[:, 0:PANEL], ACT.Copy).then_inc(free, 1)
                    if n < 6:
                        left_pp()
                        if n >= 2:
                            act.wait_ge(qk_ready, due(qk_ready))
                        act.activation(SQ[:, n % 2, :], big[:, n, :], ACT.Square).then_inc(o_ready, 1)
                        root(16 * n, 16)
                    if 2 <= n < 8:
                        for t in range(TILES):
                            to_features(QKT[:, n - 2, :, t * P:(t + 1) * P])
                due(qk_ready, 2)
                for it in range(2 * HEADS):
                    t = it // HEADS
                    w = 3 * P * (t + 1)
                    state["p"] += 1
                    act.wait_ge(sc_ready, due(sc_ready))
                    act.activation(PB[:, it % 2, 0:w], PB[:, it % 2, 0:w], ACT.Exp, bias=stat[:, 0, it:it + 1],
                                   accum_out=stat[:, 1, it:it + 1]).then_inc(prob_ready, 1)
                    if it == HEADS:
                        act.wait_ge(v_full, due(v_full))
                        act.activation(big[:, 8, PANEL:], MI[:, 1, :], ACT.Copy).then_inc(v_ready, 1)
                    if it >= 2:
                        act.wait_ge(pv_done, due(pv_done))
                    for half in range(t + 1):
                        to_features(PT[:, it % 2, 3 * half * P:(3 * half + 3) * P].rearrange("p (b c) -> p b c", b=3), 3)
                    if it == AT_TURN:
                        to_features(AYT[:, :, 0:P])
                due(pv_done, 2)
                to_features(AYT[:, :, P:S])
                state["p"] += 2

            def retention(l):
                for j in range(8):
                    move_panel(j)
                state["p"] += 4
                for pair in range(2):
                    for h in range(2 * pair, 2 * pair + 2):
                        move_panel(8 + h, ACT.Silu)
                    for h in range(2 * pair, 2 * pair + 2):
                        ps, free = take_pp()
                        if h == 0:
                            act.wait_ge(qk_ready, due(qk_ready))
                        for t in range(TILES):
                            mine.step(act.activation(RJ[:, 2 * h + t, :], ps[:, t * PANEL:(t + 1) * PANEL],
                                                     ACT.Square, accum_out=stat[:, 0, 2 * h + t:2 * h + t + 1]))
                        act.activation(RO[:, h, :, :].rearrange("p t c -> p (t c)"), ps, ACT.Copy).then_inc(free, 1)
                        settle()
                        left_pp()
                        act.nop().then_inc(o_ready, 1)
                    root(4 * pair, 4)
                state["k"] += 8
                state["p"] += 2

            def peer(l):
                if l % 3 == 2:
                    norm_root(0, more=2)
                    norm_root(1, more=0)
                    norm_features(0)
                else:
                    norm_root(0)
                    norm_features(0)
                    norm_root(1)
                for pair in range(PAIRS):
                    quads = slice(4 * pair, 4 * pair + 4)
                    if pair == 0:
                        act.wait_ge(query_full, due(query_full))
                        half_pp = PP[:, state["p"] % 2, :].rearrange("p (c s) -> p c s", c=4)
                        act.activation(PQ[:, quads, 0:P], half_pp[:, :, 0:P], ACT.Copy).then_inc(query_ready, 1)
                        to_features(KEYST[:, quads, :])
                        to_features(SC[:, 0, quads, :])
                        norm_features(1)
                        ps, free = take_pp()
                        act.activation(PQ[:, quads, P:S], half_pp[:, :, P:S], ACT.Copy).then_inc(free, 1)
                    else:
                        ps, free = take_pp()
                        act.activation(PQ[:, quads, :].rearrange("p c s -> p (c s)"), ps, ACT.Copy).then_inc(free, 1)
                        to_features(KEYST[:, quads, :])
                        to_features(SC[:, 0, quads, :])
                for pair in range(PAIRS):
                    to_features(SC[:, 1, 4 * pair:4 * pair + 4, :])
                for t in range(TILES):
                    act.wait_ge(shift_ready, due(shift_ready, PAIRS + 1 - t))
                    act.activation(gate[:, t, :], gate[:, t, :], ACT.Exp).then_inc(gate_exp, 1)
                    act.wait_ge(dots_ready, due(dots_ready))
                    act.activation(act_v[:, t, :], act_v[:, t, :], ACT.Gelu).then_inc(gelu_ready, 1)
                    act.wait_ge(w_ready, due(w_ready))
                    base = (l * TILES + t) * SLOTS // RING * len(V_PE)

                    def group(i, before):
                        for n, r in enumerate(V_PE):
                            if before is not None:
                                act.wait_ge(vp_used, before + (n + 1))
                            act.wait_ge(w_ready, due(w_ready, 0))
                            act.activation(DIAG[:, r, :], ident[:, :], ACT.Copy,
                                           scale=act_v[:, t, bass.ds(i * RING + r, 1)]).then_inc(diag_ready, 1)

                    group(0, base - len(V_PE) if base else None)
                    with act.Fori(0, SLOTS // RING - 1) as i:
                        group(i + 1, i * len(V_PE) + base)
                    state["p"] += 1
                    if l + 1 < DEPTH:
                        norm_root(t)
                        norm_features(t)

            for t in range(TILES):
                norm_root(t, first=True)
            for t in range(TILES):
                norm_features(t)
            act.wait_ge(trig_arg, due(trig_arg))
            act.activation(sin_t[:, :], sin_t[:, :], ACT.Sin).then_inc(trig_ready, 1)
            act.activation(cos_t[:, :], cos_t[:, :], ACT.Sin).then_inc(trig_ready, 1)
            state["k"] += 1
            act.wait_ge(lb_arg, due(lb_arg))
            act.activation(feat[:, 0:32], feat[:, 0:32], ACT.Exp).then_inc(lb_exp, 1)
            for l in range(DEPTH):
                (hgrn, attention, retention)[l % 3](l)
                peer(l)

        @block.vector
        def _(dve):
            due = Due()
            mine = Mine(dve_done)
            state = {"p": 0, "k": 0}
            step = mine.step

            def settle():
                dve.wait_ge(dve_done, mine.n)

            def take_pp():
                p = state["p"]
                dve.wait_ge(pp_full, p + 1)
                state["p"] = p + 1
                return PP[:, p % 2, :], pp_free[p % 2]

            def take_tp():
                k = state["k"]
                dve.wait_ge(tp_full, k + 1)
                state["k"] = k + 1
                return TP[:, k % 2, :], tp_free[k % 2]

            def do(instruction):
                step(instruction)
                settle()

            def tell(sem_):
                settle()
                dve.nop().then_inc(sem_, 1)

            def inverse_root(first, n, width):
                at = slice(first, first + n)
                dve.tensor_scalar(stat[:, 1, at], stat[:, 0, at], 1.0 / width, EPS, ALU.mult, ALU.add).then_inc(ms_ready, 1)
                dve.wait_ge(root_ready, due(root_ready))
                do(dve.reciprocal(stat[:, 2, at], stat[:, 2, at]))

            def norm(t):
                dve.wait_ge(sq_ready, due(sq_ready))
                inverse_root(t, 1, D)
                if t == 0:
                    dve.wait_ge(gain_in, due(gain_in, 16))
                dve.scalar_tensor_tensor(hn[:, t, :], x[:, t, :], stat[:, 2, t:t + 1], gain[:, :],
                                         ALU.mult, ALU.mult).then_inc(hn_ready, 1)
                dve.wait_ge(hn_ready, due(hn_ready))
                state["k"] += 2

            def left_pp(back=1):
                p = state["p"] - back
                dve.wait_ge(pp_free[p % 2], p // 2 + 2)

            def residual_by_tile():
                for t in range(TILES):
                    ps, free = take_pp()
                    do(dve.tensor_tensor(x[:, t, :], ps, x[:, t, :], ALU.add))
                    dve.nop().then_inc(free, 1)
                    dve.nop().then_inc(x_ready, 1)
                    norm(t)

            def residual_by_panel():
                for c in range(2):
                    ps, free = take_pp()
                    xs = x[:, :, c * PANEL:(c + 1) * PANEL]
                    do(dve.tensor_tensor(xs, ps.rearrange("p (t n) -> p t n", t=TILES), xs, ALU.add))
                    dve.nop().then_inc(free, 1)
                    dve.nop().then_inc(x_ready, 1)
                for t in range(TILES):
                    norm(t)

            def gained(dst, first, n=4):
                tp, free = take_tp()
                g = feat[:, first:first + n].unsqueeze(2).to_broadcast([P, n, P])
                dve.tensor_tensor(dst, tp.rearrange("p (b c) -> p b c", b=n), g, ALU.mult).then_inc(free, 1)

            def hgrn(l):
                n_l = l // 3
                state["p"] += 4
                lbb = lb[:, n_l, 0, :].unsqueeze(2).to_broadcast([P, HEADS, S])
                omb = lb[:, n_l, 1, :].unsqueeze(2).to_broadcast([P, HEADS, S])

                def by_head(a):
                    return a.rearrange("p (h s) -> p h s", h=HEADS)

                kk = big_f[:, 8 * D:10 * D]
                fg = big_f[:, 12 * D:14 * D]
                up = big_f[:, 14 * D:16 * D]
                tiny = E[2]
                dve.wait_ge(sig_ready, due(sig_ready, 2))
                do(dve.tensor_tensor(by_head(fg), by_head(fg), omb, ALU.mult))
                do(dve.tensor_tensor(by_head(fg), by_head(fg), lbb, ALU.add))
                do(dve.tensor_scalar(tiny, fg, 2.0 ** -40, None, ALU.is_lt))
                do(dve.tensor_scalar(up, tiny, 2.0 ** LN_SHIFT, 1.0, ALU.mult, ALU.add))
                dve.scalar_tensor_tensor(fg, fg, TINY, up, ALU.max, ALU.mult).then_inc(forget_ready, 1)
                dve.wait_ge(log_ready, due(log_ready))
                do(dve.scalar_tensor_tensor(fg, tiny, -LN_SHIFT * math.log(2.0), B, ALU.mult, ALU.add))
                for n in range(2 * HEADS):
                    seg = slice(n * P, (n + 1) * P)
                    step(dve.tensor_tensor_scan(B[:, seg], ones[:, :], fg[:, seg], 0.0, ALU.mult, ALU.add))
                tell(sums_ready)
                state["p"] += 3
                for f in range(2):
                    ps, free = take_pp()
                    a = ATT[:, f * 1024:(f + 1) * 1024].rearrange("p (n t) -> p n t", n=8)
                    idb = ident[:, :].unsqueeze(1).to_broadcast([P, 8, P])
                    dve.tensor_tensor(a, ps.rearrange("p (n t) -> p n t", n=8), idb, ALU.mult).then_inc(free, 1)
                dve.wait_ge(key_ready, due(key_ready))
                dve.wait_ge(table_in, due(table_in, 16))

                def products(n):
                    m = (LEVELS + [P])[n]
                    dve.wait_ge(exp_ready, due(exp_ready))

                    def half(a, which):
                        return a.rearrange("p (n two m) -> p n two m", two=2, m=m)[:, :, which, :]

                    e = E[n % 3]
                    step(dve.tensor_tensor(half(e, 0), half(e, 0), half(kk, 0), ALU.mult))
                    step(dve.tensor_tensor(half(e, 1), half(e, 1), half(Q3, 1), ALU.mult))
                    tell(pair_ready)

                def select(n):
                    if n == len(LEVELS):
                        ps, free = take_pp()
                        dve.tensor_copy(ATTX, ps).then_inc(free, 1)
                    else:
                        for f in range(2):
                            ps, free = take_pp()
                            left_pp(3)
                            a = ATT[:, f * 1024:(f + 1) * 1024].rearrange("p (n t) -> p n t", n=8)
                            mask = lvl[:, n, :].unsqueeze(1).to_broadcast([P, 8, P])
                            dve.copy_predicated(a, mask, ps.rearrange("p (n t) -> p n t", n=8)).then_inc(free, 1)
                            if n in GATE_AFTER and f == 1:
                                left_pp()
                                state["p"] += 1
                    if n not in GATE_AFTER:
                        left_pp()
                    dve.nop().then_inc(level_taken, 1)

                total = len(LEVELS) + 1
                for n in range(total):
                    products(n)
                    if n:
                        select(n - 1)
                dve.nop().then_inc(att_ready, 1)
                select(total - 1)
                dve.nop().then_inc(att_ready, 1)
                state["p"] += 2
                for t in range(TILES):
                    dve.wait_ge(o_ready, due(o_ready))
                    o_t = O[:, t * D:(t + 1) * D]
                    by_h = o_t.rearrange("p (n c) -> p n c", c=P)
                    do(dve.tensor_reduce(stat[:, 0, 8 * t:8 * t + 8],
                                         E[0][:, t * D:(t + 1) * D].rearrange("p (n c) -> p n c", c=P), AX.X, ALU.add))
                    inverse_root(8 * t, 8, P)
                    do(dve.tensor_tensor(by_h, by_h,
                                         stat[:, 2, 8 * t:8 * t + 8].unsqueeze(2).to_broadcast([P, 8, P]), ALU.mult))
                    o_c = o_t.rearrange("p (c n) -> p c n", c=2)
                    dve.tensor_tensor(o_c, o_c, big[:, 6:8, t * PANEL:(t + 1) * PANEL], ALU.mult).then_inc(y_ready, 1)
                    for c in range(2):
                        gained(YT[:, 4 * c:4 * c + 4, t * P:(t + 1) * P], 32 + 8 * n_l + 4 * c)
                residual_by_tile()

            def attention(l):
                state["p"] += 9
                dve.wait_ge(atgain_in, 32)
                for n in range(6):
                    dve.wait_ge(o_ready, due(o_ready))
                    do(dve.tensor_reduce(stat[:, 0, 16 * n:16 * n + 16],
                                         SQ[:, n % 2, :].rearrange("p (n c) -> p n c", c=AT_DIM), AX.X, ALU.add))
                    inverse_root(16 * n, 16, AT_DIM)
                    v16 = big[:, n, :].rearrange("p (n c) -> p n c", c=AT_DIM)
                    do(dve.tensor_tensor(v16, v16, stat[:, 2, 16 * n:16 * n + 16].unsqueeze(2).to_broadcast([P, 16, AT_DIM]),
                                         ALU.mult))
                    do(dve.tensor_tensor(v16, v16, at_gain[:, n, :].unsqueeze(1).to_broadcast([P, 16, AT_DIM]), ALU.mult))
                    v = big[:, n, :].rearrange("p (t h a c) -> p t h a c", t=2, h=8, a=2)
                    w = TMP[:, 0:2048].rearrange("p (a t h c) -> p a t h c", a=4, t=2, h=8)
                    for t in range(TILES):
                        x1, x2 = v[:, t, :, 0, :], v[:, t, :, 1, :]
                        c = cos_t[:, 256 + 32 * t:288 + 32 * t].unsqueeze(1).to_broadcast([P, 8, 32])
                        s = sin_t[:, 256 + 32 * t:288 + 32 * t].unsqueeze(1).to_broadcast([P, 8, 32])
                        step(dve.tensor_tensor(w[:, 0, t], x1, c, ALU.mult))
                        step(dve.tensor_tensor(w[:, 1, t], x2, s, ALU.mult))
                        step(dve.tensor_tensor(w[:, 2, t], x2, c, ALU.mult))
                        step(dve.tensor_tensor(w[:, 3, t], x1, s, ALU.mult))
                    settle()
                    step(dve.tensor_tensor(v[:, :, :, 0, :], w[:, 0], w[:, 1], ALU.subtract))
                    step(dve.tensor_tensor(v[:, :, :, 1, :], w[:, 2], w[:, 3], ALU.add))
                    tell(qk_ready)
                state["k"] += 12
                dve.wait_ge(table_in, due(table_in, 16))

                def merged(t):
                    at = slice(HEADS * t, HEADS * (t + 1))
                    dve.wait_ge(pv_done, due(pv_done, HEADS))
                    dve.wait_ge(prob_ready, due(prob_ready, HEADS))
                    do(dve.reciprocal(stat[:, 2, at], stat[:, 1, at]))
                    dve.tensor_tensor(AO[:, t, :].rearrange("p (h c) -> p h c", h=8),
                                      MI[:, t, :].rearrange("p (h c) -> p h c", h=8),
                                      stat[:, 2, at].unsqueeze(2).to_broadcast([P, HEADS, AT_DIM]),
                                      ALU.mult).then_inc(y_ready, 1)

                for it in range(2 * HEADS):
                    t = it // HEADS
                    n = P * (t + 1)
                    ps, free = take_pp()
                    if it == AT_TURN + 1:
                        merged(0)
                    if it >= 2:
                        k_done = state["k"] + (it - 1 if it - 1 <= HEADS else HEADS + 2 * (it - 1 - HEADS))
                        if it - 2 > AT_TURN:
                            k_done += 1
                        dve.wait_ge(tp_full, k_done)
                    pb_ = PB[:, it % 2, 0:3 * n].rearrange("p (g k) -> p g k", g=NG)
                    mask = table[:, 3 * P * t:3 * P * t + 3 * n].rearrange("p (g k) -> p g k", g=NG)
                    dve.scalar_tensor_tensor(pb_, ps[:, 0:3 * S].rearrange("p (g k) -> p g k", g=NG)[:, :, 0:n],
                                             AT_DIM ** -0.5, mask, ALU.mult, ALU.add).then_inc(free, 1)
                    left_pp()
                    dve.tensor_reduce(stat[:, 0, it:it + 1], PB[:, it % 2, 0:3 * n], AX.X, ALU.max,
                                      negate=True).then_inc(sc_ready, 1)
                state["k"] += 8 + 16
                merged(1)
                state["k"] += 2
                residual_by_tile()

            def retention(l):
                state["p"] += 4
                left_pp(1)
                left_pp(2)
                v = big_f[:, 0:4 * D].rearrange("p (h a s) -> p h a s", a=2, s=S)
                x1, x2 = v[:, :, 0, :], v[:, :, 1, :]
                c = cos_t[:, 0:S].unsqueeze(1).to_broadcast([P, 8, S])
                s = sin_t[:, 0:S].unsqueeze(1).to_broadcast([P, 8, S])
                w = [r.rearrange("p (h s) -> p h s", h=8) for r in RTMP]
                step(dve.tensor_tensor(w[0], x1, c, ALU.mult))
                step(dve.tensor_tensor(w[1], x2, s, ALU.mult))
                step(dve.tensor_tensor(w[2], x2, c, ALU.mult))
                do(dve.tensor_tensor(w[3], x1, s, ALU.mult))
                step(dve.tensor_tensor(x1, w[0], w[1], ALU.subtract))
                step(dve.tensor_tensor(x2, w[2], w[3], ALU.add))
                tell(qk_ready)
                state["p"] += 4
                dve.wait_ge(table_in, due(table_in, 16))
                for h in range(RT_HEADS):
                    ps, free = take_pp()
                    do(dve.tensor_tensor(RATT[:, h, :, :].rearrange("p j t -> p (j t)"), ps[:, 0:3 * P],
                                         table[:, h * 3 * P:(h + 1) * 3 * P], ALU.mult))
                    dve.nop().then_inc(free, 1)
                    dve.nop().then_inc(att_ready, 1)
                state["p"] += 8
                for pair in range(2):
                    dve.wait_ge(o_ready, due(o_ready, 2))
                    inverse_root(4 * pair, 4, PANEL)
                    for h in range(2 * pair, 2 * pair + 2):
                        for t in range(TILES):
                            n = 2 * h + t
                            step(dve.scalar_tensor_tensor(RO[:, h, t, :], RO[:, h, t, :], stat[:, 2, n:n + 1],
                                                          big[:, 8 + h, t * PANEL:(t + 1) * PANEL], ALU.mult, ALU.mult))
                        tell(y_ready)
                    for n in range(2 * TILES):
                        h, t = 2 * pair + n // TILES, n % TILES
                        gained(RYT[:, 4 * h:4 * h + 4, t * P:(t + 1) * P], 48 + 4 * h)
                residual_by_panel()

            def top16(src, n, out_v, out_i):
                for half in range(2):
                    lo = slice(8 * half, 8 * half + 8)
                    for c in range(n):
                        step(dve.max(out_v[:, c, lo], src[:, c, :]))
                    settle()
                    for c in range(n):
                        step(dve.max_index(out_i[:, c, lo], out_v[:, c, lo], src[:, c, :]))
                    settle()
                    if half == 0:
                        for c in range(n):
                            step(dve.match_replace(src[:, c, :], out_v[:, c, lo], src[:, c, :], NEG))
                        settle()

            def route(t, pair, head=0, heads=2):
                n = heads * TOPK
                k = (12 + pair if t else 5 + 2 * pair if pair else 3) + state["k"]
                dve.wait_ge(tp_free[k % 2], k // 2 + 1)
                first = 4 * pair + 2 * head
                top16(SC[:, t, first:first + 2 * heads, :], 2 * heads, val, nidx)
                fi = small(0, 2 * n)
                v = val[:, 0:2 * heads, :].rearrange("p (h c) k -> p h c k", c=2)
                a = v[:, :, 0, :].unsqueeze(3).to_broadcast([P, heads, TOPK, TOPK])
                b = v[:, :, 1, :].unsqueeze(2).to_broadcast([P, heads, TOPK, TOPK])
                step(dve.tensor_copy(fi, nidx[:, 0:2 * heads, :].rearrange("p c k -> p (c k)")))
                cand, one4 = CAND[:, 0:heads], ONE[:, 0:heads]
                do(dve.tensor_tensor(cand, a, b, ALU.add))
                top_v = small(64, n).rearrange("p (h k) -> p h k", h=heads)
                pos = small(96, n).bitcast(U32)
                top16(cand.rearrange("p h a b -> p h (a b)"), heads, top_v, pos.rearrange("p (h k) -> p h k", h=heads))
                mine_ = slice(PAIR * pair + TOPK * head, PAIR * pair + TOPK * head + n)
                dve.tensor_tensor(gate[:, t, mine_].rearrange("p (h k) -> p h k", h=heads), top_v,
                                  top_v[:, :, 0:1].to_broadcast([P, heads, TOPK]), ALU.subtract).then_inc(shift_ready, 1)
                ab = small(128, 2 * n).bitcast(U32)
                step(dve.tensor_scalar(ab[:, 0:n], pos, 4, None, ALU.logical_shift_right))
                do(dve.tensor_scalar(ab[:, n:], pos, 15, None, ALU.bitwise_and))
                abf = small(192, 2 * n)
                do(dve.tensor_copy(abf, ab))
                f4 = fi.rearrange("p (h c k) -> p h c k", h=heads, c=2)
                got = small(256, 2 * n)
                for c in range(2):
                    one = one4.rearrange("p h k i -> p (h k) i")
                    do(dve.tensor_tensor(one, abf[:, n * c:n * (c + 1)].unsqueeze(2).to_broadcast([P, n, TOPK]),
                                         iota[:, :].unsqueeze(1).to_broadcast([P, n, TOPK]), ALU.is_equal))
                    do(dve.tensor_tensor(one4, one4, f4[:, :, c, :].unsqueeze(2).to_broadcast([P, heads, TOPK, TOPK]),
                                         ALU.mult))
                    do(dve.tensor_reduce(got[:, n * c:n * (c + 1)], one, AX.X, ALU.add))
                do(dve.scalar_tensor_tensor(idx[:, t, mine_], got[:, 0:n], float(NKEYS), got[:, n:],
                                            ALU.mult, ALU.add))
                dve.nop().then_inc(idx_ready, 1)

            def dots(l, t, pair):
                base = (l * TILES + t) * SLOTS + PAIR * pair
                turns = (l * TILES + t) * 2 * SLOTS // RING + 2 * pair
                copies = mine.n
                with dve.Fori(0, 2) as i:
                    dve.wait_ge(dve_done, i + copies)
                    for r in range(RING):
                        dve.wait_ge(land[r], i * 16 + (turns + 1) * 16)
                        dve.tensor_tensor_reduce(big[:, r, :], big[:, r, :], hn[:, t, :], 1.0, 0.0, ALU.mult,
                                                 ALU.add, dot16[:, r:r + 1]).then_inc(u_used, 1)
                    dve.wait_ge(u_used, i * RING + (base + RING))
                    dve.wait_ge(idx_ready, routings(l, t, pair))
                    dve.tensor_copy(act_v[:, t, bass.ds(i * RING + PAIR * pair, RING)], dot16[:, :]).then_inc(dve_done, 1)
                mine.n += 2

            def sums(l, t, pair):
                turns = (l * TILES + t) * 2 * SLOTS // RING + SLOTS // RING + 2 * pair
                base = (l * TILES + t) * (1 + PAIRS * 2 * len(V_DVE)) + 1 + 2 * pair * len(V_DVE)
                with dve.Fori(0, 2) as i:
                    for n, r in enumerate(V_DVE):
                        dve.wait_ge(land[r], i * 16 + (turns + 1) * 16)
                        dve.wait_ge(vd_used, i * len(V_DVE) + (base + n))
                        dve.scalar_tensor_tensor(ACC[t], big[:, r, :],
                                                 act_v[:, t, bass.ds(i * RING + (PAIR * pair + r), 1)], ACC[t],
                                                 ALU.mult, ALU.add).then_inc(vd_used, 1)

            def weigh(t):
                dve.wait_ge(gate_exp, due(gate_exp))
                g3 = gate[:, t, :].rearrange("p (h k) -> p h k", h=HEADS)
                do(dve.tensor_reduce(stat[:, 0, 0:8], g3, AX.X, ALU.add))
                do(dve.reciprocal(stat[:, 1, 0:8], stat[:, 0, 0:8]))
                do(dve.tensor_tensor(g3, g3, stat[:, 1, 0:8].unsqueeze(2).to_broadcast([P, HEADS, TOPK]), ALU.mult))
                dve.wait_ge(gelu_ready, due(gelu_ready))
                do(dve.tensor_tensor(act_v[:, t, :], act_v[:, t, :], gate[:, t, :], ALU.mult))
                dve.nop().then_inc(w_ready, 1)

            def peer(l):
                state["p"] += 4
                state["k"] -= 4
                scored = state["k"] + 4 + PAIRS * 3
                route(0, 0, 0, 1)
                route(0, 0, 1, 1)
                route(0, 1)
                dots(l, 0, 0)
                route(0, 2)
                dots(l, 0, 1)
                route(0, 3)
                dots(l, 0, 2)
                dots(l, 0, 3)
                tell(dots_ready)
                weigh(0)
                dve.wait_ge(tp_full, scored)
                for t in range(TILES):
                    dve.memset(ACC[t], 0.0).then_inc(vd_used, 1)
                    for pair in range(PAIRS):
                        sums(l, t, pair)
                        if t == 0:
                            route(1, pair)
                    if t == 0:
                        for pair in range(PAIRS):
                            dots(l, 1, pair)
                            if pair == 1:
                                state["k"] = scored
                                finish(l, 0)
                        tell(dots_ready)
                        weigh(1)
                finish(l, 1)

            def finish(l, t):
                ps, free = take_pp()
                dve.wait_ge(vd_used, (l * TILES + t + 1) * (1 + PAIRS * 2 * len(V_DVE)))
                do(dve.tensor_tensor(x[:, t, :], ps, ACC[t], ALU.add))
                dve.nop().then_inc(free, 1)
                dve.nop().then_inc(x_ready, 1)
                if l + 1 < DEPTH:
                    norm(t)

            for s in range(2):
                dve.nop().then_inc(pp_free[s], 1)
            dve.wait_ge(x_in, 16)
            for t in range(TILES):
                norm(t)
            dve.wait_ge(ident_in, 16)
            dve.wait_ge(consts_in, 16 * 8)
            ang, w1, w2 = E[1][:, 0:320], E[1][:, 320:640], E[1][:, 640:960]
            wi = E[1][:, 960:1280].bitcast(I32)
            pf = E[2][:, 0:258]
            step(dve.memset(ones[:, :], 1.0))
            do(dve.tensor_copy(pf, E[0][:, 0:258].bitcast(I32)))
            step(dve.tensor_scalar(ang[:, 0:256], pf[:, 0:256], E[0][:, 258:259], None, ALU.mult))
            for t in range(TILES):
                step(dve.tensor_scalar(ang[:, 256 + 32 * t:288 + 32 * t], E[0][:, 260:292], pf[:, 256 + t:257 + t],
                                       None, ALU.mult))
            settle()
            do(dve.tensor_scalar(w1, ang, 1.0 / TWO_PI, None, ALU.mult))
            do(dve.tensor_copy(wi, w1))
            do(dve.tensor_copy(w1, wi))
            for part in (C1, C2, C3):
                do(dve.scalar_tensor_tensor(ang, w1, -part, ang, ALU.mult, ALU.add))
            for limit, compare, shift in ((math.pi, ALU.is_gt, -TWO_PI), (-math.pi, ALU.is_lt, TWO_PI)):
                do(dve.tensor_scalar(w2, ang, limit, shift, compare, ALU.mult))
                do(dve.tensor_tensor(ang, ang, w2, ALU.add))
            do(dve.tensor_scalar(sin_t[:, :], ang, PI_IN, -PI_IN, ALU.min, ALU.max))
            do(dve.scalar_tensor_tensor(w2, sin_t[:, :], -1.0, sin_t[:, :], ALU.mult, ALU.max))
            do(dve.tensor_scalar(cos_t[:, :], w2, -1.0, math.pi / 2, ALU.mult, ALU.add))
            dve.nop().then_inc(trig_arg, 1)
            tp, free = take_tp()
            do(dve.tensor_copy(feat[:, :], tp[:, 0:64]))
            dve.nop().then_inc(free, 1)
            f4 = feat[:, 0:32].rearrange("p (l h) -> p l h", l=DEPTH)
            m8 = stat[:, 3, 0:8]
            do(dve.tensor_reduce(m8, feat[:, 0:32].rearrange("p (l h) -> p h l", l=DEPTH), AX.X, ALU.max))
            do(dve.tensor_tensor(f4, f4, m8.unsqueeze(1).to_broadcast([P, DEPTH, HEADS]), ALU.subtract))
            dve.nop().then_inc(lb_arg, 1)
            dve.wait_ge(lb_exp, due(lb_exp))
            do(dve.tensor_reduce(m8, feat[:, 0:32].rearrange("p (l h) -> p h l", l=DEPTH), AX.X, ALU.add))
            do(dve.reciprocal(stat[:, 3, 8:16], m8))
            do(dve.tensor_tensor(f4, f4, stat[:, 3, 8:16].unsqueeze(1).to_broadcast([P, DEPTH, HEADS]), ALU.mult))
            run = stat[:, 3, 16:24]
            do(dve.tensor_copy(run, f4[:, 0, :]))
            for l in range(DEPTH):
                if l:
                    do(dve.tensor_tensor(run, run, f4[:, l, :], ALU.add))
                if l % 3 == 0:
                    do(dve.tensor_tensor(lb[:, l // 3, 0, :], run, f4[:, 0, :], ALU.subtract))
                    do(dve.tensor_scalar(lb[:, l // 3, 1, :], lb[:, l // 3, 0, :], -1.0, 1.0, ALU.mult, ALU.add))
            dve.nop().then_inc(lb_ready, 1)
            dve.wait_ge(trig_ready, due(trig_ready, 2))
            for l in range(DEPTH):
                (hgrn, attention, retention)[l % 3](l)
                peer(l)


def kernel(**inputs):
    import concourse.bacc as _bacc
    from concourse.bass_utils import run_bass_kernel_spmd as _run

    nc = _bacc.Bacc("TRN2", target_bir_lowering=False, num_devices=1)
    arrays, args = {}, {}
    for name, a in {**inputs, **shape_constants()}.items():
        a = np.ascontiguousarray(a)
        arrays[f"in_{name}"] = a
        args[name] = nc.dram_tensor(f"in_{name}", a.shape, mybir.dt.from_np(a.dtype), kind="ExternalInput").ap()
    out = nc.dram_tensor("out_0", (1, S, D), F32, kind="ExternalOutput").ap()
    trunk(nc, args, out)
    r = _run(nc, [arrays], core_ids=[0])
    return r.results[0]["out_0"]
```
